# Optimizing a Trainium2 kernel written in Bass

```python
import numpy as np
import jax, jax.numpy as jnp
from jax import lax
import math
import jax
import jax.numpy as jnp

D_MODEL = 1024
BATCH = 1
SEQ = 256
DEPTH = 2

ROPE_THETA = 500000.0
NORM_EPS = 1e-6
Q_BLOCK = 128
MLA_HEADS = 8
MLA_NOPE_DIM = 64
MLA_ROPE_DIM = 32
MLA_QK_DIM = MLA_NOPE_DIM + MLA_ROPE_DIM
MLA_V_DIM = 64
MLA_Q_RANK = 384
MLA_KV_RANK = 256
CONV_CH = 512
CONV_WIDTH = 31
NSA_HEADS = 8
NSA_KV_GROUPS = 2
NSA_HEAD_DIM = 64
NSA_ROPE_DIM = NSA_HEAD_DIM // 4
NSA_N_BRANCH = 3
CMP_BLOCK = 32
CMP_STRIDE = 16
CMP_HIDDEN = 128
SLC_BLOCK = 64
SLC_TOP_N = 16
WINDOW = 512
NSA_Q_BLOCK = 64
FORCED_BLOCK_SCORE = 1e6
N_MIXERS = 3
D_FF = 4 * D_MODEL

IN_SPLITS = (
    MLA_Q_RANK,
    MLA_KV_RANK,
    MLA_ROPE_DIM,
    2 * CONV_CH,
    NSA_HEADS * NSA_HEAD_DIM,
    2 * NSA_N_BRANCH * NSA_KV_GROUPS * NSA_HEAD_DIM,
    NSA_N_BRANCH * NSA_HEADS,
    N_MIXERS * D_MODEL,
)
D_IN = sum(IN_SPLITS)
SPLIT_IDX = tuple(int(v) for v in np.cumsum(IN_SPLITS)[:-1])


def rms_norm(x, g):
    xf = x.astype(jnp.float32)
    y = xf * lax.rsqrt(jnp.mean(xf * xf, axis=-1, keepdims=True) + NORM_EPS)
    return (y * g.astype(jnp.float32)).astype(x.dtype)

def layer_norm(x, g, b):
    xf = x.astype(jnp.float32)
    mu = jnp.mean(xf, axis=-1, keepdims=True)
    var = jnp.mean(jnp.square(xf - mu), axis=-1, keepdims=True)
    y = (xf - mu) * lax.rsqrt(var + NORM_EPS)
    return (y * g.astype(jnp.float32) + b.astype(jnp.float32)).astype(x.dtype)

def rope(x, pos, rot_dim):
    half = rot_dim // 2
    inv = jnp.power(jnp.float32(ROPE_THETA), -jnp.arange(half, dtype=jnp.float32) * (2.0 / rot_dim))
    ang = pos.astype(jnp.float32)[:, None] * inv
    cos = jnp.cos(ang)[:, None, :]
    sin = jnp.sin(ang)[:, None, :]
    xf = x.astype(jnp.float32)
    x1, x2 = xf[..., :half], xf[..., half:rot_dim]
    out = jnp.concatenate([x1 * cos - x2 * sin, x2 * cos + x1 * sin, xf[..., rot_dim:]], axis=-1)
    return out.astype(x.dtype)

def masked_softmax(s, mask):
    s = jnp.where(mask, s.astype(jnp.float32), -jnp.inf)
    m = jnp.max(s, axis=-1, keepdims=True)
    m = jnp.where(jnp.isfinite(m), m, 0.0)
    p = jnp.exp(s - m)
    return p / jnp.maximum(jnp.sum(p, axis=-1, keepdims=True), 1e-30)

def mla_mixer(c_q, c_kv, k_rope, g_cq, g_ckv, w_uq, w_ukv, g_q, g_k, w_o, pos):
    B, S, _ = c_q.shape
    dt = c_q.dtype
    q = (rms_norm(c_q, g_cq) @ w_uq).reshape(B, S, MLA_HEADS, MLA_QK_DIM)
    kv = (rms_norm(c_kv, g_ckv) @ w_ukv).reshape(B, S, MLA_HEADS, MLA_NOPE_DIM + MLA_V_DIM)
    k_nope, v = kv[..., :MLA_NOPE_DIM], kv[..., MLA_NOPE_DIM:]
    k_r = jnp.broadcast_to(k_rope[:, :, None, :], (B, S, MLA_HEADS, MLA_ROPE_DIM))
    k = jnp.concatenate([k_r, k_nope], axis=-1)
    q = rope(rms_norm(q, g_q), pos, MLA_ROPE_DIM)
    k = rope(rms_norm(k, g_k), pos, MLA_ROPE_DIM)
    scale = MLA_QK_DIM ** -0.5

    def block(i):
        qb = lax.dynamic_slice_in_dim(q, i * Q_BLOCK, Q_BLOCK, axis=1)
        t = i * Q_BLOCK + jnp.arange(Q_BLOCK)
        s = jnp.einsum('bqhd,bkhd->bhqk', qb, k) * scale
        p = masked_softmax(s, pos[None, :] <= t[:, None])
        return jnp.einsum('bhqk,bkhd->bqhd', p.astype(dt), v)

    o = lax.map(block, jnp.arange(S // Q_BLOCK))
    o = jnp.moveaxis(o, 0, 1).reshape(B, S, MLA_HEADS * MLA_V_DIM)
    return o @ w_o

def conv_mixer(u2, b_glu, w_dw, b_dw, g_ln, b_ln, w_out, b_out):
    a, gate = jnp.split(u2 + b_glu, 2, axis=-1)
    u = a * jax.nn.sigmoid(gate)
    u = lax.conv_general_dilated(u, w_dw[:, None, :], (1,), [(CONV_WIDTH - 1, 0)],
                                 dimension_numbers=('NWC', 'WIO', 'NWC'),
                                 feature_group_count=CONV_CH) + b_dw
    u = jax.nn.silu(layer_norm(u, g_ln, b_ln))
    return u @ w_out + b_out

def compress(tok, pe, w1, w2):
    B, S, G, dh = tok.shape
    n_cmp = (S - CMP_BLOCK) // CMP_STRIDE + 1
    idx = (jnp.arange(n_cmp) * CMP_STRIDE)[:, None] + jnp.arange(CMP_BLOCK)[None, :]
    blocks = tok[:, idx] + pe[None, None, :, None, :]
    blocks = jnp.moveaxis(blocks, 2, 3).reshape(B, n_cmp, G, CMP_BLOCK * dh)
    return jax.nn.silu(blocks @ w1) @ w2

def nsa_mixer(q_raw, kv_raw, gate_logits, pe_k, pe_v, w_ck1, w_ck2, w_cv1, w_cv2, g_q, g_k, w_o, pos):
    B, S, _ = q_raw.shape
    dt = q_raw.dtype
    H, G, dh = NSA_HEADS, NSA_KV_GROUPS, NSA_HEAD_DIM
    hpg = H // G
    QB = NSA_Q_BLOCK
    q = rope(rms_norm(q_raw.reshape(B, S, H, dh), g_q), pos, NSA_ROPE_DIM)
    kv = kv_raw.reshape(B, S, 2 * NSA_N_BRANCH, G, dh)
    kc, vc, ks, vs, kw, vw = [kv[:, :, j] for j in range(2 * NSA_N_BRANCH)]
    n_cmp = (S - CMP_BLOCK) // CMP_STRIDE + 1
    cmp_pos = jnp.arange(n_cmp) * CMP_STRIDE + CMP_BLOCK - 1
    k_cmp = rope(rms_norm(compress(kc, pe_k, w_ck1, w_ck2), g_k), cmp_pos, NSA_ROPE_DIM)
    v_cmp = compress(vc, pe_v, w_cv1, w_cv2)
    n_slc = S // SLC_BLOCK
    top_n = min(SLC_TOP_N, n_slc)
    k_slc = rope(rms_norm(ks, g_k), pos, NSA_ROPE_DIM)
    k_slc_blk = k_slc.reshape(B, n_slc, SLC_BLOCK, G, dh).transpose(0, 3, 1, 2, 4)
    v_slc_blk = vs.reshape(B, n_slc, SLC_BLOCK, G, dh).transpose(0, 3, 1, 2, 4)
    c_start = jnp.arange(n_cmp) * CMP_STRIDE
    s_start = jnp.arange(n_slc) * SLC_BLOCK
    overlap = ((c_start[:, None] < s_start[None, :] + SLC_BLOCK)
               & (c_start[:, None] + CMP_BLOCK > s_start[None, :])).astype(jnp.float32)
    k_win = rope(rms_norm(kw, g_k), pos, NSA_ROPE_DIM)
    k_win_pad = jnp.pad(k_win, ((0, 0), (WINDOW, 0), (0, 0), (0, 0)))
    v_win_pad = jnp.pad(vw, ((0, 0), (WINDOW, 0), (0, 0), (0, 0)))
    scale = dh ** -0.5
    bi = jnp.arange(B)[:, None, None, None]
    gi = jnp.arange(G)[None, :, None, None]
    j_blk = jnp.arange(n_slc)

    def block(i):
        q0 = i * QB
        t = q0 + jnp.arange(QB)
        qb = lax.dynamic_slice_in_dim(q, q0, QB, axis=1).reshape(B, QB, G, hpg, dh)
        s_c = jnp.einsum('bqghd,bcgd->bghqc', qb, k_cmp) * scale
        p_c = masked_softmax(s_c, cmp_pos[None, :] <= t[:, None])
        o_c = jnp.einsum('bghqc,bcgd->bqghd', p_c.astype(dt), v_cmp)
        imp = jnp.einsum('bghqc,cn->bgqn', p_c, overlap)
        blk_t = t // SLC_BLOCK
        forced = ((j_blk[None, :] == 0) | (j_blk[None, :] == blk_t[:, None])
                  | (j_blk[None, :] == blk_t[:, None] - 1))
        imp = jnp.where(forced, FORCED_BLOCK_SCORE, imp)
        imp = jnp.where(j_blk[None, :] > blk_t[:, None], -jnp.inf, imp)
        _, idx = lax.top_k(imp, top_n)
        k_sel = k_slc_blk[bi, gi, idx]
        v_sel = v_slc_blk[bi, gi, idx]
        s_s = jnp.einsum('bqghd,bgqnkd->bghqnk', qb, k_sel) * scale
        kpos = idx[..., None] * SLC_BLOCK + jnp.arange(SLC_BLOCK)
        m_s = (kpos <= t[None, None, :, None, None])[:, :, None]
        p_s = masked_softmax(s_s.reshape(B, G, hpg, QB, top_n * SLC_BLOCK),
                             m_s.reshape(B, G, 1, QB, top_n * SLC_BLOCK))
        o_s = jnp.einsum('bghqnk,bgqnkd->bqghd', p_s.reshape(s_s.shape).astype(dt), v_sel)
        k_w = lax.dynamic_slice_in_dim(k_win_pad, q0, WINDOW + QB, axis=1)
        v_w = lax.dynamic_slice_in_dim(v_win_pad, q0, WINDOW + QB, axis=1)
        wpos = q0 - WINDOW + jnp.arange(WINDOW + QB)
        m_w = ((wpos[None, :] <= t[:, None]) & (wpos[None, :] > t[:, None] - WINDOW)
               & (wpos[None, :] >= 0))
        s_w = jnp.einsum('bqghd,bkgd->bghqk', qb, k_w) * scale
        p_w = masked_softmax(s_w, m_w)
        o_w = jnp.einsum('bghqk,bkgd->bqghd', p_w.astype(dt), v_w)
        return jnp.stack([o_c, o_s, o_w], axis=-2)

    o = lax.map(block, jnp.arange(S // QB))
    o = jnp.moveaxis(o, 0, 1).reshape(B, S, H, NSA_N_BRANCH, dh)
    g = jax.nn.sigmoid(gate_logits.reshape(B, S, H, NSA_N_BRANCH).astype(jnp.float32)).astype(dt)
    o = jnp.einsum('bshnd,bshn->bshd', o, g).reshape(B, S, H * dh)
    return o @ w_o

def hybrid_layer(x, pos, g_mix, w_in, g_cq, g_ckv, w_uq, w_ukv, g_q_mla, g_k_mla, w_o_mla,
                 b_glu, w_dw, b_dw, g_conv_ln, b_conv_ln, w_conv_out, b_conv_out,
                 pe_cmp_k, pe_cmp_v, w_cmp_k1, w_cmp_k2, w_cmp_v1, w_cmp_v2,
                 g_q_nsa, g_k_nsa, w_o_nsa, w_out, g_ffn, w_ff1, w_ff2):
    dt = x.dtype
    h = rms_norm(x, g_mix)
    z = h @ w_in
    c_q, c_kv, k_rope, u2, q_nsa, kv_nsa, gate_nsa, gate_mix = jnp.split(z, SPLIT_IDX, axis=-1)
    o_a = mla_mixer(c_q, c_kv, k_rope, g_cq, g_ckv, w_uq, w_ukv, g_q_mla, g_k_mla, w_o_mla, pos)
    o_b = conv_mixer(u2, b_glu, w_dw, b_dw, g_conv_ln, b_conv_ln, w_conv_out, b_conv_out)
    o_c = nsa_mixer(q_nsa, kv_nsa, gate_nsa, pe_cmp_k, pe_cmp_v, w_cmp_k1, w_cmp_k2,
                    w_cmp_v1, w_cmp_v2, g_q_nsa, g_k_nsa, w_o_nsa, pos)
    g_a, g_b, g_c = jnp.split(jax.nn.sigmoid(gate_mix.astype(jnp.float32)).astype(dt), N_MIXERS, axis=-1)
    x = x + (g_a * o_a + g_b * o_b + g_c * o_c) @ w_out
    h = rms_norm(x, g_ffn)
    x = x + jnp.square(jax.nn.relu(h @ w_ff1)) @ w_ff2
    return x

def first_inputs(seed: int = 0) -> dict:
    key = jax.random.key(seed)
    ks = iter(jax.random.split(key, 40))
    L = DEPTH
    res = (2.0 * DEPTH) ** -0.5

    def nrm(shape, scale):
        return jax.random.normal(next(ks), shape, jnp.float32) * scale

    def gain(shape):
        return 1.0 + nrm(shape, 0.02)

    return {
        "x": nrm((BATCH, SEQ, D_MODEL), 1.0),
        "g_mix": gain((L, D_MODEL)),
        "w_in": nrm((L, D_MODEL, D_IN), D_MODEL ** -0.5),
        "g_cq": gain((L, MLA_Q_RANK)),
        "g_ckv": gain((L, MLA_KV_RANK)),
        "w_uq": nrm((L, MLA_Q_RANK, MLA_HEADS * MLA_QK_DIM), MLA_Q_RANK ** -0.5),
        "w_ukv": nrm((L, MLA_KV_RANK, MLA_HEADS * (MLA_NOPE_DIM + MLA_V_DIM)), MLA_KV_RANK ** -0.5),
        "g_q_mla": gain((L, MLA_QK_DIM)),
        "g_k_mla": gain((L, MLA_QK_DIM)),
        "w_o_mla": nrm((L, MLA_HEADS * MLA_V_DIM, D_MODEL), (MLA_HEADS * MLA_V_DIM) ** -0.5),
        "b_glu": nrm((L, 2 * CONV_CH), 0.01),
        "w_dw": nrm((L, CONV_WIDTH, CONV_CH), CONV_WIDTH ** -0.5),
        "b_dw": nrm((L, CONV_CH), 0.01),
        "g_conv_ln": gain((L, CONV_CH)),
        "b_conv_ln": nrm((L, CONV_CH), 0.01),
        "w_conv_out": nrm((L, CONV_CH, D_MODEL), CONV_CH ** -0.5),
        "b_conv_out": nrm((L, D_MODEL), 0.01),
        "pe_cmp_k": nrm((L, CMP_BLOCK, NSA_HEAD_DIM), 0.1),
        "pe_cmp_v": nrm((L, CMP_BLOCK, NSA_HEAD_DIM), 0.1),
        "w_cmp_k1": nrm((L, CMP_BLOCK * NSA_HEAD_DIM, CMP_HIDDEN), (CMP_BLOCK * NSA_HEAD_DIM) ** -0.5),
        "w_cmp_k2": nrm((L, CMP_HIDDEN, NSA_HEAD_DIM), CMP_HIDDEN ** -0.5),
        "w_cmp_v1": nrm((L, CMP_BLOCK * NSA_HEAD_DIM, CMP_HIDDEN), (CMP_BLOCK * NSA_HEAD_DIM) ** -0.5),
        "w_cmp_v2": nrm((L, CMP_HIDDEN, NSA_HEAD_DIM), CMP_HIDDEN ** -0.5),
        "g_q_nsa": gain((L, NSA_HEAD_DIM)),
        "g_k_nsa": gain((L, NSA_HEAD_DIM)),
        "w_o_nsa": nrm((L, NSA_HEADS * NSA_HEAD_DIM, D_MODEL), (NSA_HEADS * NSA_HEAD_DIM) ** -0.5),
        "w_out": nrm((L, D_MODEL, D_MODEL), D_MODEL ** -0.5 * res),
        "g_ffn": gain((L, D_MODEL)),
        "w_ff1": nrm((L, D_MODEL, D_FF), D_MODEL ** -0.5),
        "w_ff2": nrm((L, D_FF, D_MODEL), D_FF ** -0.5 * res),
    }

def first_block(x, g_mix, w_in, g_cq, g_ckv, w_uq, w_ukv, g_q_mla, g_k_mla, w_o_mla,
              b_glu, w_dw, b_dw, g_conv_ln, b_conv_ln, w_conv_out, b_conv_out,
              pe_cmp_k, pe_cmp_v, w_cmp_k1, w_cmp_k2, w_cmp_v1, w_cmp_v2,
              g_q_nsa, g_k_nsa, w_o_nsa, w_out, g_ffn, w_ff1, w_ff2):
    pos = jnp.arange(x.shape[1])
    for l in range(DEPTH):
        x = hybrid_layer(x, pos, g_mix[l], w_in[l], g_cq[l], g_ckv[l], w_uq[l], w_ukv[l],
                         g_q_mla[l], g_k_mla[l], w_o_mla[l], b_glu[l], w_dw[l], b_dw[l],
                         g_conv_ln[l], b_conv_ln[l], w_conv_out[l], b_conv_out[l],
                         pe_cmp_k[l], pe_cmp_v[l], w_cmp_k1[l], w_cmp_k2[l], w_cmp_v1[l], w_cmp_v2[l],
                         g_q_nsa[l], g_k_nsa[l], w_o_nsa[l], w_out[l], g_ffn[l], w_ff1[l], w_ff2[l])
    return x


DEPTH_2 = 1

CTX_LEN = 256
GRID_W = 64
N_MOD = 6
EPS = 1e-6
DA_HEADS = 8
DA_QK = 64
DA_V = 2 * DA_QK
DA_QK_COLS = DA_HEADS * 2 * DA_QK
DA_WIDTH = DA_HEADS * DA_V
ROPE_THETA_2 = 10000.0
ROPE_FREQS = DA_QK // 4
RW_HEADS = 16
RW_HEAD = 64
RW_WIDTH = RW_HEADS * RW_HEAD
RW_W_LORA = 64
RW_A_LORA = 64
RW_G_LORA = 128
RW_SHIFT_CH = 3 * RW_WIDTH + RW_W_LORA + RW_A_LORA + RW_G_LORA
RW_LN_EPS = 64e-5
L2_EPS = 1e-12
RW_SPLIT_IDX = (RW_WIDTH, 2 * RW_WIDTH, 3 * RW_WIDTH, 3 * RW_WIDTH + RW_W_LORA, 3 * RW_WIDTH + RW_W_LORA + RW_A_LORA)
N_BRANCH = 2
IN_SPLIT_IDX = (DA_QK_COLS, 2 * DA_QK_COLS, 2 * DA_QK_COLS + DA_WIDTH, 2 * DA_QK_COLS + DA_WIDTH + RW_SHIFT_CH)
IN_WIDTH = 2 * DA_QK_COLS + DA_WIDTH + RW_SHIFT_CH + N_BRANCH * D_MODEL
PEER_HEADS = 8
N_KEYS = 128
N_EXPERTS = N_KEYS * N_KEYS
PEER_TOPK = 16
PEER_QDIM = 256
PEER_CHUNK = 128


def rmsnorm(x, g):
    xf = x.astype(jnp.float32)
    y = xf * lax.rsqrt(jnp.mean(xf * xf, axis=-1, keepdims=True) + EPS)
    return (y * g.astype(jnp.float32)).astype(x.dtype)

def modulate(h, shift, scale):
    return h * (1 + scale) + shift

def axial_angles(n_tokens):
    rows = n_tokens // GRID_W
    row = jnp.repeat(jnp.arange(rows, dtype=jnp.float32), GRID_W)
    col = jnp.tile(jnp.arange(GRID_W, dtype=jnp.float32), rows)
    inv = ROPE_THETA_2 ** (-jnp.arange(ROPE_FREQS, dtype=jnp.float32) / ROPE_FREQS)
    return jnp.stack([row[:, None] * inv, col[:, None] * inv], axis=1)

def apply_axial_rope(x, ang):
    xs = x.reshape(x.shape[:-1] + (2, 2, ROPE_FREQS))
    cos = jnp.cos(ang)[:, None, None, :, None, :].astype(x.dtype)
    sin = jnp.sin(ang)[:, None, None, :, None, :].astype(x.dtype)
    x1, x2 = xs[..., 0:1, :], xs[..., 1:2, :]
    out = jnp.concatenate([x1 * cos - x2 * sin, x2 * cos + x1 * sin], axis=-2)
    return out.reshape(x.shape)

def diff_heads(q, k, v, q_g, k_g, ang):
    B, T, _ = q.shape
    q = rmsnorm(q.reshape(B, T, DA_HEADS, 2, DA_QK), q_g)
    k = rmsnorm(k.reshape(B, T, DA_HEADS, 2, DA_QK), k_g)
    if ang is not None:
        q = apply_axial_rope(q, ang)
        k = apply_axial_rope(k, ang)
    q = q.transpose(0, 3, 2, 1, 4)
    k = k.transpose(0, 3, 2, 1, 4)
    v = v.reshape(B, T, DA_HEADS, DA_V).transpose(0, 2, 1, 3)
    return q, k, v

def diff_attention(q, k, v, lam):
    B, _, H, T, d = q.shape
    nb = T // Q_BLOCK
    qb = q.reshape(B, 2, H, nb, Q_BLOCK, d).transpose(3, 0, 1, 2, 4, 5)
    scale = d ** -0.5

    def one_block(q_blk):
        s = jnp.einsum('bmhqd,bmhkd->bmhqk', q_blk, k).astype(jnp.float32) * scale
        p = jax.nn.softmax(s, axis=-1)
        pd = (p[:, 0] - lam * p[:, 1]).astype(v.dtype)
        return jnp.einsum('bhqk,bhkd->bhqd', pd, v)

    o = lax.map(one_block, qb)
    return o.transpose(1, 0, 3, 2, 4).reshape(B, T, H * v.shape[-1])

def diff_post(o, out_g, lam_init):
    B, T, _ = o.shape
    o = rmsnorm(o.reshape(B, T, DA_HEADS, DA_V), out_g) * (1 - lam_init)
    return o.reshape(B, T, DA_WIDTH)

def centred_shift(z, w):
    zp = jnp.pad(z, ((0, 0), (1, 1), (0, 0)))
    return w[0] * zp[:, :-2] + w[1] * zp[:, 1:-1] + w[2] * zp[:, 2:]

def head_l2norm(t):
    th = t.reshape(t.shape[:-1] + (RW_HEADS, RW_HEAD)).astype(jnp.float32)
    th = th * lax.rsqrt(jnp.sum(th * th, axis=-1, keepdims=True) + L2_EPS)
    return th.reshape(t.shape).astype(t.dtype)

def dual(t):
    return jnp.stack([t, t])

def to_scan(t):
    t = jnp.stack([t[0], t[1][:, ::-1]]).astype(jnp.float32)
    return t.reshape(t.shape[:3] + (RW_HEADS, RW_HEAD)).transpose(2, 0, 1, 3, 4)

def from_scan(y):
    y = y.transpose(1, 2, 0, 3, 4)
    return y[0] + y[1][:, ::-1]

def rwkv_prepare(z, shift_w, w0, w_up, a0, a_up, k_k, k_a):
    z = centred_shift(z, shift_w)
    r, k, v, wd, ad, gd = jnp.split(z, RW_SPLIT_IDX, axis=-1)
    w_log = -jax.nn.softplus(-(w0[:, None, None, :] + jnp.einsum('btr,drc->dbtc', jnp.tanh(wd), w_up))) - 0.5
    decay = jnp.exp(-jnp.exp(w_log.astype(jnp.float32)))
    a = jax.nn.sigmoid(a0[:, None, None, :] + jnp.einsum('btr,drc->dbtc', ad, a_up))
    kk = head_l2norm(k * k_k)
    k_eff = k[None] * (1 + (a - 1) * k_a)
    scan_in = (to_scan(decay), to_scan(dual(kk)), to_scan(a), to_scan(k_eff), to_scan(dual(v)), to_scan(dual(r)))
    return scan_in, (r, k, v, gd)

def wkv_scan(s0, scan_in):
    def step(s, inp):
        w, kk, a, k, v, r = inp
        sa = jnp.einsum('dbhij,dbhj->dbhi', s, kk)
        s = s * w[..., None, :] - sa[..., :, None] * (kk * a)[..., None, :] + v[..., :, None] * k[..., None, :]
        return s, jnp.einsum('dbhij,dbhj->dbhi', s, r)
    return lax.scan(step, s0, scan_in)

def rwkv_post(y, r, k, v, gd, g_up, r_k, ln_g, ln_b):
    B, T, C = r.shape
    mu = jnp.mean(y, axis=-1, keepdims=True)
    var = jnp.mean(jnp.square(y - mu), axis=-1, keepdims=True)
    yn = ((y - mu) * lax.rsqrt(var + RW_LN_EPS)).reshape(B, T, C) * ln_g + ln_b
    hs = lambda t: t.reshape(B, T, RW_HEADS, RW_HEAD)
    bonus = jnp.sum(hs(r) * hs(k) * r_k, axis=-1, keepdims=True) * hs(v)
    g = jax.nn.sigmoid(gd) @ g_up
    return (yn.astype(r.dtype) + bonus.reshape(B, T, C)) * g

def merge_branches(o_a, o_b, z_gate, w_branch_a, w_branch_b, w_out):
    g_a, g_b = jnp.split(jax.nn.sigmoid(z_gate), N_BRANCH, axis=-1)
    return (g_a * (o_a @ w_branch_a) + g_b * (o_b @ w_branch_b)) @ w_out

def peer_ffn(h, peer_wq, peer_keys, peer_u, peer_v):
    B, T, D = h.shape
    tok = h.reshape(-1, PEER_CHUNK, D)

    def one_chunk(xc):
        q = (xc @ peer_wq).reshape(PEER_CHUNK, PEER_HEADS, 2, PEER_QDIM // 2)
        s = jnp.einsum('chpd,hpkd->chpk', q, peer_keys).astype(jnp.float32)
        sv, si = lax.top_k(s, PEER_TOPK)
        cand = (sv[..., 0, :, None] + sv[..., 1, None, :]).reshape(PEER_CHUNK, PEER_HEADS, PEER_TOPK * PEER_TOPK)
        cidx = (si[..., 0, :, None] * N_KEYS + si[..., 1, None, :]).reshape(PEER_CHUNK, PEER_HEADS, PEER_TOPK * PEER_TOPK)
        top_s, pos = lax.top_k(cand, PEER_TOPK)
        eidx = jnp.take_along_axis(cidx, pos, axis=-1)
        gate = jax.nn.softmax(top_s, axis=-1)
        act = jax.nn.gelu(jnp.einsum('chkd,cd->chk', peer_u[eidx], xc))
        return jnp.einsum('chk,chkd->cd', (gate * act).astype(xc.dtype), peer_v[eidx])

    return lax.map(one_chunk, tok).reshape(B, T, D)

def hybrid_layer_2(x, ctx, c, c_ctx, w_mod, b_mod, norm1_g, w_in, q_norm_g, k_norm_g, diff_lambda, diff_out_g,
                 rw_shift, rw_w0, rw_w_up, rw_a0, rw_a_up, rw_g_up, rw_k_k, rw_k_a, rw_r_k, rw_ln_g, rw_ln_b,
                 w_branch_a, w_branch_b, w_out, norm2_g, peer_wq, peer_keys, peer_u, peer_v, layer_idx, update_ctx):
    B, S, _ = x.shape
    lam_init = 0.8 - 0.6 * math.exp(-0.3 * layer_idx)
    mod_x = jnp.split((jax.nn.silu(c) @ w_mod + b_mod)[:, None, :], N_MOD, axis=-1)
    mod_c = jnp.split((jax.nn.silu(c_ctx) @ w_mod + b_mod)[None, None, :], N_MOD, axis=-1)
    zx = jnp.split(modulate(rmsnorm(x, norm1_g), mod_x[0], mod_x[1]) @ w_in, IN_SPLIT_IDX, axis=-1)
    zc = jnp.split(modulate(rmsnorm(ctx, norm1_g), mod_c[0], mod_c[1]) @ w_in, IN_SPLIT_IDX, axis=-1)

    qx, kx, vx = diff_heads(zx[0], zx[1], zx[2], q_norm_g, k_norm_g, axial_angles(S))
    qc, kc, vc = diff_heads(zc[0], zc[1], zc[2], q_norm_g, k_norm_g, None)
    lam = jnp.exp(jnp.sum(diff_lambda[0] * diff_lambda[1])) - jnp.exp(jnp.sum(diff_lambda[2] * diff_lambda[3])) + lam_init
    k_all = jnp.concatenate([kc, kx], axis=3)
    v_all = jnp.concatenate([vc, vx], axis=2)
    o_ax = diff_post(diff_attention(qx, k_all, v_all, lam), diff_out_g, lam_init)

    scan_c, aux_c = rwkv_prepare(zc[3], rw_shift, rw_w0, rw_w_up, rw_a0, rw_a_up, rw_k_k, rw_k_a)
    scan_x, aux_x = rwkv_prepare(zx[3], rw_shift, rw_w0, rw_w_up, rw_a0, rw_a_up, rw_k_k, rw_k_a)
    s0 = jnp.zeros((2, B, RW_HEADS, RW_HEAD, RW_HEAD), jnp.float32)
    s_ctx, y_c = wkv_scan(s0, scan_c)
    _, y_x = wkv_scan(s_ctx, scan_x)
    o_bx = rwkv_post(from_scan(y_x), *aux_x, rw_g_up, rw_r_k, rw_ln_g, rw_ln_b)

    x = x + mod_x[2] * merge_branches(o_ax, o_bx, zx[4], w_branch_a, w_branch_b, w_out)
    x = x + mod_x[5] * peer_ffn(modulate(rmsnorm(x, norm2_g), mod_x[3], mod_x[4]), peer_wq, peer_keys, peer_u, peer_v)

    if update_ctx:
        o_ac = diff_post(diff_attention(qc, kc, vc, lam), diff_out_g, lam_init)
        o_bc = rwkv_post(from_scan(y_c), *aux_c, rw_g_up, rw_r_k, rw_ln_g, rw_ln_b)
        ctx = ctx + mod_c[2] * merge_branches(o_ac, o_bc, zc[4], w_branch_a, w_branch_b, w_out)
        ctx = ctx + mod_c[5] * peer_ffn(modulate(rmsnorm(ctx, norm2_g), mod_c[3], mod_c[4]), peer_wq, peer_keys, peer_u, peer_v)
    return x, ctx

def second_inputs(seed: int = 0) -> dict:
    key = jax.random.key(seed)
    ks = iter(jax.random.split(key, 40))
    nrm = lambda shape, s: jax.random.normal(next(ks), shape, jnp.float32) * s
    L, D = DEPTH_2, D_MODEL
    return {
        'x': nrm((BATCH, SEQ, D), 1.0),
        'c': nrm((BATCH, D), 1.0),
        'ctx': nrm((BATCH, CTX_LEN, D), 1.0),
        'c_ctx': nrm((D,), 1.0),
        'w_mod': nrm((L, D, N_MOD * D), D ** -0.5),
        'b_mod': nrm((L, N_MOD * D), 0.01),
        'norm1_g': 1.0 + nrm((L, D), 0.02),
        'w_in': nrm((L, D, IN_WIDTH), D ** -0.5),
        'q_norm_g': 1.0 + nrm((L, DA_QK), 0.02),
        'k_norm_g': 1.0 + nrm((L, DA_QK), 0.02),
        'diff_lambda': nrm((L, 4, DA_QK), 0.1),
        'diff_out_g': 1.0 + nrm((L, DA_V), 0.02),
        'rw_shift': jnp.array([0.25, 0.5, 0.25], jnp.float32)[None, :, None] + nrm((L, 3, RW_SHIFT_CH), 0.1),
        'rw_w0': -6.0 + 5.0 * jax.random.uniform(next(ks), (L, 2, RW_WIDTH), jnp.float32),
        'rw_w_up': nrm((L, 2, RW_W_LORA, RW_WIDTH), 0.1 * RW_W_LORA ** -0.5),
        'rw_a0': nrm((L, 2, RW_WIDTH), 0.5),
        'rw_a_up': nrm((L, 2, RW_A_LORA, RW_WIDTH), 0.1 * RW_A_LORA ** -0.5),
        'rw_g_up': nrm((L, RW_G_LORA, RW_WIDTH), RW_G_LORA ** -0.5),
        'rw_k_k': 0.85 + nrm((L, RW_WIDTH), 0.1),
        'rw_k_a': 1.0 + nrm((L, RW_WIDTH), 0.05),
        'rw_r_k': nrm((L, RW_HEADS, RW_HEAD), 0.1),
        'rw_ln_g': 1.0 + nrm((L, RW_WIDTH), 0.02),
        'rw_ln_b': nrm((L, RW_WIDTH), 0.01),
        'w_branch_a': nrm((L, DA_WIDTH, D), DA_WIDTH ** -0.5),
        'w_branch_b': nrm((L, RW_WIDTH, D), RW_WIDTH ** -0.5),
        'w_out': nrm((L, D, D), D ** -0.5),
        'norm2_g': 1.0 + nrm((L, D), 0.02),
        'peer_wq': nrm((L, D, PEER_HEADS * PEER_QDIM), D ** -0.5),
        'peer_keys': nrm((L, PEER_HEADS, 2, N_KEYS, PEER_QDIM // 2), (PEER_QDIM // 2) ** -0.5),
        'peer_u': nrm((L, N_EXPERTS, D), D ** -0.5),
        'peer_v': nrm((L, N_EXPERTS, D), PEER_HEADS ** -0.5),
    }

def second_block(x, c, ctx, c_ctx, w_mod, b_mod, norm1_g, w_in, q_norm_g, k_norm_g, diff_lambda, diff_out_g,
              rw_shift, rw_w0, rw_w_up, rw_a0, rw_a_up, rw_g_up, rw_k_k, rw_k_a, rw_r_k, rw_ln_g, rw_ln_b,
              w_branch_a, w_branch_b, w_out, norm2_g, peer_wq, peer_keys, peer_u, peer_v):
    for l in range(DEPTH_2):
        x, ctx = hybrid_layer_2(
            x, ctx, c, c_ctx, w_mod[l], b_mod[l], norm1_g[l], w_in[l], q_norm_g[l], k_norm_g[l], diff_lambda[l],
            diff_out_g[l], rw_shift[l], rw_w0[l], rw_w_up[l], rw_a0[l], rw_a_up[l], rw_g_up[l], rw_k_k[l], rw_k_a[l],
            rw_r_k[l], rw_ln_g[l], rw_ln_b[l], w_branch_a[l], w_branch_b[l], w_out[l], norm2_g[l], peer_wq[l],
            peer_keys[l], peer_u[l], peer_v[l], layer_idx=l, update_ctx=l < DEPTH_2 - 1)
    return x


def setup_inputs(seed=0):
    out = dict(first_inputs(seed))
    for name, value in second_inputs(seed + 1).items():
        if name != "x":
            out[name + "_2"] = value
    return out


def reference(
    x, g_mix, w_in, g_cq, g_ckv, w_uq, w_ukv, g_q_mla, g_k_mla, w_o_mla, b_glu, w_dw, b_dw,
    g_conv_ln, b_conv_ln, w_conv_out, b_conv_out, pe_cmp_k, pe_cmp_v, w_cmp_k1, w_cmp_k2,
    w_cmp_v1, w_cmp_v2, g_q_nsa, g_k_nsa, w_o_nsa, w_out, g_ffn, w_ff1, w_ff2, c_2, ctx_2,
    c_ctx_2, w_mod_2, b_mod_2, norm1_g_2, w_in_2, q_norm_g_2, k_norm_g_2, diff_lambda_2,
    diff_out_g_2, rw_shift_2, rw_w0_2, rw_w_up_2, rw_a0_2, rw_a_up_2, rw_g_up_2, rw_k_k_2,
    rw_k_a_2, rw_r_k_2, rw_ln_g_2, rw_ln_b_2, w_branch_a_2, w_branch_b_2, w_out_2, norm2_g_2,
    peer_wq_2, peer_keys_2, peer_u_2, peer_v_2,
):
    x = first_block(
        x, g_mix, w_in, g_cq, g_ckv, w_uq, w_ukv, g_q_mla, g_k_mla, w_o_mla, b_glu, w_dw, b_dw,
        g_conv_ln, b_conv_ln, w_conv_out, b_conv_out, pe_cmp_k, pe_cmp_v, w_cmp_k1, w_cmp_k2,
        w_cmp_v1, w_cmp_v2, g_q_nsa, g_k_nsa, w_o_nsa, w_out, g_ffn, w_ff1, w_ff2,
    )
    return second_block(
        x, c_2, ctx_2, c_ctx_2, w_mod_2, b_mod_2, norm1_g_2, w_in_2, q_norm_g_2, k_norm_g_2,
        diff_lambda_2, diff_out_g_2, rw_shift_2, rw_w0_2, rw_w_up_2, rw_a0_2, rw_a_up_2,
        rw_g_up_2, rw_k_k_2, rw_k_a_2, rw_r_k_2, rw_ln_g_2, rw_ln_b_2, w_branch_a_2,
        w_branch_b_2, w_out_2, norm2_g_2, peer_wq_2, peer_keys_2, peer_u_2, peer_v_2,
    )


_drawn_inputs = setup_inputs


def setup_inputs(seed=0):
    import zlib

    import numpy as np

    out = dict(_drawn_inputs(seed))
    spreads = {}
    factors = {'g_mix': 5.167,
     'g_cq': 8.0,
     'g_ckv': 8.0,
     'g_q_mla': 8.0,
     'g_k_mla': 8.0,
     'b_glu': 8.0,
     'b_dw': 6.498,
     'g_conv_ln': 6.046,
     'b_conv_ln': 8.0,
     'b_conv_out': 7.457,
     'pe_cmp_k': 8.0,
     'pe_cmp_v': 3.734,
     'g_q_nsa': 8.0,
     'g_k_nsa': 8.0,
     'g_ffn': 2.782,
     'b_mod_2': 3.873,
     'norm1_g_2': 6.38,
     'q_norm_g_2': 46.556,
     'k_norm_g_2': 45.433,
     'diff_lambda_2': 2.907,
     'diff_out_g_2': 59.104,
     'rw_w_up_2': 52.258,
     'rw_a_up_2': 6.204,
     'rw_ln_g_2': 64.0,
     'rw_ln_b_2': 64.0,
     'norm2_g_2': 32.496,
     'rw_a0_2': 8.0,
     'rw_k_k_2': 3.14,
     'rw_k_a_2': 5.269}
    for name, (base, spread) in spreads.items():
        noise = np.random.default_rng([zlib.crc32(name.encode()), seed]).standard_normal(out[name].shape)
        drawn = base * np.exp(spread * noise) if base else spread * noise
        out[name] = jnp.asarray(drawn.astype(out[name].dtype))
    for name, factor in factors.items():
        out[name] = (out[name] * factor).astype(out[name].dtype)
    return out
```

```python
from contextlib import ExitStack

import numpy as np

import concourse.bass as bass
from concourse import mybir
from concourse.alu_op_type import AluOpType as ALU

F32 = mybir.dt.float32
U32 = mybir.dt.uint32
ACT = mybir.ActivationFunctionType
AX = mybir.AxisListType

P = 128
T = 256
TT = T // P
D = 1024
DC = D // P
EPS = 1e-6
NEG = -1e30
LAYERS = 2

MH, MQK, MROPE, MNOPE, MV = 8, 96, 32, 64, 64
NH, NG, ND, NROPE, NCMP = 8, 2, 64, 16, 15
CONV_W = 31
C_CQ, C_CKV, C_U, C_QN, C_KVN, C_GN, C_GM = 0, 384, 672, 1696, 2208, 2976, 3000

SLOT = 4608
SLOTS = 3
MEM_COLS = 53200

NA_LAYER, ND_LAYER, NA_ATT, ND_ATT, NA_SCAN, ND_SCAN, STEPS = 92, 64, 120, 24, 24, 36, 8


def sections(layer, att, scan):
    return {"layers": (0, layer), "attention": (LAYERS * layer, 0), "scan": (LAYERS * layer + att, scan),
            "post": (LAYERS * layer + att + STEPS * scan, 0)}


SECTIONS_ACT = sections(NA_LAYER, NA_ATT, NA_SCAN)
SECTIONS_DVE = sections(ND_LAYER, ND_ATT, ND_SCAN)

ITEMS1 = ([("u_gate", 4096), ("u_a", 4096), ("cq", 3072), ("ckv_uq", 4608), ("ukv_kvn2", 4288),
           ("qn", 4096), ("kvn1", 4096), ("cmp", 4096)]
          + [(f"{m}{n}", 4096) for m in "ABC" for n in ("g0", "g1", "o")]
          + [("out0", 4096), ("out1", 4096)]
          + [(f"ff1_{i}", 4096) for i in range(8)] + [(f"ff2_{i}", 4096) for i in range(8)]
          + [("pad", 0)])
ITEMS2 = ([(f"mod{i}", 4096) for i in range(12)]
          + [("q0", 4096), ("q1", 4096), ("k0", 4096), ("k1", 4096), ("v0", 4096), ("v1", 4096)]
          + [(f"rw{i}", 4096) for i in range(6)] + [("rw6", 2048)]
          + [("g0A", 4096), ("g1A", 4096), ("oA0", 4096), ("oA1", 4096),
             ("g0B", 4096), ("g1B", 4096), ("oB0", 4096), ("oB1", 4096), ("out0", 4096), ("out1", 4096)]
          + [(f"wq{i}", 4096) for i in range(4)])


def offsets(items):
    out, at = {}, 0
    for name, n in items:
        out[name] = at
        at += n
    return out, at


def layout(fields):
    return offsets(fields)


VEC1 = [("g_mix", 8), ("g_cq", 3), ("g_ckv", 2), ("b_glu", 8), ("b_dw", 4), ("g_ln", 4), ("b_ln", 4),
        ("b_co", 8), ("g_ffn", 8), ("w_dw", 4 * CONV_W), ("pe", 32), ("k2", 64), ("v2", 64),
        ("g_q_mla", 96), ("g_k_mla", 96), ("g_q_nsa", 64), ("g_k_nsa", 64)]
CON = [("ident", 128), ("cmask", 256), ("cmpmask", 2 * NCMP), ("mcos", 32), ("msin", 32),
       ("ncos", 16), ("nsin", 16), ("ccos", 8), ("csin", 8), ("eps", 1), ("l2eps", 1), ("lneps", 1), ("ones", 64)]
CON2 = [("acos", 64), ("asin", 64), ("id2", 64), ("onesbd", 128), ("strict", 128), ("incl", 128),
        ("level", 6 * 128), ("iota16", 16)]
VEC2 = [("norm1", 8), ("norm2", 8), ("b_mod", 32), ("c", 16), ("q_norm", 64), ("k_norm", 64), ("lam", 256),
        ("out_g", 128), ("shift", 78), ("w0", 16), ("a0", 16), ("k_k", 8), ("k_a", 8), ("r_k", 8),
        ("ln_g", 8), ("ln_b", 8)]


def constants():
    o, n = layout(CON)
    c = np.zeros((P, n), np.float32)
    p = np.arange(P)

    def put(name, a):
        a = np.asarray(a, np.float32).reshape(a.shape[0], -1)
        c[:a.shape[0], o[name]:o[name] + a.shape[1]] = a

    put("ident", np.eye(P))
    put("cmask", np.concatenate([np.zeros((P, P)), np.where(p[None, :] <= p[:, None], 0.0, NEG)], 1))
    t = p[:, None] + P * np.arange(TT)[None, :]
    cp = np.arange(NCMP) * 16 + 31
    put("cmpmask", np.where(cp[None, None, :] <= t[:, :, None], 0.0, NEG))

    def rot(pos, rot_dim, theta):
        half = rot_dim // 2
        inv = np.power(np.float32(theta), -np.arange(half, dtype=np.float32) * np.float32(2.0 / rot_dim))
        ang = pos[..., None].astype(np.float32) * inv.astype(np.float32)
        return np.cos(ang), np.sin(ang)

    for name, (cs, sn) in (("m", rot(t, MROPE, 500000.0)), ("n", rot(t, NROPE, 500000.0)),
                           ("c", rot(np.tile(cp, NG), NROPE, 500000.0))):
        put(name + "cos", cs)
        put(name + "sin", sn)
    c[:, o["eps"]] = EPS
    c[:, o["l2eps"]] = 1e-12
    c[:, o["lneps"]] = 64e-5
    c[:, o["ones"]:o["ones"] + 64] = 1.0
    return c


def constants2():
    o, n = layout(CON2)
    c = np.zeros((P, n), np.float32)
    p = np.arange(P)

    def put(name, a):
        a = np.asarray(a, np.float32).reshape(P, -1)
        c[:, o[name]:o[name] + a.shape[1]] = a

    t = p[:, None] + P * np.arange(TT)[None, :]
    inv = (10000.0 ** (-np.arange(16, dtype=np.float32) / 16)).astype(np.float32)
    ang = np.stack([(t // 64).astype(np.float32)[..., None] * inv, (t % 64).astype(np.float32)[..., None] * inv], 2)
    put("acos", np.cos(ang))
    put("asin", np.sin(ang))
    put("id2", np.tile(np.eye(64), (2, 1)))
    put("onesbd", p[:, None] // 64 == p[None, :] // 64)
    s = np.arange(64)
    before = np.stack([s[:, None] < s[None, :], s[:, None] > s[None, :]], 1)
    put("strict", np.tile(before, (2, 1, 1)))
    put("incl", np.tile(before | np.eye(64, dtype=bool)[:, None, :], (2, 1, 1)))
    levels = []
    for m in (1, 2, 4, 8, 16, 32):
        same = (s[:, None] // (2 * m) == s[None, :] // (2 * m)) & (s[:, None] // m != s[None, :] // m)
        levels.append(before & same[:, None, :])
    put("level", np.tile(np.stack(levels, 1), (2, 1, 1, 1)))
    put("iota16", np.tile(np.arange(16), (P, 1)))
    return c


def km(w):
    k, n = w.shape
    return w.reshape(k // P, P, n).transpose(1, 0, 2).reshape(P, -1)


def cols(v):
    return v.reshape(-1, P).T


def rows(v):
    return np.broadcast_to(v.reshape(1, -1), (P, v.size))


KV_ORDER = np.concatenate([np.arange(o, o + 64) for o in (0, 128, 64, 192)] + [np.arange(256, 512)])


def pack_weights1(a, l):
    w = a["w_in"][l]
    u = C_U
    parts = [km(w[:, u + 512:u + 1024]), km(w[:, u:u + 512]), km(w[:, C_CQ:C_CKV]),
             km(w[:, C_CKV:C_U]), km(a["w_uq"][l]), km(a["w_ukv"][l]), km(w[:, C_KVN + 512:C_GM]),
             km(w[:, C_QN:C_KVN]), km(w[:, C_KVN:C_KVN + 512][:, KV_ORDER])]
    c1 = [a[n][l].reshape(32, 64, P).transpose(1, 0, 2).reshape(64, -1) for n in ("w_cmp_k1", "w_cmp_v1")]
    parts.append(np.concatenate(c1, 0))
    for m, o in enumerate(("w_o_mla", "w_conv_out", "w_o_nsa")):
        g = C_GM + m * D
        parts += [km(w[:, g:g + 512]), km(w[:, g + 512:g + 1024]), km(a[o][l])]
    parts += [km(a["w_out"][l][:, :512]), km(a["w_out"][l][:, 512:])]
    parts += [km(a["w_ff1"][l][:, i * 512:(i + 1) * 512]) for i in range(8)]
    parts += [km(a["w_ff2"][l][i * 512:(i + 1) * 512]) for i in range(8)]
    return np.concatenate(parts, 1)


def pack_vectors1(a, l):
    f = {"g_mix": cols(a["g_mix"][l]), "g_cq": cols(a["g_cq"][l]), "g_ckv": cols(a["g_ckv"][l]),
         "b_glu": cols(a["b_glu"][l]), "b_dw": cols(a["b_dw"][l]), "g_ln": cols(a["g_conv_ln"][l]),
         "b_ln": cols(a["b_conv_ln"][l]), "b_co": cols(a["b_conv_out"][l]), "g_ffn": cols(a["g_ffn"][l]),
         "w_dw": a["w_dw"][l].reshape(CONV_W, 4, P).transpose(2, 1, 0).reshape(P, -1),
         "pe": np.concatenate([a["pe_cmp_k"][l].T, a["pe_cmp_v"][l].T], 0),
         "k2": a["w_cmp_k2"][l], "v2": a["w_cmp_v2"][l],
         "g_q_mla": rows(a["g_q_mla"][l]), "g_k_mla": rows(a["g_k_mla"][l]),
         "g_q_nsa": rows(a["g_q_nsa"][l]), "g_k_nsa": rows(a["g_k_nsa"][l])}
    return np.concatenate([f[n] for n, _ in VEC1], 1)


def pack_weights2(a):
    g = {n[:-2]: v[0] for n, v in a.items() if n.endswith("_2") and v.ndim > 1 and n not in ("c_2", "ctx_2")}
    w, m = g["w_in"], g["w_mod"]
    parts = [km(m[:, i * 512:(i + 1) * 512]) for i in range(12)]
    parts += [km(w[:, i * 512:(i + 1) * 512]) for i in range(6)]
    parts += [km(w[:, 3072 + i * 512:min(3072 + (i + 1) * 512, 6400)]) for i in range(7)]
    for i, n in enumerate(("w_branch_a", "w_branch_b")):
        gate = w[:, 6400 + i * D:6400 + (i + 1) * D]
        parts += [km(gate[:, :512]), km(gate[:, 512:]), km(g[n][:, :512]), km(g[n][:, 512:])]
    parts += [km(g["w_out"][:, :512]), km(g["w_out"][:, 512:])]
    parts += [km(g["peer_wq"][:, i * 512:(i + 1) * 512]) for i in range(4)]
    up = np.concatenate([g["rw_w_up"], g["rw_a_up"]], 1).transpose(1, 0, 2).reshape(P, -1)
    keys = g["peer_keys"].reshape(16, P, P).transpose(2, 0, 1).reshape(P, -1)
    parts += [up, g["rw_g_up"], keys]
    return np.concatenate(parts, 1)


def pack_vectors2(a):
    b = a["b_mod_2"][0]
    r = lambda v: cols(v.reshape(-1))
    f = {"norm1": cols(a["norm1_g_2"][0]), "norm2": cols(a["norm2_g_2"][0]),
         "b_mod": np.concatenate([cols(b[m * D:(m + 1) * D]) for m in (0, 1, 3, 4)], 1),
         "c": np.stack([cols(a["c_2"][0]), cols(a["c_ctx_2"])], 2).reshape(P, 16),
         "q_norm": rows(a["q_norm_g_2"][0]), "k_norm": rows(a["k_norm_g_2"][0]), "lam": rows(a["diff_lambda_2"][0]),
         "out_g": rows(a["diff_out_g_2"][0]), "shift": r(a["rw_shift_2"][0]),
         "w0": r(a["rw_w0_2"][0]), "a0": r(a["rw_a0_2"][0]), "k_k": r(a["rw_k_k_2"][0]), "k_a": r(a["rw_k_a_2"][0]),
         "r_k": r(a["rw_r_k_2"][0]), "ln_g": r(a["rw_ln_g_2"][0]), "ln_b": r(a["rw_ln_b_2"][0])}
    return np.concatenate([f[n] for n, _ in VEC2], 1)


def gate_rows2(a):
    b = a["b_mod_2"][0]
    return np.concatenate([rows(b[2 * D:3 * D]), rows(b[5 * D:6 * D])], 1)


class Signal:

    def __init__(self, sem, per):
        self.sem, self.per = sem, per

    def at(self, l, i=0):
        return self.sem, l * self.per + i + 1


class PsumRing:

    def __init__(self, banks, full, free, sections):
        self.banks, self.full, self.free, self.sections = banks, full, free, sections
        self.filled = {name: [] for name in sections}
        self.emptied = {name: [] for name in sections}
        self.pe_section = self.section = "layers"

    def count(self, section, l, n):
        before, per = self.sections[section]
        return before + l * per + n + 1

    def open(self, pe, l, tag):
        tags = self.filled[self.pe_section]
        tags.append(tag)
        n = len(tags) - 1
        pe.wait_ge(self.free, self.count(self.pe_section, l, n))
        return self.banks[:, n % 4, :]

    def take(self, eng, l, tag):
        tags = self.emptied[self.section]
        tags.append(tag)
        n = len(tags) - 1
        eng.wait_ge(self.full, self.count(self.section, l, n))
        return self.banks[:, n % 4, :]

    def peek(self, eng, section, tag, k):
        n = [i for i, t in enumerate(self.filled[section]) if t == tag][k]
        eng.wait_ge(self.full, self.count(section, 0, n))
        return self.banks[:, n % 4, :]

    def check(self, section):
        f, e = self.filled[section], self.emptied[section]
        assert f == e, [z for z in zip(f + [None] * 9, e + [None] * 9) if z[0] != z[1]][:3]


class WeightRing:

    def __init__(self, slots, landed, used):
        self.slots, self.landed, self.used = slots, landed, used

    def view(self, n, count):
        s = (n % SLOTS) * SLOT
        return self.slots[:, s:s + count]

    def loads_before(self, n):
        return sum(1 for m in range(n % SLOTS, n + 1, SLOTS) if ITEMS1[m][1])


def km_view(ap, n):
    return ap.rearrange("p (k n) -> p k n", n=n)


def build_program(nc, W1, V1, K1, W2, VV2, K2, R2, PU, PV, xin, cin, out):
    ctx = ExitStack()
    mem = ctx.enter_context(nc.sbuf_tensor("mem", [P, MEM_COLS], F32))
    psum = ctx.enter_context(nc.psum_tensor("psum", [P, 8, 512], F32))
    used_cols = [0]

    def sb(n, at=None):
        if at is None:
            at = used_cols[0]
            used_cols[0] += n
        return mem[:, at:at + n]

    def sem(name):
        return ctx.enter_context(nc.semaphore(name))

    def signal(name, per=1):
        return Signal(sem(name), per)

    def bc(ap, axis, n):
        ap = ap.unsqueeze(axis)
        shape = list(ap.shape)
        shape[axis] = n
        return ap.to_broadcast(shape)

    x = sb(TT * D).rearrange("p (t n) -> p t n", t=TT)
    hT = sb(DC * T).rearrange("p (c t) -> p c t", c=DC)
    slots = sb(SLOTS * SLOT)
    vo1, nv1 = layout(VEC1)
    co, ncon = layout(CON)
    vec, con = sb(nv1), sb(ncon)
    V = {n: vec[:, vo1[n]:vo1[n] + w] for n, w in VEC1}
    C = {n: con[:, co[n]:co[n] + w] for n, w in CON}
    ident = C["ident"]
    vo2, nv2 = layout(VEC2)
    co2, ncon2 = layout(CON2)
    vec2, con2 = sb(nv2), sb(ncon2)
    V2 = {n: vec2[:, vo2[n]:vo2[n] + w] for n, w in VEC2}
    C2 = {n: con2[:, co2[n]:co2[n] + w] for n, w in CON2}
    base = used_cols[0]

    junk = sb(2560)
    xn = junk[:, 0:2048].rearrange("p (t n) -> p t n", t=TT)
    sg = sb(1024).rearrange("p (c t) -> p c t", c=4)
    upad = sb(4 * (T + CONV_W - 1)).rearrange("p (c t) -> p c t", c=4)
    cacc = sb(1024).rearrange("p (c t) -> p c t", c=4)
    cvT = sb(1024).rearrange("p (c t) -> p c t", c=4)
    r1 = used_cols[0]
    cq = sb(768).rearrange("p (t n) -> p t n", t=TT)
    ckvr = sb(576).rearrange("p (t n) -> p t n", t=TT)
    cqT = sb(768).rearrange("p (c t) -> p c t", c=3)
    ckvT = sb(512).rearrange("p (c t) -> p c t", c=2)
    r2 = used_cols[0]
    qm = sb(1536).rearrange("p (t h n) -> p t h n", t=TT, h=MH)
    kf = sb(1536).rearrange("p (t h n) -> p t h n", t=TT, h=MH)
    r3 = used_cols[0]
    qT = sb(2048).rearrange("p (h t) -> p h t", h=MH)
    kT = sb(2048).rearrange("p (h t) -> p h t", h=MH)
    vm = sb(1024).rearrange("p (t h n) -> p t h n", t=TT, h=MH)
    S = sb(8 * 384).rearrange("p (h n) -> p h n", h=8)
    PT = sb(8 * 384).rearrange("p (h n) -> p h n", h=8)
    oTm = sb(1024).rearrange("p (c t) -> p c t", c=4)
    oTn = sb(1024).rearrange("p (c t) -> p c t", c=4)
    qn = sb(1024).rearrange("p (t h n) -> p t h n", t=TT, h=NH)
    kvn = sb(TT * 792).rearrange("p (t n) -> p t n", t=TT)
    nk = sb(512).rearrange("p (s t g n) -> p s t g n", s=2, t=TT, g=NG)
    small = sb(512)
    gates = sb(48)
    hid = sb(180)
    kc = sb(64)
    scmp = sb(240).rearrange("p (t h n) -> p t h n", t=TT, h=NH)
    pcmp = sb(512).rearrange("p (t h n) -> p t h n", t=TT, h=NH)
    vbd = sb(512).rearrange("p (c n) -> p c n", c=4)
    blk = sb(960, r1).rearrange("p (l g c) -> p l g c", l=32, g=NG)
    kcT = sb(512, r1 + 960).rearrange("p (g t) -> p g t", g=NG)
    pcT = sb(512, r1 + 1472).rearrange("p (g t) -> p g t", g=NG)
    nkT = sb(1024, r2).rearrange("p (s g t) -> p s g t", s=2, g=NG)
    kcmpT = sb(30, r2 + 1024)
    qnT = qT
    gsig = sb(4096, r2).rearrange("p (b c t) -> p b c t", b=2, c=DC)
    mg = sb(2048, r2 + 4096).rearrange("p (c t) -> p c t", c=DC)
    fT = sb(8192, r2).rearrange("p (f t) -> p f t", f=32)
    assert r2 + 8192 <= MEM_COLS
    ss, sd, rs = small[:, 0:16], small[:, 16:32], small[:, 32:48]
    mx, neg, se, scl = (small[:, 64 + 16 * i:80 + 16 * i].rearrange("p (h t) -> p h t", h=8) for i in range(4))
    stats = small[:, 128:140].rearrange("p (t n) -> p t n", t=TT)
    aggr = small[:, 140:144].rearrange("p (t n) -> p t n", t=TT)
    css, csd, crs = small[:, 144:148], small[:, 148:152], small[:, 152:156]
    cmx, cse, cgs = small[:, 160:176], small[:, 176:192], small[:, 192:208]
    lsd, lrs = small[:, 208:210], small[:, 210:212]
    nss, nsd, nrs = small[:, 216:218], small[:, 218:220], small[:, 220:222]

    act_ring = PsumRing(psum[:, 0:4, :], sem("act_bank_full"), sem("act_bank_free"), SECTIONS_ACT)
    dve_ring = PsumRing(psum[:, 4:8, :], sem("dve_bank_full"), sem("dve_bank_free"), SECTIONS_DVE)
    weights = WeightRing(slots, [sem(f"weights_landed{s}") for s in range(SLOTS)], sem("weights_used"))
    pe_step, act_step, dve_step = sem("pe_step"), sem("act_step"), sem("dve_step")
    const_landed, vec_landed, x_landed = sem("const_landed"), sem("vec_landed"), sem("x_landed")
    layer_done = signal("layer_done")
    sumsq_ready = signal("sumsq_ready", 2)
    root_ready = signal("root_ready", 2)
    xn_ready = signal("xn_ready", 2)
    hT_by_act, hT_by_dve = signal("hT_by_act", 2), signal("hT_by_dve", 2)
    glu_gate_ready = signal("glu_gate_ready")
    latent_root_ready = signal("latent_root_ready")
    latent_ready = signal("latent_ready")
    latentT_ready = signal("latentT_ready")
    qm_copied = signal("qm_copied")
    vm_ready = signal("vm_ready")
    kvn_copied = signal("kvn_copied")
    qn_copied = signal("qn_copied")
    gates_ready = signal("gates_ready")
    conv_ready = signal("conv_ready")
    ln_var_ready, ln_root_ready = signal("ln_var_ready"), signal("ln_root_ready")
    conv_normed = signal("conv_normed")
    conv_silu_parts = signal("conv_silu_parts")
    conv_act_ready = signal("conv_act_ready")
    head_sumsq_ready, head_root_ready = signal("head_sumsq_ready", 5), signal("head_root_ready", 5)
    heads_ready = signal("heads_ready", 5)
    qkT_ready = signal("qkT_ready", 2)
    score_max_ready = signal("score_max_ready", 6)
    exp_ready = signal("exp_ready", 6)
    probs_ready = signal("probs_ready", 6)
    probsT_ready = signal("probsT_ready", 6)
    mla_out_ready = signal("mla_out_ready")
    blocks_copied = signal("blocks_copied")
    blocks_ready = signal("blocks_ready")
    hidden_parts_ready = signal("hidden_parts_ready")
    hidden_ready = signal("hidden_ready")
    kcmpT_ready = signal("kcmpT_ready")
    vcmp_ready = signal("vcmp_ready")
    cmp_shifted_ready, cmp_exp_ready = signal("cmp_shifted_ready"), signal("cmp_exp_ready")
    cmp_probs_ready, cmp_probsT_ready = signal("cmp_probs_ready"), signal("cmp_probsT_ready")
    nsa_out_ready = signal("nsa_out_ready")
    merge_gate_ready = signal("merge_gate_ready", 3)
    merge_gate_used = signal("merge_gate_used", 3)
    merged_ready = signal("merged_ready")
    relu_ready = signal("relu_ready", 16)
    ff_ready = signal("ff_ready", 16)
    stored = sem("stored")
    const2_landed = sem("const2_landed")

    first_block = ExitStack()
    block = first_block.enter_context(nc.Block())
    ITEM = {name: i for i, (name, _) in enumerate(ITEMS1)}
    N1 = len(ITEMS1)
    w1_off, _ = offsets(ITEMS1)

    @block.sync
    def _(sp):
        sp.dma_start(con, K1).then_inc(const_landed, 16)
        sp.dma_start(x, xin.rearrange("(t p) n -> p t n", p=P)).then_inc(x_landed, 16)
        sp.dma_start(con2, K2).then_inc(const2_landed, 16)
        sp.dma_start(vec2, VV2).then_inc(const2_landed, 16)
        with sp.Fori(0, LAYERS) as l:
            for n, (name, count) in enumerate(ITEMS1):
                if not count:
                    continue
                sp.wait_ge(weights.used, l * N1 + n + 2)
                sp.dma_start(weights.view(n, count), W1[l, :, w1_off[name]:w1_off[name] + count]).then_inc(
                    weights.landed[n % SLOTS], 16)

    @block.tensor
    def _(pe):
        pe.sem_inc(weights.used, SLOTS)

        def stand():
            pe.sem_inc(pe_step, 1)

        item_now = {}

        def item(l, name):
            n = ITEM[name]
            loads = sum(1 for m in range(n % SLOTS, N1, SLOTS) if ITEMS1[m][1])
            pe.wait_ge(weights.landed[n % SLOTS], (l * loads + weights.loads_before(n)) * 16)
            stand()
            item_now["fresh"] = True
            return weights.view(n, ITEMS1[n][1])

        def mm(out, lhsT, rhs, start, stop, skip=False):
            ins = pe.matmul(out, lhsT, rhs, start=start, stop=stop, skip_group_check=skip)
            if item_now.get("fresh"):
                item_now["fresh"] = False
                assert not stop
                ins.then_inc(weights.used, 1)
            return ins

        def open_(ring, l, tag):
            b = ring.open(pe, l, tag)
            stand()
            return b

        def transposes(ring, l, tag, blocks, rows_=P):
            b = open_(ring, l, tag)
            at = 0
            for src in blocks:
                n = src.shape[0]
                last = pe.transpose(b[0:rows_, at:at + n], src, ident[0:n, 0:n])
                at += n
            last.then_inc(ring.full, 1)

        def normed_transposes(l, i):
            pe.wait_ge(*xn_ready.at(l, i))
            for pair in range(4):
                ring = (act_ring, dve_ring)[pair % 2]
                transposes(ring, l, f"hT{pair}", [xn[:, t, (2 * pair + c) * P:(2 * pair + c + 1) * P]
                                                  for c in range(2) for t in range(TT)])

        def token_major(ring, l, tag, srcT, w, kchunks, n0, n1):
            for t in range(TT):
                b = open_(ring, l, tag)
                for k in range(kchunks):
                    last = mm(b[:, 0:n1 - n0], srcT[:, k, t * P:(t + 1) * P], w[:, k, n0:n1], k == 0, k == kchunks - 1)
                last.then_inc(ring.full, 1)

        def channel_major(ring, l, tag, srcT, w, kchunks, chunks):
            for c in range(0, chunks, 2):
                b = open_(ring, l, tag)
                for j in range(2):
                    for k in range(kchunks):
                        last = mm(b[:, j * T:(j + 1) * T], w[:, k, (c + j) * P:(c + j + 1) * P], srcT[:, k, :],
                                  k == 0, k == kchunks - 1)
                last.then_inc(ring.full, 1)

        def attend(l, r, q, k, v, d):
            for h in range(8):
                b = open_(dve_ring, l, f"S{r}")
                mm(b[:, 0:P], q(h)[0:d, 0:P], k(h)[0:d, 0:P], True, True)
                mm(b[:, P:3 * P], q(h)[0:d, P:T], k(h)[0:d, :], True, True).then_inc(dve_ring.full, 1)
            for half in range(2):
                pe.wait_ge(*probs_ready.at(l, 2 * r + half))
                for part in range(3):
                    transposes(act_ring, l, f"PT{r}", [
                        S[:, half * 4 + (part * 4 + j) // 3, ((part * 4 + j) % 3) * P:((part * 4 + j) % 3 + 1) * P]
                        for j in range(4)])
            ring = act_ring if r == 0 else dve_ring
            for half in range(2):
                pe.wait_ge(*probsT_ready.at(l, 2 * r + half))
                b = open_(ring, l, f"PV{r}")
                for pair in range(2):
                    for e in range(2):
                        h = half * 4 + pair * 2 + e
                        o = b[64 * e:64 * e + 64, pair * T:(pair + 1) * T]
                        mm(o, v(h, 0), PT[:, h, 0:T], True, False, skip=True)
                        last = mm(o[:, P:T], v(h, 1), PT[:, h, T:T + P], False, True, skip=True)
                last.then_inc(ring.full, 1)

        pe.wait_ge(const_landed, 16)
        with pe.Fori(0, LAYERS) as l:
            normed_transposes(l, 0)
            pe.wait_ge(*hT_by_act.at(l, 0))
            pe.wait_ge(*hT_by_dve.at(l, 0))
            channel_major(act_ring, l, "u_gate", hT, km_view(item(l, "u_gate"), 512), 8, 4)
            channel_major(dve_ring, l, "u_a", hT, km_view(item(l, "u_a"), 512), 8, 4)
            token_major(act_ring, l, "cq", hT, km_view(item(l, "cq"), 384), 8, 0, 384)
            w = item(l, "ckv_uq")
            token_major(act_ring, l, "ckv", hT, km_view(w[:, 0:2304], 288), 8, 0, 288)
            pe.wait_ge(*latent_ready.at(l))
            blocks = [cq[:, t, c * P:(c + 1) * P] for c in range(3) for t in range(TT)]
            blocks += [ckvr[:, t, c * P:(c + 1) * P] for c in range(2) for t in range(TT)]
            for i in range(0, 10, 4):
                transposes(act_ring, l, "latentT", blocks[i:i + 4])
            pe.wait_ge(*latentT_ready.at(l))
            wq = km_view(w[:, 2304:4608], 768)
            for n0 in (0, 384):
                token_major(act_ring, l, "qm", cqT, wq, 3, n0, n0 + 384)
            w = item(l, "ukv_kvn2")
            for n0 in (0, 512):
                token_major(dve_ring, l, "kvm", ckvT, km_view(w[:, 0:2048], 1024), 2, n0, n0 + 512)
            token_major(act_ring, l, "kvn2", hT, km_view(w[:, 2048:4288], 280), 8, 0, 280)
            token_major(act_ring, l, "qn", hT, km_view(item(l, "qn"), 512), 8, 0, 512)
            token_major(act_ring, l, "kvn1", hT, km_view(item(l, "kvn1"), 512), 8, 0, 512)

            pe.wait_ge(*conv_ready.at(l))
            for t in range(TT):
                transposes(dve_ring, l, "conv", [cacc[:, c, t * P:(t + 1) * P] for c in range(4)])
            pe.wait_ge(*conv_normed.at(l))
            yn = cacc.rearrange("p c t -> p (c t)").rearrange("p (t n) -> p t n", t=TT)
            for c in range(0, 4, 2):
                transposes(act_ring, l, "convT", [yn[:, t, (c + j) * P:(c + j + 1) * P] for j in range(2) for t in range(TT)])

            pe.wait_ge(*heads_ready.at(l, 0))
            for h in range(0, 8, 2):
                transposes(act_ring, l, "qmT", [qm[:, t, h + j, :] for j in range(2) for t in range(TT)], MQK)
            pe.wait_ge(*heads_ready.at(l, 1))
            for h in range(0, 8, 2):
                transposes(act_ring, l, "kmT", [kf[:, t, h + j, :] for j in range(2) for t in range(TT)], MQK)
            pe.wait_ge(*qkT_ready.at(l, 0))
            pe.wait_ge(*vm_ready.at(l))
            attend(l, 0, lambda h: qT[:, h, :], lambda h: kT[:, h, :], lambda h, t: vm[:, t, h, :], MQK)

            pe.wait_ge(*kvn_copied.at(l))
            transposes(act_ring, l, "kcT", [kvn[:, t, g * P:(g + 1) * P] for g in range(NG) for t in range(TT)])
            w = km_view(item(l, "cmp"), P)
            pe.wait_ge(*blocks_ready.at(l))
            for s in range(2):
                b = open_(act_ring, l, "hid")
                for j in range(32):
                    last = mm(b[:, 0:30], w[64 * s:64 * s + 64, j, :],
                              blk[64 * s:64 * s + 64, j, :, :].rearrange("p g c -> p (g c)"), j == 0, j == 31)
                last.then_inc(act_ring.full, 1)
            pe.wait_ge(*hidden_ready.at(l))
            b = open_(dve_ring, l, "kvcmp")
            mm(b[0:30, 0:64], hid[:, 120:150], V["k2"], True, True)
            for g in range(NG):
                for j in range(4):
                    last = mm(b[32 * j:32 * j + NCMP, 64 + 64 * g:128 + 64 * g],
                              hid[:, 150 + NCMP * g:150 + NCMP * (g + 1)], V["v2"], True, True)
            last.then_inc(dve_ring.full, 1)
            pe.wait_ge(*heads_ready.at(l, 2))
            for s in range(2):
                transposes(act_ring, l, "nkT", [nk[:, s, t, g, :] for g in range(NG) for t in range(TT)], 64)
            pe.wait_ge(*heads_ready.at(l, 3))
            for h in range(0, 8, 2):
                transposes(act_ring, l, "qnT", [qn[:, t, h + j, :] for j in range(2) for t in range(TT)], 64)
            pe.wait_ge(*heads_ready.at(l, 4))
            transposes(act_ring, l, "kcmpT", [kc[0:30, :]], 64)
            pe.wait_ge(*kcmpT_ready.at(l))
            b = open_(dve_ring, l, "Scmp")
            for t in range(TT):
                for h in range(8):
                    g = h // 4
                    last = mm(b[:, t * T + h * 32:t * T + h * 32 + NCMP], qnT[0:64, h, t * P:(t + 1) * P],
                              kcmpT[0:64, g * NCMP:(g + 1) * NCMP], True, True)
            last.then_inc(dve_ring.full, 1)
            pe.wait_ge(*cmp_probs_ready.at(l))
            transposes(act_ring, l, "PTcmp", [pcmp[:, t, 4 * g:4 * g + 4, :].rearrange("p h n -> p (h n)")
                                              for g in range(NG) for t in range(TT)])
            pe.wait_ge(*cmp_probsT_ready.at(l))
            pe.wait_ge(*vcmp_ready.at(l))
            for g in range(NG):
                b = open_(dve_ring, l, "PVcmp")
                for j in range(2):
                    last = mm(b[:, j * T:(j + 1) * T], vbd[:, 2 * g + j, :], pcT[:, g, :], True, True)
                last.then_inc(dve_ring.full, 1)
            pe.wait_ge(*qkT_ready.at(l, 1))
            for r in (1, 2):
                c0 = 384 + 256 * (r - 1)
                attend(l, r, lambda h: qnT[:, h, :], lambda h: nkT[:, r - 1, h // 4, :],
                       lambda h, t: kvn[:, t, c0 + 64 * (h // 4):c0 + 64 * (h // 4) + 64], 64)

            for m, (name, ready, src) in enumerate((("A", mla_out_ready, oTm), ("B", conv_act_ready, cvT),
                                                    ("C", nsa_out_ready, oTn))):
                for half in range(2):
                    channel_major(act_ring, l, "gate", hT, km_view(item(l, f"{name}g{half}"), 512), 8, 4)
                pe.wait_ge(*ready.at(l))
                channel_major(dve_ring, l, "mix", src, km_view(item(l, f"{name}o"), D), 4, 8)
            pe.wait_ge(*merged_ready.at(l))
            for half in range(2):
                token_major(dve_ring, l, "out", mg, km_view(item(l, f"out{half}"), 512), 8, 0, 512)

            normed_transposes(l, 1)
            pe.wait_ge(*hT_by_act.at(l, 1))
            pe.wait_ge(*hT_by_dve.at(l, 1))
            for i in range(8):
                channel_major(act_ring, l, "ff1", hT, km_view(item(l, f"ff1_{i}"), 512), 8, 4)
            banks = []
            for i in range(8):
                w = km_view(item(l, f"ff2_{i}"), D)
                pe.wait_ge(*ff_ready.at(l, 2 * i + 1))
                for k in range(4):
                    for t in range(TT):
                        for half in range(2):
                            if i == 0 and k == 0:
                                banks.append(open_(dve_ring, l, "ff2"))
                            last = mm(banks[2 * t + half], fT[:, 4 * i + k, t * P:(t + 1) * P],
                                      w[:, k, half * 512:(half + 1) * 512], i + k == 0, i == 7 and k == 3)
                            if i == 7 and k == 3:
                                last.then_inc(dve_ring.full, 1)
            pe.drain().then_inc(weights.used, 1)
            while len(act_ring.filled["layers"]) % 4:
                open_(act_ring, l, "pad")
                pe.drain().then_inc(act_ring.full, 1)
        assert len(act_ring.filled["layers"]) == 92 and len(dve_ring.filled["layers"]) == 64

    @block.scalar
    def _(act):
        act.sem_inc(act_ring.free, 4)
        A = act.activation

        def normed_evac(l, i, gain):
            for pair in range(0, 4, 2):
                b = act_ring.take(act, l, f"hT{pair}")
                for c in range(2):
                    last = A(hT[:, 2 * pair + c, :], b[:, c * T:(c + 1) * T], ACT.Copy, scale=gain[:, 2 * pair + c:2 * pair + c + 1])
                last.then_inc(act_ring.free, 1)
                act.drain()
            act.sem_inc(hT_by_act.sem, 1)

        def roots(l, i):
            act.wait_ge(*sumsq_ready.at(l, i))
            A(nsd, nss, ACT.Sqrt, bias=C["eps"], scale=1.0 / D).then_inc(root_ready.sem, 1)

        def head_roots(l, i, rows_, n, d):
            act.wait_ge(*head_sumsq_ready.at(l, i))
            A(sd[0:rows_, 0:n], ss[0:rows_, 0:n], ACT.Sqrt, bias=C["eps"][0:rows_, :], scale=1.0 / d).then_inc(head_root_ready.sem, 1)

        def copy_bank(l, tag, dst, src=None, func=ACT.Copy):
            b = act_ring.take(act, l, tag)
            return A(dst, src(b) if src else b, func).then_inc(act_ring.free, 1)

        def attend(l, r, scale):
            for half in range(2):
                act.wait_ge(*score_max_ready.at(l, 2 * r + half))
                for h in range(4 * half, 4 * half + 4):
                    A(S[:, h, 0:P], S[:, h, 0:P], ACT.Exp, bias=neg[:, h, 0:1], accum_out=se[:, h, 0:1])
                    last = A(S[:, h, P:3 * P], S[:, h, P:3 * P], ACT.Exp, bias=neg[:, h, 1:2], accum_out=se[:, h, 1:2])
                last.then_inc(exp_ready.sem, 1)
            for half in range(2):
                for part in range(3):
                    f = PT[:, 4 * half:4 * half + 4, :].rearrange("p h n -> p (h n)")
                    copy_bank(l, f"PT{r}", f[:, part * 512:(part + 1) * 512])
                act.drain().then_inc(probsT_ready.sem, 1)
            if r == 0:
                for half in range(2):
                    copy_bank(l, "PV0", oTm[:, 2 * half:2 * half + 2, :], lambda b: b.rearrange("p (c t) -> p c t", c=2))
                act.drain().then_inc(mla_out_ready.sem, 1)

        with act.Fori(0, LAYERS) as l:
            act.wait_ge(const_landed, 16)
            roots(l, 0)
            act.wait_ge(vec_landed, l * 16 + 16)
            normed_evac(l, 0, V["g_mix"])
            for c in range(0, 4, 2):
                b = act_ring.take(act, l, "u_gate")
                for j in range(2):
                    last = A(sg[:, c + j, :], b[:, j * T:(j + 1) * T], ACT.Sigmoid, bias=V["b_glu"][:, 4 + c + j:5 + c + j])
                last.then_inc(act_ring.free, 1)
            act.drain().then_inc(glu_gate_ready.sem, 1)
            for t in range(TT):
                b = act_ring.take(act, l, "cq")
                A(cq[:, t, :], b[:, 0:384], ACT.Copy)
                A(junk[:, 0:384], b[:, 0:384], ACT.Square, accum_out=css[:, t:t + 1]).then_inc(act_ring.free, 1)
                act.drain()
            for t in range(TT):
                b = act_ring.take(act, l, "ckv")
                A(ckvr[:, t, :], b[:, 0:288], ACT.Copy)
                A(junk[:, 0:256], b[:, 0:256], ACT.Square, accum_out=css[:, 2 + t:3 + t]).then_inc(act_ring.free, 1)
                act.drain()
            A(csd[:, 0:2], css[:, 0:2], ACT.Sqrt, bias=C["eps"], scale=1.0 / 384)
            A(csd[:, 2:4], css[:, 2:4], ACT.Sqrt, bias=C["eps"], scale=1.0 / 256).then_inc(latent_root_ready.sem, 1)
            for i in range(3):
                b = act_ring.take(act, l, "latentT")
                for j in range(2 if i < 2 else 1):
                    c = 2 * i + j
                    dst = cqT[:, c, :] if c < 3 else ckvT[:, c - 3, :]
                    gain = V["g_cq"][:, c:c + 1] if c < 3 else V["g_ckv"][:, c - 3:c - 2]
                    last = A(dst, b[:, j * T:(j + 1) * T], ACT.Copy, scale=gain)
                last.then_inc(act_ring.free, 1)
            act.drain().then_inc(latentT_ready.sem, 1)
            qf = qm.rearrange("p t h n -> p t (h n)")
            for half in range(2):
                for t in range(TT):
                    copy_bank(l, "qm", qf[:, t, half * 384:(half + 1) * 384], lambda b: b[:, 0:384])
            act.drain().then_inc(qm_copied.sem, 1)
            for t in range(TT):
                copy_bank(l, "kvn2", kvn[:, t, 512:792], lambda b: b[:, 0:280])
            for t in range(TT):
                copy_bank(l, "qn", qn[:, t, :, :].rearrange("p h n -> p (h n)"))
            act.drain().then_inc(qn_copied.sem, 1)
            for t in range(TT):
                copy_bank(l, "kvn1", kvn[:, t, 0:512])
            act.drain().then_inc(kvn_copied.sem, 1)
            A(gates.rearrange("p (t n) -> p t n", t=TT), kvn[:, :, 768:792], ACT.Sigmoid).then_inc(gates_ready.sem, 1)
            act.wait_ge(*ln_var_ready.at(l))
            A(lsd, aggr[:, :, 1], ACT.Sqrt, bias=C["eps"]).then_inc(ln_root_ready.sem, 1)
            for c in range(0, 4, 2):
                b = act_ring.take(act, l, "convT")
                for j in range(2):
                    k = c + j
                    A(cvT[:, k, :], b[:, j * T:(j + 1) * T], ACT.Identity, bias=V["b_ln"][:, k:k + 1], scale=V["g_ln"][:, k:k + 1])
                    last = A(sg[:, k, :], b[:, j * T:(j + 1) * T], ACT.Sigmoid, bias=V["b_ln"][:, k:k + 1], scale=V["g_ln"][:, k:k + 1])
                last.then_inc(act_ring.free, 1)
            act.drain().then_inc(conv_silu_parts.sem, 1)
            head_roots(l, 0, P, 16, MQK)
            head_roots(l, 1, P, 16, MQK)
            for dst, tag in ((qT, "qmT"), (kT, "kmT")):
                for h in range(0, 8, 2):
                    copy_bank(l, tag, dst[0:MQK, h:h + 2, :], lambda b: b[0:MQK, :].rearrange("p (h t) -> p h t", h=2))
            act.drain().then_inc(qkT_ready.sem, 1)
            attend(l, 0, 1.0)
            copy_bank(l, "kcT", kcT, lambda b: b.rearrange("p (g t) -> p g t", g=NG))
            act.drain().then_inc(blocks_copied.sem, 1)
            for s in range(2):
                b = act_ring.take(act, l, "hid")
                A(hid[:, 30 * s:30 * s + 30], b[:, 0:30], ACT.Copy)
                A(hid[:, 60 + 30 * s:90 + 30 * s], b[:, 0:30], ACT.Sigmoid).then_inc(act_ring.free, 1)
            act.drain().then_inc(hidden_parts_ready.sem, 1)
            head_roots(l, 2, P, 8, 64)
            head_roots(l, 3, P, 16, 64)
            for s in range(2):
                copy_bank(l, "nkT", nkT[0:64, s, :, :], lambda b: b[0:64, :].rearrange("p (g t) -> p g t", g=NG))
            for h in range(0, 8, 2):
                copy_bank(l, "qnT", qnT[0:64, h:h + 2, :], lambda b: b[0:64, :].rearrange("p (h t) -> p h t", h=2))
            act.drain().then_inc(qkT_ready.sem, 1)
            head_roots(l, 4, 30, 1, 64)
            copy_bank(l, "kcmpT", kcmpT[0:64, :], lambda b: b[0:64, 0:30])
            act.drain().then_inc(kcmpT_ready.sem, 1)
            act.wait_ge(*cmp_shifted_ready.at(l))
            A(pcmp[:, :, :, 0:NCMP].rearrange("p t h n -> p (t h) n"), scmp.rearrange("p t h n -> p (t h) n"),
              ACT.Exp, scale=ND ** -0.5).then_inc(cmp_exp_ready.sem, 1)
            copy_bank(l, "PTcmp", pcT, lambda b: b.rearrange("p (g t) -> p g t", g=NG))
            act.drain().then_inc(cmp_probsT_ready.sem, 1)
            attend(l, 1, 1.0)
            attend(l, 2, 1.0)
            for m in range(3):
                if m == 2:
                    act.wait_ge(*merge_gate_used.at(l, 0))
                for c in range(0, 8, 2):
                    copy_bank(l, "gate", gsig[:, m % 2, c:c + 2, :], lambda b: b.rearrange("p (c t) -> p c t", c=2), ACT.Sigmoid)
                act.drain().then_inc(merge_gate_ready.sem, 1)
            roots(l, 1)
            normed_evac(l, 1, V["g_ffn"])
            for i in range(16):
                b = act_ring.take(act, l, "ff1")
                A(fT[:, 2 * i:2 * i + 2, :], b.rearrange("p (c t) -> p c t", c=2), ACT.Relu).then_inc(act_ring.free, 1)
                act.drain().then_inc(relu_ready.sem, 1)
            while len(act_ring.emptied["layers"]) % 4:
                act_ring.take(act, l, "pad")
                act.sem_inc(act_step, 1)
                act.drain().then_inc(act_ring.free, 1)
        act_ring.check("layers")

    @block.vector
    def _(v):
        v.sem_inc(dve_ring.free, 4)
        v.memset(upad, 0.0)
        v.memset(vbd, 0.0)
        v.memset(pcmp, 0.0)
        v.drain()

        def model_norm(l, i):
            for t in range(TT):
                v.tensor_tensor_reduce(xn[:, t, :], x[:, t, :], x[:, t, :], 1.0, 0.0, ALU.mult, ALU.add, nss[:, t:t + 1])
            v.drain().then_inc(sumsq_ready.sem, 1)
            v.wait_ge(*root_ready.at(l, i))
            v.reciprocal(nrs, nsd)
            v.drain()
            for t in range(TT):
                v.tensor_scalar(xn[:, t, :], x[:, t, :], nrs[:, t:t + 1], None, ALU.mult)
            v.drain().then_inc(xn_ready.sem, 1)

        def normed_evac(l, i, gain):
            for pair in range(1, 4, 2):
                b = dve_ring.take(v, l, f"hT{pair}")
                for c in range(2):
                    k = 2 * pair + c
                    last = v.tensor_scalar(hT[:, k, :], b[:, c * T:(c + 1) * T], gain[:, k:k + 1], None, ALU.mult)
                last.then_inc(dve_ring.free, 1)
            v.drain().then_inc(hT_by_dve.sem, 1)

        def head_norm(l, i, y, gain):
            p, n, d = y.shape
            sq = junk[0:p, 0:n * d].rearrange("p (n d) -> p n d", n=n)
            v.tensor_tensor(sq, y, y, ALU.mult)
            v.drain()
            v.tensor_reduce(ss[0:p, 0:n], sq, AX.X, ALU.add).then_inc(head_sumsq_ready.sem, 1)
            v.wait_ge(*head_root_ready.at(l, i))
            v.reciprocal(rs[0:p, 0:n], sd[0:p, 0:n])
            v.drain()
            v.tensor_tensor(y, y, bc(rs[0:p, 0:n], 2, d), ALU.mult)
            v.drain()
            v.tensor_tensor(y, y, bc(gain[0:p, :], 1, n), ALU.mult)
            v.drain()

        def rope(y, cos, sin):
            p, t, n, _ = y.shape
            half = cos.shape[2]
            x1, x2 = y[:, :, :, 0:half], y[:, :, :, half:2 * half]
            k = t * n * half
            a, b, c, d = (junk[0:p, 1536 + i * k:1536 + (i + 1) * k].rearrange("p (t n h) -> p t n h", t=t, n=n) for i in range(4))
            cb, sn = bc(cos, 2, n), bc(sin, 2, n)
            v.tensor_tensor(a, x1, cb, ALU.mult)
            v.tensor_tensor(b, x2, sn, ALU.mult)
            v.tensor_tensor(c, x2, cb, ALU.mult)
            v.tensor_tensor(d, x1, sn, ALU.mult)
            v.drain()
            v.tensor_tensor(x1, a, b, ALU.subtract)
            return v.tensor_tensor(x2, c, d, ALU.add)

        def table(name, t):
            return C[name].rearrange("p (t n) -> p t n", t=t)

        def attend(l, r, scale):
            for half in range(2):
                for h in range(4 * half, 4 * half + 4):
                    b = dve_ring.take(v, l, f"S{r}")
                    v.sem_inc(dve_step, 1)
                    v.tensor_tensor_reduce(S[:, h, 0:P], b[:, 0:P], C["cmask"][:, P:T], scale, -3e38, ALU.add, ALU.max, mx[:, h, 0:1])
                    v.tensor_tensor_reduce(S[:, h, P:3 * P], b[:, P:3 * P], C["cmask"], scale, -3e38, ALU.add, ALU.max,
                                           mx[:, h, 1:2]).then_inc(dve_ring.free, 1)
                v.drain()
                v.tensor_scalar(neg[:, 4 * half:4 * half + 4, :], mx[:, 4 * half:4 * half + 4, :], -1.0, None,
                                ALU.mult).then_inc(score_max_ready.sem, 1)
            for half in range(2):
                hs = slice(4 * half, 4 * half + 4)
                v.wait_ge(*exp_ready.at(l, 2 * r + half))
                v.reciprocal(scl[:, hs, :], se[:, hs, :])
                v.drain()
                if r:
                    g = gates.rearrange("p (t h n) -> p h t n", t=TT, h=NH)[:, hs, :, r]
                    v.tensor_tensor(scl[:, hs, :], scl[:, hs, :], g, ALU.mult)
                    v.drain()
                v.tensor_tensor(S[:, hs, 0:P], S[:, hs, 0:P], bc(scl[:, hs, 0], 2, P), ALU.mult)
                v.tensor_tensor(S[:, hs, P:3 * P], S[:, hs, P:3 * P], bc(scl[:, hs, 1], 2, T), ALU.mult).then_inc(probs_ready.sem, 1)
            if r:
                for half in range(2):
                    b = dve_ring.take(v, l, f"PV{r}").rearrange("p (c t) -> p c t", c=2)
                    o = oTn[:, 2 * half:2 * half + 2, :]
                    v.tensor_tensor(o, b, o, ALU.add).then_inc(dve_ring.free, 1)
                v.drain()

        v.wait_ge(x_landed, 16)
        v.wait_ge(const_landed, 16)
        with v.Fori(0, LAYERS) as l:
            model_norm(l, 0)
            v.wait_ge(vec_landed, l * 16 + 16)
            normed_evac(l, 0, V["g_mix"])
            v.wait_ge(*glu_gate_ready.at(l))
            for c in range(0, 4, 2):
                b = dve_ring.take(v, l, "u_a")
                for j in range(2):
                    k = c + j
                    last = v.scalar_tensor_tensor(upad[:, k, CONV_W - 1:], b[:, j * T:(j + 1) * T], V["b_glu"][:, k:k + 1],
                                                  sg[:, k, :], ALU.add, ALU.mult)
                last.then_inc(dve_ring.free, 1)
            v.drain()
            v.wait_ge(*latent_root_ready.at(l))
            v.reciprocal(crs, csd)
            v.drain()
            for t in range(TT):
                v.tensor_scalar(cq[:, t, :], cq[:, t, :], crs[:, t:t + 1], None, ALU.mult)
                v.tensor_scalar(ckvr[:, t, 0:256], ckvr[:, t, 0:256], crs[:, 2 + t:3 + t], None, ALU.mult)
            v.tensor_copy(kf[:, :, :, 0:MROPE], bc(ckvr[:, :, 256:288], 2, MH))
            v.drain().then_inc(latent_ready.sem, 1)
            for half in range(2):
                for t in range(TT):
                    b = dve_ring.take(v, l, "kvm").rearrange("p (h s n) -> p h s n", h=4, s=2)
                    v.tensor_copy(kf[:, t, 4 * half:4 * half + 4, MROPE:MQK], b[:, :, 0, :])
                    v.tensor_copy(vm[:, t, 4 * half:4 * half + 4, :], b[:, :, 1, :]).then_inc(dve_ring.free, 1)
            v.drain().then_inc(vm_ready.sem, 1)
            for tap in range(CONV_W):
                for c in range(4):
                    w = V["w_dw"][:, c * CONV_W + tap:c * CONV_W + tap + 1]
                    src = upad[:, c, tap:tap + T]
                    if tap == 0:
                        v.tensor_scalar(cacc[:, c, :], src, w, V["b_dw"][:, c:c + 1], ALU.mult, ALU.add)
                    else:
                        v.scalar_tensor_tensor(cacc[:, c, :], src, w, cacc[:, c, :], ALU.mult, ALU.add)
                if tap < CONV_W - 1:
                    v.drain()
            v.drain().then_inc(conv_ready.sem, 1)
            yn = cacc.rearrange("p c t -> p (c t)").rearrange("p (t n) -> p t n", t=TT)
            b2 = [dve_ring.take(v, l, "conv") for _ in range(TT)]
            for t in range(TT):
                v.bn_stats(stats[:, t, :], b2[t])
            v.drain()
            for t in range(TT):
                v.bn_aggr(aggr[:, t, :], stats[:, t, :])
            v.drain().then_inc(ln_var_ready.sem, 1)
            v.wait_ge(*ln_root_ready.at(l))
            v.reciprocal(lrs, lsd)
            v.drain()
            for t in range(TT):
                v.tensor_scalar(yn[:, t, :], b2[t], aggr[:, t, 0:1], lrs[:, t:t + 1], ALU.subtract, ALU.mult).then_inc(dve_ring.free, 1)
            v.drain().then_inc(conv_normed.sem, 1)
            v.wait_ge(*conv_silu_parts.at(l))
            v.tensor_tensor(cvT, cvT, sg, ALU.mult).then_inc(conv_act_ready.sem, 1)
            v.wait_ge(*qm_copied.at(l))
            head_norm(l, 0, qm.rearrange("p t h n -> p (t h) n"), V["g_q_mla"])
            rope(qm, table("mcos", TT), table("msin", TT)).then_inc(heads_ready.sem, 1)
            v.drain()
            head_norm(l, 1, kf.rearrange("p t h n -> p (t h) n"), V["g_k_mla"])
            rope(kf, table("mcos", TT), table("msin", TT)).then_inc(heads_ready.sem, 1)
            v.drain()
            attend(l, 0, MQK ** -0.5)
            v.wait_ge(*blocks_copied.at(l))
            kb = kcT.rearrange("p g (n b) -> p b g n", b=16)
            for a in range(2):
                pe_b = bc(bc(V["pe"][:, 16 * a:16 * a + 16], 2, NG), 3, NCMP)
                v.tensor_tensor(blk[:, 16 * a:16 * a + 16, :, :], kb[:, :, :, a:a + NCMP], pe_b, ALU.add)
            v.drain().then_inc(blocks_ready.sem, 1)
            v.wait_ge(*hidden_parts_ready.at(l))
            v.tensor_tensor(hid[:, 120:180], hid[:, 0:60], hid[:, 60:120], ALU.mult).then_inc(hidden_ready.sem, 1)
            v.wait_ge(*kvn_copied.at(l))
            for s in range(2):
                v.tensor_copy(nk[:, s, :, :, :], kvn[:, :, 256 + 256 * s:384 + 256 * s].rearrange("p t (g n) -> p t g n", g=NG))
            b = dve_ring.take(v, l, "kvcmp")
            v.tensor_copy(kc[0:30, :], b[0:30, 0:64])
            for g in range(NG):
                for j in range(4):
                    last = v.tensor_copy(vbd[32 * j:32 * j + NCMP, 2 * g + j // 2, (j % 2) * 64:(j % 2) * 64 + 64],
                                         b[32 * j:32 * j + NCMP, 64 + 64 * g:128 + 64 * g])
            last.then_inc(dve_ring.free, 1)
            v.drain().then_inc(vcmp_ready.sem, 1)
            head_norm(l, 2, nk.rearrange("p s t g n -> p (s t g) n"), V["g_k_nsa"])
            for s in range(2):
                last = rope(nk[:, s, :, :, :], table("ncos", TT), table("nsin", TT))
                v.drain()
            v.sem_inc(heads_ready.sem, 1)
            v.wait_ge(*qn_copied.at(l))
            head_norm(l, 3, qn.rearrange("p t h n -> p (t h) n"), V["g_q_nsa"])
            rope(qn, table("ncos", TT), table("nsin", TT)).then_inc(heads_ready.sem, 1)
            v.drain()
            head_norm(l, 4, kc[0:30, :].unsqueeze(1), V["g_k_nsa"])
            rope(kc[0:30, :].unsqueeze(1).unsqueeze(1), C["ccos"][0:30, :].unsqueeze(1),
                 C["csin"][0:30, :].unsqueeze(1)).then_inc(heads_ready.sem, 1)
            b = dve_ring.take(v, l, "Scmp").rearrange("p (t h n) -> p t h n", t=TT, h=NH)[:, :, :, 0:NCMP]
            v.tensor_tensor(scmp, b, bc(C["cmpmask"].rearrange("p (t n) -> p t n", t=TT), 2, NH), ALU.add).then_inc(dve_ring.free, 1)
            v.drain()
            s3, p3 = scmp.rearrange("p t h n -> p (t h) n"), pcmp.rearrange("p t h n -> p (t h) n")[:, :, 0:NCMP]
            v.tensor_reduce(cmx, s3, AX.X, ALU.max)
            v.drain()
            v.tensor_scalar(cmx, cmx, NEG * 1e-5, None, ALU.max)
            v.drain()
            v.tensor_tensor(s3, s3, bc(cmx, 2, NCMP), ALU.subtract).then_inc(cmp_shifted_ready.sem, 1)
            v.wait_ge(*cmp_exp_ready.at(l))
            v.tensor_reduce(cse, p3, AX.X, ALU.add)
            v.drain()
            v.tensor_scalar(cse, cse, 1e-30, None, ALU.max)
            v.drain()
            v.reciprocal(cgs, cse)
            v.wait_ge(*gates_ready.at(l))
            v.tensor_copy(cmx, gates.rearrange("p (n k) -> p n k", k=3)[:, :, 0])
            v.drain()
            v.tensor_tensor(cgs, cgs, cmx, ALU.mult)
            v.drain()
            v.tensor_tensor(p3, p3, bc(cgs, 2, NCMP), ALU.mult).then_inc(cmp_probs_ready.sem, 1)
            for g in range(NG):
                b = dve_ring.take(v, l, "PVcmp")
                v.tensor_copy(oTn[:, 2 * g:2 * g + 2, :], b.rearrange("p (c t) -> p c t", c=2)).then_inc(dve_ring.free, 1)
            v.drain()
            attend(l, 1, ND ** -0.5)
            attend(l, 2, ND ** -0.5)
            v.sem_inc(nsa_out_ready.sem, 1)
            for m in range(3):
                v.wait_ge(*merge_gate_ready.at(l, m))
                for c in range(0, 8, 2):
                    b = dve_ring.take(v, l, "mix").rearrange("p (c t) -> p c t", c=2)
                    g, o = gsig[:, m % 2, c:c + 2, :], mg[:, c:c + 2, :]
                    if m == 0:
                        v.tensor_tensor(o, b, g, ALU.mult).then_inc(dve_ring.free, 1)
                    elif m == 1:
                        for j in range(2):
                            last = v.scalar_tensor_tensor(g[:, j, :], b[:, j, :], V["b_co"][:, c + j:c + j + 1], g[:, j, :], ALU.add, ALU.mult)
                        last.then_inc(dve_ring.free, 1)
                    else:
                        v.tensor_tensor(g, b, g, ALU.mult).then_inc(dve_ring.free, 1)
                v.drain()
                if m:
                    for c in range(0, 8, 2):
                        v.tensor_tensor(mg[:, c:c + 2, :], mg[:, c:c + 2, :], gsig[:, m % 2, c:c + 2, :], ALU.add)
                    v.drain()
                v.sem_inc(merge_gate_used.sem, 1)
            v.sem_inc(merged_ready.sem, 1)
            for half in range(2):
                for t in range(TT):
                    xs = x[:, t, half * 512:(half + 1) * 512]
                    v.tensor_tensor(xs, dve_ring.take(v, l, "out"), xs, ALU.add).then_inc(dve_ring.free, 1)
            v.drain()
            model_norm(l, 1)
            normed_evac(l, 1, V["g_ffn"])
            for i in range(16):
                v.wait_ge(*relu_ready.at(l, i))
                f = fT[:, 2 * i:2 * i + 2, :]
                v.tensor_tensor(f, f, f, ALU.mult).then_inc(ff_ready.sem, 1)
            for t in range(TT):
                for half in range(2):
                    xs = x[:, t, half * 512:(half + 1) * 512]
                    v.tensor_tensor(xs, dve_ring.take(v, l, "ff2"), xs, ALU.add).then_inc(dve_ring.free, 1)
            v.drain().then_inc(layer_done.sem, 1)
        dve_ring.check("layers")

    @block.gpsimd
    def _(pool):
        for l in range(LAYERS):
            if l:
                pool.wait_ge(*layer_done.at(l - 1))
            pool.dma_start(vec, V1[l]).then_inc(vec_landed, 16)

    first_block.close()

    top = [base]

    def sb2(n, at=None):
        if at is None:
            at = top[0]
            top[0] += n
        return mem[:, at:at + n]

    sb2(2560)
    hcT = sb2(2048).rearrange("p (c t) -> p c t", c=DC)
    rows2 = sb2(2048).rearrange("p (m n) -> p m n", m=2)
    oaxT = sb2(2048).rearrange("p (c t) -> p c t", c=DC)
    modT = sb2(64).rearrange("p (m c s) -> p m c s", m=4, c=DC)
    AB = sb2(48).rearrange("p (k c) -> p k c", k=6)
    sm2 = sb2(224)
    free2 = top[0]
    ctxs = sb2(2048).rearrange("p (t n) -> p t n", t=TT)
    q2 = sb2(2048).rearrange("p (t n) -> p t n", t=TT)
    k2 = sb2(4096).rearrange("p (t n) -> p t n", t=4)
    v2 = sb2(4096).rearrange("p (t n) -> p t n", t=4)
    qT2 = sb2(2048).rearrange("p (h t) -> p h t", h=8)
    kT2 = sb2(4096).rearrange("p (h t) -> p h t", h=8)
    o2 = sb2(2048).rearrange("p (t n) -> p t n", t=TT)
    PT2 = sb2(2048).rearrange("p (h n) -> p h n", h=4)
    S_junk = sb2(1024, top[0] - 1024)
    S2 = sb2(4096, free2).rearrange("p (h m n) -> p h m n", h=4, m=2)
    assert top[0] <= MEM_COLS, top[0]
    csb = sb2(1024, free2 + 4096).rearrange("p (k n) -> p k n", k=8)
    cs = sm2[:, 0:16].rearrange("p (k s) -> p k s", s=2)
    csig = sm2[:, 16:32].rearrange("p (k s) -> p k s", s=2)
    ss2, sd2, rs2 = sm2[:, 32:48], sm2[:, 48:64], sm2[:, 64:80]
    mx2, se2, sc2 = (sm2[:, 80 + 8 * i:88 + 8 * i].rearrange("p (h m) -> p h m", m=2) for i in range(3))
    lam2, nlam = sm2[:, 104:106], sm2[:, 106:107]
    css2, csd2, crs2 = sm2[:, 108:110], sm2[:, 110:112], sm2[:, 112:114]
    ys, yd, yr = sm2[:, 120:152], sm2[:, 152:184], sm2[:, 184:216]

    HALF = 512
    rtop = [free2]

    def rb(n):
        at = rtop[0]
        rtop[0] += n
        return mem[:, at:at + n]

    zs = rb(26 * HALF).rearrange("p (c t) -> p c t", c=26)
    kk = sb2(8 * HALF, base).rearrange("p (c t) -> p c t", c=8)
    yb = rb(4096).rearrange("p (d c s n) -> p d c s n", d=2, c=8, s=4)
    lora = rb(3072)
    Wc = rb(16)
    lor = rb(128).rearrange("p (d t) -> p d t", d=2)
    restart = rb(512)
    zraw = sb2(1024, base).rearrange("p (b t) -> p b t", b=2)
    slots_at = 2 * TT * D
    Z = [sb2(1024, slots_at + 1024 * i) for i in range(14)] + [rb(1024)]
    assert slots_at + 14 * 1024 <= base - nv2 - ncon2 - ncon and rtop[0] <= MEM_COLS, rtop[0]
    a0, a1, a2, a3, Pm, Qm, Km, Rm, Vt, VT_TOK, Kt, Qt, Arq, LT, St = Z
    SIG2 = sb2(2048, slots_at)
    Z_sq = sb2(4096, slots_at).rearrange("p (c t) -> p c t", c=8)
    Apk, Ark = a2, a3
    Dm, DTm = Qm, Km
    Loff, ARm, U0, nU = a0, a1, a0, a1
    YOUT = Vt

    def ch(ap):
        return ap.rearrange("p (c n) -> p c n", c=16)

    def ch2(ap):
        return ap.rearrange("p (d c n) -> p d c n", d=2, c=8)

    gsig2 = sb2(2048, free2).rearrange("p (c t) -> p c t", c=DC)
    mg2 = sb2(2048, free2 + 2048).rearrange("p (c t) -> p c t", c=DC)
    obx = sb2(2048, base).rearrange("p (c t) -> p c t", c=DC)
    rtmp = sb2(2048, base + 2048).rearrange("p (c t) -> p c t", c=DC)
    BON = yb[:, 1, :, :, :].rearrange("p c s n -> p c (s n)")
    ptop = [free2]

    def pb(n):
        at = ptop[0]
        ptop[0] += n
        return mem[:, at:at + n]

    h2 = sb2(2048, base + 2560 + 4096).rearrange("p (t n) -> p t n", t=TT)
    acc = sb2(2048, base + 2560).rearrange("p (t n) -> p t n", t=TT)
    qTp = pb(4096).rearrange("p (c t) -> p c t", c=16)
    sp_ = pb(4096).rearrange("p (t c n) -> p t c n", t=TT, c=16)
    keysT = pb(2048).rearrange("p (c n) -> p c n", c=16)
    sv = pb(512).rearrange("p (t c n) -> p t c n", t=TT, c=16)
    siu = pb(512)
    sif = pb(512).rearrange("p (t c n) -> p t c n", t=TT, c=16)
    cand = sb2(2048, slots_at + 9216).rearrange("p (h n) -> p h n", h=8)
    eqb = sb2(2048, slots_at + 11264)
    tops = pb(256).rearrange("p (t h n) -> p t h n", t=TT, h=8)
    posu, hiu, lou, eidx = (pb(256) for _ in range(4))
    hif, lof, i1f, i2f = (pb(128) for _ in range(4))
    gatep = pb(256).rearrange("p (t h n) -> p t h n", t=TT, h=8)
    actp, g1, g2 = (pb(256) for _ in range(3))
    idx8 = pb(16)
    dot8 = pb(16)
    wt8 = pb(16)
    gmx, gsm, grc = (pb(16) for _ in range(3))
    GB = 8
    gat = sb2(GB * D, slots_at).rearrange("p (b n) -> p b n", b=GB)
    assert ptop[0] <= MEM_COLS, ptop[0]
    siu_u = siu.bitcast(U32).rearrange("p (t c n) -> p t c n", t=TT, c=16)
    posu_u = posu.bitcast(U32).rearrange("p (t h n) -> p t h n", t=TT, h=8)
    hiu_u, lou_u, eidx_u, idx8_u = hiu.bitcast(U32), lou.bitcast(U32), eidx.bitcast(U32), idx8.bitcast(U32)

    w2_off, w2_total = offsets(ITEMS2)
    ITEM2 = {name: i for i, (name, _) in enumerate(ITEMS2)}
    N2 = len(ITEMS2)
    LAST_BEFORE_SCAN = ITEM2["rw6"]
    landed0 = [LAYERS * sum(1 for m in range(s, len(ITEMS1), SLOTS) if ITEMS1[m][1]) for s in range(SLOTS)]
    used0 = LAYERS * len(ITEMS1)
    DECAY = -float(np.exp(np.float32(-0.5)))

    rows_landed, ctx_landed, lora_landed, keys_landed = sem("rows_landed"), sem("ctx_landed"), sem("lora_landed"), sem("keys_landed")
    cond_sig_ready, cond_ready = signal("cond_sig_ready"), signal("cond_ready")
    mod_ready = signal("mod_ready")
    sumsq2_ready, root2_ready, xn2_ready = signal("sumsq2_ready"), signal("root2_ready"), signal("xn2_ready")
    hT2_by_act, hT2_by_dve = signal("hT2_by_act"), signal("hT2_by_dve")
    qk2_copied = signal("qk2_copied")
    head2_sumsq_ready, head2_root_ready = signal("head2_sumsq_ready"), signal("head2_root_ready")
    qk2_ready, qkT2_ready = signal("qk2_ready"), signal("qkT2_ready")
    v2_copied = signal("v2_copied")
    lam_parts_ready, lam_exp_ready = signal("lam_parts_ready"), signal("lam_exp_ready")
    diff_max_ready, diff_exp_ready, diff_probs_ready, diff_probsT_ready = (
        signal("diff_max_ready"), signal("diff_exp_ready"), signal("diff_probs_ready"), signal("diff_probsT_ready"))
    diff_out_copied, diff_out_ready, oaxT_ready = signal("diff_out_copied"), signal("diff_out_ready"), signal("oaxT_ready")
    shift_parts_ready, shift_parts_used = signal("shift_parts_ready"), signal("shift_parts_used")
    shifted_ready, lora_act_ready = signal("shifted_ready"), signal("lora_act_ready")
    kk_sq_ready, kk_root_ready, scan_ready = signal("kk_sq_ready"), signal("kk_root_ready"), signal("scan_ready")
    step_in_ready, lora_sums_ready, rates_ready = signal("step_in_ready"), signal("lora_sums_ready"), signal("rates_ready")
    cumsum_ready, decays_ready = signal("cumsum_ready"), signal("decays_ready")
    pqkr_ready, tokens_ready = signal("pqkr_ready"), signal("tokens_ready")
    intra_ready, inverse_ready = signal("intra_ready"), signal("inverse_ready", 6)
    level_mask_ready, level_left_ready = signal("level_mask_ready", 5), signal("level_left_ready", 5)
    u0_ready, u_ready, y_stored, state_ready = signal("u0_ready"), signal("u_ready"), signal("y_stored"), signal("state_ready")
    scan_done_act, scan_done_dve = sem("scan_done_act"), sem("scan_done_dve")
    y_var_ready, y_root_ready, y_ready = signal("y_var_ready"), signal("y_root_ready"), signal("y_ready")
    bonus_in_ready, gd_sig_ready, obx_ready = signal("bonus_in_ready"), signal("gd_sig_ready"), signal("obx_ready")
    gate2_ready, gate2_used, merged2_ready = signal("gate2_ready"), signal("gate2_used"), signal("merged2_ready")
    qTp_ready, h2_ready, scores_ready = signal("qTp_ready"), signal("h2_ready"), signal("scores_ready")
    gate_shift_ready, gate_exp_ready = signal("gate_shift_ready"), signal("gate_exp_ready")
    experts_ready = signal("experts_ready")
    idx_used = sem("idx_used")
    pool_copied = sem("pool_copied")
    row_landed = [sem(f"row_landed{i}") for i in range(GB)]
    row_used = [sem(f"row_used{i}") for i in range(GB)]
    gelu_in_ready, gelu_tanh_ready = signal("gelu_in_ready"), signal("gelu_tanh_ready")
    out_ready = signal("out_ready")

    act_ring.pe_section = act_ring.section = dve_ring.pe_section = dve_ring.section = "attention"
    second_block = ExitStack()
    block = second_block.enter_context(nc.Block())

    @block.sync
    def _(sp):
        sp.dma_start(rows2, R2.rearrange("p (m n) -> p m n", m=2)).then_inc(rows_landed, 16)
        sp.dma_start(ctxs, cin.rearrange("(t p) n -> p t n", p=P)).then_inc(ctx_landed, 16)
        for n, (name, count) in enumerate(ITEMS2):
            if n == LAST_BEFORE_SCAN + 1:
                sp.wait_ge(shift_parts_ready.sem, 1)
                sp.dma_start(lora, W2[:, w2_total:w2_total + 3072]).then_inc(lora_landed, 16)
                sp.wait_ge(scan_done_act, 1)
                sp.wait_ge(scan_done_dve, 1)
            sp.wait_ge(weights.used, used0 + n + 2)
            sp.dma_start(weights.view(n, count), W2[:, w2_off[name]:w2_off[name] + count]).then_inc(
                weights.landed[n % SLOTS], 16)
        sp.wait_ge(*obx_ready.at(0))
        sp.wait_ge(*merged2_ready.at(0))
        sp.dma_start(keysT, W2[:, w2_total + 3072:w2_total + 5120].rearrange("p (c n) -> p c n", c=16)).then_inc(keys_landed, 16)
        sp.wait_ge(*out_ready.at(0))
        sp.dma_start(out.rearrange("(t p) n -> p t n", p=P), x).then_inc(stored, 16)
        sp.wait_ge(stored, 16)

    @block.tensor
    def _(pe):
        item_now = {}

        def item(name):
            n = ITEM2[name]
            s = n % SLOTS
            pe.wait_ge(weights.landed[s], (landed0[s] + n // SLOTS + 1) * 16)
            item_now["fresh"] = True
            return weights.view(n, ITEMS2[n][1])

        def mm(out, lhsT, rhs, start, stop, skip=False):
            ins = pe.matmul(out, lhsT, rhs, start=start, stop=stop, skip_group_check=skip)
            if item_now.get("fresh"):
                item_now["fresh"] = False
                assert not stop
                ins.then_inc(weights.used, 1)
            return ins

        def transposes(ring, tag, blocks):
            b = ring.open(pe, 0, tag)
            for j, src in enumerate(blocks):
                last = pe.transpose(b[:, j * P:(j + 1) * P], src, ident)
            last.then_inc(ring.full, 1)

        def token_major(ring, tag, srcT, w, kchunks, t):
            b = ring.open(pe, 0, tag)
            for k in range(kchunks):
                last = mm(b, srcT[:, k, t * P:(t + 1) * P], w[:, k, :], k == 0, k == kchunks - 1)
            last.then_inc(ring.full, 1)

        def channel_major(ring, tag, srcT, w, kchunks, chunks):
            for c in range(0, chunks, 2):
                b = ring.open(pe, 0, tag)
                for j in range(2):
                    for k in range(kchunks):
                        last = mm(b[:, j * T:(j + 1) * T], w[:, k, (c + j) * P:(c + j + 1) * P], srcT[:, k, :],
                                  k == 0, k == kchunks - 1)
                last.then_inc(ring.full, 1)

        def normed_transposes(src):
            for pair in range(4):
                ring = (act_ring, dve_ring)[pair % 2]
                transposes(ring, f"hT{pair}", [src[:, t, (2 * pair + c) * P:(2 * pair + c + 1) * P]
                                               for c in range(2) for t in range(TT)])

        def pad(section, na, nd):
            for ring, n in ((act_ring, na), (dve_ring, nd)):
                while len(ring.filled[section]) < n:
                    ring.open(pe, 0, "pad")
                    pe.drain().then_inc(ring.full, 1)
                assert len(ring.filled[section]) == n, (section, len(ring.filled[section]), n)

        pe.wait_ge(*cond_ready.at(0))
        for i in range(12):
            w = km_view(item(f"mod{i}"), 512)
            b = dve_ring.open(pe, 0, "mod")
            if i // 2 in (2, 5):
                for k in range(8):
                    last = mm(b, csb[:, k, :], w[:, k, :], k == 0, k == 7)
            else:
                for j in range(4):
                    for k in range(8):
                        last = mm(b[:, 2 * j:2 * j + 2], w[:, k, j * P:(j + 1) * P], cs[:, k, :], k == 0, k == 7)
            last.then_inc(dve_ring.full, 1)
        pe.wait_ge(*xn2_ready.at(0, 0))
        normed_transposes(xn)
        pe.wait_ge(*xn2_ready.at(0, 1))
        normed_transposes(ctxs)
        pe.wait_ge(*hT2_by_act.at(0, 1))
        pe.wait_ge(*hT2_by_dve.at(0, 1))
        for i in range(2):
            w = km_view(item(f"q{i}"), 512)
            for t in range(TT):
                token_major(act_ring, "q2", hT, w, 8, t)
        for n in "kv":
            for i in range(2):
                w = km_view(item(f"{n}{i}"), 512)
                for t in range(4):
                    token_major(act_ring if n == "k" else dve_ring, n + "2", (hcT, hT)[t // 2], w, 8, t % 2)
        for t in range(TT):
            pe.wait_ge(*qk2_ready.at(0, t))
        for h in range(0, 8, 2):
            transposes(act_ring, "qT2", [q2[:, t, (h + j) * P:(h + j + 1) * P] for j in range(2) for t in range(TT)])
        for t in range(2, 6):
            pe.wait_ge(*qk2_ready.at(0, t))
        for h in range(8):
            transposes(act_ring, "kT2", [k2[:, t, h * P:(h + 1) * P] for t in range(4)])
        pe.wait_ge(*qkT2_ready.at(0))
        pe.wait_ge(*v2_copied.at(0))
        for t in range(TT):
            for half in range(2):
                grp = 2 * t + half
                for hh in range(4):
                    h = 4 * half + hh
                    for m in range(2):
                        b = act_ring.open(pe, 0, "S2")
                        mm(b, qT2[64 * m:64 * m + 64, h, t * P:(t + 1) * P], kT2[64 * m:64 * m + 64, h, :], True, True).then_inc(act_ring.full, 1)
                pe.wait_ge(*diff_probs_ready.at(0, grp))
                for hh in range(4):
                    transposes(act_ring, "PT2", [S2[:, hh, 0, j * P:(j + 1) * P] for j in range(4)])
                pe.wait_ge(*diff_probsT_ready.at(0, grp))
                b = act_ring.open(pe, 0, "PV2")
                for hh in range(4):
                    h = 4 * half + hh
                    for j in range(4):
                        last = mm(b[:, hh * P:(hh + 1) * P], PT2[:, hh, j * P:(j + 1) * P], v2[:, j, h * P:(h + 1) * P], j == 0, j == 3)
                last.then_inc(act_ring.full, 1)
        pe.wait_ge(*diff_out_ready.at(0))
        for h in range(0, 8, 2):
            transposes(act_ring, "oaxT", [o2[:, t, (h + j) * P:(h + j + 1) * P] for j in range(2) for t in range(TT)])
        for i in range(7):
            w = km_view(item(f"rw{i}"), 512 if i < 6 else 256)
            for c in range(4 if i < 6 else 2):
                b = act_ring.open(pe, 0, "rw")
                for s, src in enumerate((hcT, hT)):
                    for k in range(8):
                        last = mm(b[:, s * T:(s + 1) * T], w[:, k, c * P:(c + 1) * P], src[:, k, :], k == 0, k == 7)
                last.then_inc(act_ring.full, 1)
        pe.wait_ge(*kk_sq_ready.at(0))
        sq = Z_sq
        for c in range(8):
            b = act_ring.open(pe, 0, "kk")
            mm(b, C2["onesbd"], sq[:, c, :], True, True).then_inc(act_ring.full, 1)
        pad("attention", NA_ATT, ND_ATT)

        act_ring.pe_section = dve_ring.pe_section = "scan"
        pe.wait_ge(lora_landed, 16)
        pe.wait_ge(*scan_ready.at(0))
        id2 = C2["id2"]

        def stand():
            pe.sem_inc(pe_step, 1)

        def product(ring, l, tag, *terms):
            banks = []
            for d in range(2):
                banks.append(ring.open(pe, l, tag))
                stand()
            for head in range(2):
                if head:
                    pe.drain()
                s = slice(64 * head, 64 * head + 64)
                for d in range(2):
                    for c in range(8):
                        for i, (lhsT, rhs) in enumerate(terms):
                            r = id2[s, :] if rhs is None else ch(rhs)[s, 8 * d + c, :]
                            last = mm(banks[d][s, c * 64:(c + 1) * 64], ch(lhsT)[s, 8 * d + c, :], r,
                                      i == 0, i == len(terms) - 1, skip=True)
                    if head:
                        last.then_inc(ring.full, 1)

        with pe.Fori(0, 8) as l:
            pe.wait_ge(*step_in_ready.at(l))
            stand()
            for part in range(2):
                s = slice(64 * part, 64 * part + 64)
                for d in range(2):
                    b = dve_ring.open(pe, l, "lora")
                    stand()
                    for c in range(8):
                        last = mm(b[:, c * 64:(c + 1) * 64], lora[s, d * D + c * P:d * D + (c + 1) * P], lor[s, d, :], True, True)
                    last.then_inc(dve_ring.full, 1)
            pe.wait_ge(*lora_sums_ready.at(l))
            stand()
            product(act_ring, l, "Vt", (Vt, None))
            pe.wait_ge(*pqkr_ready.at(l))
            stand()
            product(act_ring, l, "Kt", (Km, None))
            product(act_ring, l, "Qt", (Qm, None))
            product(dve_ring, l, "Apk", (Km, Pm))
            product(dve_ring, l, "Ark", (Km, Rm))
            product(dve_ring, l, "Arq", (Qm, Rm))
            product(dve_ring, l, "LT", (Qm, Pm))
            product(dve_ring, l, "L", (Pm, Qm))
            for j in range(5):
                pe.wait_ge(*inverse_ready.at(l, j))
                stand()
                product(act_ring, l, "AL", (Loff, Dm))
                pe.wait_ge(*level_left_ready.at(l, j))
                stand()
                product(dve_ring, l, "ET", (ARm, DTm))
                if j < 4:
                    product(dve_ring, l, "E", (DTm, ARm))
            pe.wait_ge(*tokens_ready.at(l))
            stand()
            product(act_ring, l, "U0", (Pm, St), (Apk, VT_TOK))
            pe.wait_ge(*u0_ready.at(l))
            pe.wait_ge(*inverse_ready.at(l, 5))
            stand()
            product(act_ring, l, "U", (DTm, U0))
            pe.wait_ge(*u_ready.at(l))
            stand()
            product(act_ring, l, "Y", (Rm, St), (Ark, VT_TOK), (Arq, nU))
            product(dve_ring, l, "St", (Kt, VT_TOK), (Qt, nU))
            for ring, n in ((act_ring, NA_SCAN), (dve_ring, ND_SCAN)):
                while len(ring.filled["scan"]) < n:
                    ring.open(pe, l, "pad")
                    stand()
                    pe.drain().then_inc(ring.full, 1)
                assert len(ring.filled["scan"]) == n, (len(ring.filled["scan"]), n)

        act_ring.pe_section = dve_ring.pe_section = "post"
        pe.wait_ge(*y_ready.at(0))
        for c in range(0, 8, 2):
            b = dve_ring.open(pe, 0, "yT")
            for head in range(2):
                if head:
                    pe.drain()
                s = slice(64 * head, 64 * head + 64)
                for j in range(2):
                    for ck in range(4):
                        last = mm(b[s, j * T + ck * 64:j * T + ck * 64 + 64], yb[s, 0, c + j, ck, :], id2[s, :], True, True, skip=True)
            last.then_inc(dve_ring.full, 1)
        pe.wait_ge(*bonus_in_ready.at(0))
        for c in range(0, 8, 2):
            b = dve_ring.open(pe, 0, "bonus")
            mm(b, C2["onesbd"], rtmp[:, c:c + 2, :].rearrange("p c t -> p (c t)"), True, True).then_inc(dve_ring.full, 1)
        pe.wait_ge(*gd_sig_ready.at(0))
        for c in range(0, 8, 2):
            b = dve_ring.open(pe, 0, "g")
            for j in range(2):
                last = mm(b[:, j * T:(j + 1) * T], lora[:, 2048 + (c + j) * P:2048 + (c + j + 1) * P], zs[:, 25, T:2 * T], True, True)
            last.then_inc(dve_ring.full, 1)
        pe.wait_ge(*oaxT_ready.at(0))
        for m, (n, src) in enumerate((("A", oaxT), ("B", obx))):
            for half in range(2):
                channel_major(act_ring, "gate2", hT, km_view(item(f"g{half}{n}"), 512), 8, 4)
            if m:
                pe.wait_ge(*obx_ready.at(0))
            for half in range(2):
                channel_major(dve_ring, "mix2", src, km_view(item(f"o{n}{half}"), 512), 8, 4)
        pe.wait_ge(*merged2_ready.at(0))
        for half in range(2):
            w = km_view(item(f"out{half}"), 512)
            for t in range(TT):
                token_major(dve_ring, "out2", mg2, w, 8, t)
        pe.wait_ge(*xn2_ready.at(0, 2))
        normed_transposes(xn)
        pe.wait_ge(*hT2_by_act.at(0, 2))
        pe.wait_ge(*hT2_by_dve.at(0, 2))
        for t in range(TT):
            for half in range(2):
                transposes(act_ring, "h2", [hT[:, 4 * half + j, t * P:(t + 1) * P] for j in range(4)])
        for i in range(4):
            channel_major(act_ring, "qp", hT, km_view(item(f"wq{i}"), 512), 8, 4)
        pe.wait_ge(keys_landed, 16)
        pe.wait_ge(*qTp_ready.at(0))
        for t in range(TT):
            for g in range(4):
                b = act_ring.open(pe, 0, "sp")
                for j in range(4):
                    last = mm(b[:, j * P:(j + 1) * P], qTp[:, 4 * g + j, t * P:(t + 1) * P], keysT[:, 4 * g + j, :], True, True)
                last.then_inc(act_ring.full, 1)

    @block.scalar
    def _(act):
        A = act.activation

        def take(tag, l=0):
            return act_ring.take(act, l, tag)

        def done(ins):
            return ins.then_inc(act_ring.free, 1)

        def roots(i):
            act.wait_ge(*sumsq2_ready.at(0, i))
            A(csd2, css2, ACT.Sqrt, bias=C["eps"], scale=1.0 / D).then_inc(root2_ready.sem, 1)

        def normed_evac(i, dst):
            for pair in range(0, 4, 2):
                b = take(f"hT{pair}")
                for c in range(2):
                    k = 2 * pair + c
                    last = A(dst[:, k, :], b[:, c * T:(c + 1) * T], ACT.Identity, bias=AB[:, 2 * i + 1, k:k + 1], scale=AB[:, 2 * i, k:k + 1])
                done(last)
            act.drain().then_inc(hT2_by_act.sem, 1)

        def heads(n):
            for i in range(n):
                act.wait_ge(*head2_sumsq_ready.at(0, head_count[0]))
                head_count[0] += 1
                A(sd2, ss2, ACT.Sqrt, bias=C["eps"], scale=1.0 / 64 if head_count[0] <= 6 else 1.0 / P).then_inc(head2_root_ready.sem, 1)

        def pad(section, l=0):
            tags = act_ring.filled[section]
            while len(act_ring.emptied[section]) < len(tags):
                act_ring.take(act, l, "pad")
                act.sem_inc(act_step, 1)
                act.drain().then_inc(act_ring.free, 1)
            act_ring.check(section)

        head_count = [0]
        act.wait_ge(const2_landed, 32)
        A(csig, V2["c"].rearrange("p (k s) -> p k s", s=2), ACT.Sigmoid).then_inc(cond_sig_ready.sem, 1)
        roots(0)
        roots(1)
        act.wait_ge(*mod_ready.at(0))
        normed_evac(0, hT)
        normed_evac(1, hcT)
        for i in range(2):
            for t in range(TT):
                done(A(q2[:, t, i * 512:(i + 1) * 512], take("q2"), ACT.Copy))
        for i in range(2):
            for t in range(4):
                done(A(k2[:, t, i * 512:(i + 1) * 512], take("k2"), ACT.Copy))
        act.drain().then_inc(qk2_copied.sem, 1)
        act.wait_ge(*lam_parts_ready.at(0))
        A(lam2, lam2, ACT.Exp).then_inc(lam_exp_ready.sem, 1)
        heads(6)
        for h in range(0, 8, 2):
            done(A(qT2[:, h:h + 2, :], take("qT2").rearrange("p (h t) -> p h t", h=2), ACT.Copy))
        for h in range(8):
            done(A(kT2[:, h, :], take("kT2"), ACT.Copy))
        act.drain().then_inc(qkT2_ready.sem, 1)
        for grp in range(4):
            t, half = grp // 2, grp % 2
            for i in range(8):
                act.wait_ge(*diff_max_ready.at(0, 8 * grp + i))
                done(A(S2[:, i // 2, i % 2, :], take("S2"), ACT.Exp, bias=mx2[:, i // 2, i % 2:i % 2 + 1], scale=0.125,
                       accum_out=se2[:, i // 2, i % 2:i % 2 + 1]))
            act.drain().then_inc(diff_exp_ready.sem, 1)
            for hh in range(4):
                done(A(PT2[:, hh, :], take("PT2"), ACT.Copy))
            act.drain().then_inc(diff_probsT_ready.sem, 1)
            done(A(o2[:, t, half * 512:(half + 1) * 512], take("PV2"), ACT.Copy))
        act.drain().then_inc(diff_out_copied.sem, 1)
        heads(1)
        for h in range(0, 8, 2):
            done(A(oaxT[:, h:h + 2, :], take("oaxT").rearrange("p (h t) -> p h t", h=2), ACT.Copy))
        act.drain().then_inc(oaxT_ready.sem, 1)
        for c in range(26):
            b = take("rw")
            if c >= 2:
                act.wait_ge(*shift_parts_used.at(0, c - 2))
            A(zs[:, c, :], b, ACT.Copy, scale=V2["shift"][:, 26 + c:27 + c])
            done(A(zraw[:, c % 2, :], b, ACT.Copy))
            act.drain().then_inc(shift_parts_ready.sem, 1)
        act.wait_ge(*shifted_ready.at(0))
        A(zs[0:64, 24, :], zs[0:64, 24, :], ACT.Tanh).then_inc(lora_act_ready.sem, 1)
        for c in range(8):
            done(A(Z_sq[:, c, :], take("kk"), ACT.Sqrt, bias=C["l2eps"]))
        act.drain().then_inc(kk_root_ready.sem, 1)
        pad("attention")

        act_ring.section = "scan"

        def evac(l, tag, dst, func=ACT.Copy, scale=1.0):
            for d in range(2):
                done(A(dst[:, d * 512:(d + 1) * 512], take(tag, l), func, scale=scale))

        act.wait_ge(*scan_ready.at(0))
        with act.Fori(0, 8) as l:
            act.wait_ge(*lora_sums_ready.at(l))
            A(SIG2, SIG2, ACT.Sigmoid).then_inc(rates_ready.sem, 1)
            evac(l, "Vt", VT_TOK)
            act.drain()
            act.wait_ge(*cumsum_ready.at(l))
            A(a0, a2, ACT.Exp, scale=DECAY)
            A(a3, a3, ACT.Exp, scale=DECAY)
            act.drain()
            A(a2, a2, ACT.Exp, scale=-DECAY).then_inc(decays_ready.sem, 1)
            evac(l, "Kt", Kt)
            evac(l, "Qt", Qt)
            act.drain().then_inc(tokens_ready.sem, 1)
            for j in range(5):
                evac(l, "AL", ARm)
                act.drain().then_inc(level_left_ready.sem, 1)
            evac(l, "U0", U0)
            act.drain().then_inc(u0_ready.sem, 1)
            evac(l, "U", nU, scale=-1.0)
            act.drain().then_inc(u_ready.sem, 1)
            b0 = take("Y", l)
            done(A(YOUT[:, 0:512], b0, ACT.Copy))
            b1 = take("Y", l)
            done(A(YOUT[:, 512:1024], b1, ACT.Copy))
            act.drain().then_inc(y_stored.sem, 1)
            pad("scan", l)
        act.sem_inc(scan_done_act, 1)

        act_ring.section = "post"
        act.wait_ge(*y_var_ready.at(0))
        A(yd, ys, ACT.Sqrt, bias=C["lneps"], scale=1.0 / 64).then_inc(y_root_ready.sem, 1)
        A(zs[:, 25, T:2 * T], zs[:, 25, T:2 * T], ACT.Sigmoid).then_inc(gd_sig_ready.sem, 1)
        for m in range(2):
            if m:
                act.wait_ge(*gate2_used.at(0))
            else:
                act.wait_ge(*obx_ready.at(0))
            for c in range(0, 8, 2):
                done(A(gsig2[:, c:c + 2, :], take("gate2").rearrange("p (c t) -> p c t", c=2), ACT.Sigmoid))
            act.drain().then_inc(gate2_ready.sem, 1)
        roots(2)
        normed_evac(2, hT)
        for t in range(TT):
            for half in range(2):
                done(A(h2[:, t, half * 512:(half + 1) * 512], take("h2"), ACT.Copy))
        act.drain().then_inc(h2_ready.sem, 1)
        for c in range(0, 16, 2):
            done(A(qTp[:, c:c + 2, :], take("qp").rearrange("p (c t) -> p c t", c=2), ACT.Copy))
        act.drain().then_inc(qTp_ready.sem, 1)
        for t in range(TT):
            for g in range(4):
                done(A(sp_[:, t, 4 * g:4 * g + 4, :], take("sp").rearrange("p (c n) -> p c n", c=4), ACT.Copy))
                act.drain().then_inc(scores_ready.sem, 1)
        for t in range(TT):
            act.wait_ge(*gate_shift_ready.at(0, t))
            A(gatep[:, t, :, :], gatep[:, t, :, :], ACT.Exp).then_inc(gate_exp_ready.sem, 1)
        for t in range(TT):
            act.wait_ge(*gelu_in_ready.at(0, t))
            A(g1[:, t * P:(t + 1) * P], g1[:, t * P:(t + 1) * P], ACT.Tanh, scale=float(np.sqrt(2.0 / np.pi))).then_inc(gelu_tanh_ready.sem, 1)
        act_ring.check("post")

    @block.vector
    def _(v):
        def take(tag, l=0):
            return dve_ring.take(v, l, tag)

        def done(ins):
            return ins.then_inc(dve_ring.free, 1)

        def tt(o, a, b, op):
            return v.tensor_tensor(o, a, b, op)

        def model_norm(i, src, dst):
            for t in range(TT):
                v.tensor_tensor_reduce(xn[:, t, :] if dst is xn else S_junk, src[:, t, :], src[:, t, :], 1.0, 0.0, ALU.mult, ALU.add, css2[:, t:t + 1])
                if dst is not xn:
                    v.drain()
            v.drain().then_inc(sumsq2_ready.sem, 1)
            v.wait_ge(*root2_ready.at(0, i))
            v.reciprocal(crs2, csd2)
            v.drain()
            for t in range(TT):
                v.tensor_scalar(dst[:, t, :], src[:, t, :], crs2[:, t:t + 1], None, ALU.mult)
            v.drain().then_inc(xn2_ready.sem, 1)

        def normed_evac(i, dst):
            for pair in range(1, 4, 2):
                b = take(f"hT{pair}")
                for c in range(2):
                    k = 2 * pair + c
                    last = v.tensor_scalar(dst[:, k, :], b[:, c * T:(c + 1) * T], AB[:, 2 * i, k:k + 1], AB[:, 2 * i + 1, k:k + 1], ALU.mult, ALU.add)
                done(last)
            v.drain().then_inc(hT2_by_dve.sem, 1)

        def head_norm(i, y, gain, n, d, factor=None):
            sq = junk[:, 0:n * d].rearrange("p (n d) -> p n d", n=n)
            tt(sq, y, y, ALU.mult)
            v.drain()
            v.tensor_reduce(ss2[:, 0:n], sq, AX.X, ALU.add).then_inc(head2_sumsq_ready.sem, 1)
            v.wait_ge(*head2_root_ready.at(0, i))
            v.reciprocal(rs2[:, 0:n], sd2[:, 0:n])
            v.drain()
            if factor is not None:
                v.tensor_scalar(rs2[:, 0:n], rs2[:, 0:n], factor, None, ALU.mult)
                v.drain()
            tt(y, y, bc(rs2[:, 0:n], 2, d), ALU.mult)
            v.drain()
            tt(y, y, bc(gain, 1, n), ALU.mult)
            v.drain()

        def pad(section, l=0):
            tags = dve_ring.filled[section]
            while len(dve_ring.emptied[section]) < len(tags):
                dve_ring.take(v, l, "pad")
                v.sem_inc(dve_step, 1)
                v.drain().then_inc(dve_ring.free, 1)
            dve_ring.check(section)

        v.wait_ge(const2_landed, 32)
        v.wait_ge(*cond_sig_ready.at(0))
        tt(cs, V2["c"].rearrange("p (k s) -> p k s", s=2), csig, ALU.mult)
        v.drain()
        v.tensor_copy(csb, bc(cs[:, :, 0], 2, P))
        v.drain().then_inc(cond_ready.sem, 1)
        model_norm(0, x, xn)
        v.wait_ge(ctx_landed, 16)
        model_norm(1, ctxs, ctxs)
        v.wait_ge(rows_landed, 16)
        bm = V2["b_mod"].rearrange("p (m c) -> p m c", m=4)
        for i in range(12):
            m, half = i // 2, i % 2
            b = take("mod")
            if m in (2, 5):
                r = rows2[:, m // 5, half * 512:(half + 1) * 512]
                done(tt(r, b, r, ALU.add))
            else:
                mi = {0: 0, 1: 1, 3: 2, 4: 3}[m]
                done(tt(modT[:, mi, 4 * half:4 * half + 4, :], b[:, 0:8].rearrange("p (c s) -> p c s", s=2),
                        bc(bm[:, mi, 4 * half:4 * half + 4], 2, 2), ALU.add))
        v.drain()
        for i, (scale_m, shift_m, s, g) in enumerate(((1, 0, 0, "norm1"), (1, 0, 1, "norm1"), (3, 2, 0, "norm2"))):
            v.scalar_tensor_tensor(AB[:, 2 * i, :], modT[:, scale_m, :, s], 1.0, V2[g], ALU.add, ALU.mult)
            v.tensor_copy(AB[:, 2 * i + 1, :], modT[:, shift_m, :, s])
        v.drain().then_inc(mod_ready.sem, 1)
        normed_evac(0, hT)
        normed_evac(1, hcT)
        for i in range(2):
            for t in range(4):
                done(v.tensor_copy(v2[:, t, i * 512:(i + 1) * 512], take("v2")))
        v.drain().then_inc(v2_copied.sem, 1)
        lam = V2["lam"].rearrange("p (k n) -> p k n", k=4)
        for i in range(2):
            v.tensor_tensor_reduce(junk[:, 0:64], lam[:, 2 * i, :], lam[:, 2 * i + 1, :], 1.0, 0.0, ALU.mult, ALU.add, lam2[:, i:i + 1])
            v.drain()
        v.sem_inc(lam_parts_ready.sem, 1)
        v.wait_ge(*lam_exp_ready.at(0))
        tt(nlam, lam2[:, 1:2], lam2[:, 0:1], ALU.subtract)
        v.drain()
        v.tensor_scalar(nlam, nlam, -(0.8 - 0.6 * float(np.exp(-0.3 * 0))), None, ALU.add)
        v.drain()
        v.wait_ge(*qk2_copied.at(0))
        acos, asin = (C2[n].rearrange("p (t a n) -> p t a n", t=TT, a=2) for n in ("acos", "asin"))
        for i in range(6):
            src = q2[:, i, :] if i < 2 else k2[:, i - 2, :]
            head_norm(i, src.rearrange("p (n d) -> p n d", n=16), V2["q_norm"] if i < 2 else V2["k_norm"], 16, 64)
            if i < 2 or i >= 4:
                t = i % 2
                y = src.rearrange("p (n a s f) -> p n a s f", n=16, a=2, s=2)
                x1, x2 = y[:, :, :, 0, :], y[:, :, :, 1, :]
                ta, tb, tc, td = (junk[:, 512 * j:512 * (j + 1)].rearrange("p (n a f) -> p n a f", n=16, a=2) for j in range(4))
                cb, sn = bc(acos[:, t, :, :], 1, 16), bc(asin[:, t, :, :], 1, 16)
                tt(ta, x1, cb, ALU.mult)
                tt(tb, x2, sn, ALU.mult)
                tt(tc, x2, cb, ALU.mult)
                tt(td, x1, sn, ALU.mult)
                v.drain()
                tt(x1, ta, tb, ALU.subtract)
                tt(x2, tc, td, ALU.add)
                v.drain()
            v.sem_inc(qk2_ready.sem, 1)
        for grp in range(4):
            for i in range(8):
                b = act_ring.peek(v, "attention", "S2", 8 * grp + i)
                m = mx2[:, i // 2, i % 2:i % 2 + 1]
                v.tensor_reduce(m, b, AX.X, ALU.max)
                v.drain()
                v.tensor_scalar(m, m, -0.125, None, ALU.mult).then_inc(diff_max_ready.sem, 1)
            v.wait_ge(*diff_exp_ready.at(0, grp))
            v.reciprocal(sc2, se2)
            v.drain()
            v.tensor_scalar(sc2[:, :, 1], sc2[:, :, 1], nlam, None, ALU.mult)
            v.drain()
            for hh in range(4):
                v.tensor_scalar(S2[:, hh, 1, :], S2[:, hh, 1, :], sc2[:, hh, 1:2], None, ALU.mult)
            v.drain()
            for hh in range(4):
                last = v.scalar_tensor_tensor(S2[:, hh, 0, :], S2[:, hh, 0, :], sc2[:, hh, 0:1], S2[:, hh, 1, :], ALU.mult, ALU.add)
            last.then_inc(diff_probs_ready.sem, 1)
        v.wait_ge(*diff_out_copied.at(0))
        head_norm(6, o2.rearrange("p t (h n) -> p (t h) n", h=8), V2["out_g"], 16, P, factor=0.6 * float(np.exp(-0.3 * 0)) + 0.2)
        v.sem_inc(diff_out_ready.sem, 1)
        for c in range(26):
            v.wait_ge(*shift_parts_ready.at(0, c))
            z = zs[:, c, :].rearrange("p (s t) -> p s t", s=2)
            r = zraw[:, c % 2, :].rearrange("p (s t) -> p s t", s=2)
            v.scalar_tensor_tensor(z[:, :, 1:T], r[:, :, 0:T - 1], V2["shift"][:, c:c + 1], z[:, :, 1:T], ALU.mult, ALU.add)
            v.drain()
            v.scalar_tensor_tensor(z[:, :, 0:T - 1], r[:, :, 1:T], V2["shift"][:, 52 + c:53 + c], z[:, :, 0:T - 1],
                                   ALU.mult, ALU.add).then_inc(shift_parts_used.sem, 1)
        v.drain().then_inc(shifted_ready.sem, 1)
        tt(kk, zs[:, 8:16, :], bc(V2["k_k"], 2, HALF), ALU.mult)
        v.drain()
        tt(Z_sq, kk, kk, ALU.mult)
        v.drain().then_inc(kk_sq_ready.sem, 1)
        v.wait_ge(*kk_root_ready.at(0))
        v.reciprocal(Z_sq, Z_sq)
        v.drain()
        tt(kk, kk, Z_sq, ALU.mult)
        v.memset(St, 0.0)
        v.memset(restart, 1.0)
        v.drain()
        v.memset(restart.rearrange("p (c t) -> p c t", c=8)[:, :, 0:1], 0.0)
        v.wait_ge(*lora_act_ready.at(0))
        pad("attention")
        v.drain().then_inc(scan_ready.sem, 1)

        dve_ring.section = "scan"
        strict, incl = (C2[n].rearrange("p (d t) -> p d t", d=2) for n in ("strict", "incl"))
        level = C2["level"].rearrange("p (m d t) -> p m d t", m=6, d=2)
        idb = bc(C2["id2"], 1, 8)

        def masked(l, tag, dst, mask):
            for d in range(2):
                last = tt(ch(dst)[:, 8 * d:8 * d + 8, :], take(tag, l).rearrange("p (c n) -> p c n", c=8), bc(mask(d), 1, 8), ALU.mult)
                done(last)

        with v.Fori(0, 2) as stream, v.Fori(0, 4) as step:
            l = stream * 4 + step
            t0 = stream * T + step * 64
            t1 = stream * T + (3 - step) * 64
            views = []
            for d, at in enumerate((t0, t1)):
                views.append(lambda src, at=at: src[:, :, bass.ds(at, 64)])
            for d in range(2):
                v.tensor_copy(lor[:, d, :], views[d](zs[:, 24:25, :])[:, 0, :])
            v.drain().then_inc(step_in_ready.sem, 1)
            for d in range(2):
                v.tensor_copy(ch2(Vt)[:, d, :, :], views[d](zs[:, 16:24, :]))
            for part, bias in ((0, "w0"), (1, "a0")):
                for d in range(2):
                    dst = (a0, a1)[part]
                    done(tt(ch2(dst)[:, d, :, :], take("lora", l).rearrange("p (c n) -> p c n", c=8),
                            bc(V2[bias].rearrange("p (d c) -> p d c", d=2)[:, d, :], 2, 64), ALU.add))
            v.drain().then_inc(lora_sums_ready.sem, 1)
            v.wait_ge(*rates_ready.at(l))
            v.tensor_tensor_scan(a2[:, 0:512], restart, a0[:, 0:512], 0.0, ALU.mult, ALU.add)
            v.tensor_tensor_scan(a2[:, 512:1024][:, ::-1], restart, a0[:, 512:1024][:, ::-1], 0.0, ALU.mult, ALU.add)
            v.drain()
            tt(a3, a2, a0, ALU.subtract)
            v.drain().then_inc(cumsum_ready.sem, 1)
            v.wait_ge(*decays_ready.at(l))
            v.tensor_copy(Wc[:, 0:8], ch2(a0)[:, 0, :, 63])
            v.tensor_copy(Wc[:, 8:16], ch2(a0)[:, 1, :, 0])
            for d in range(2):
                tt(ch2(Pm)[:, d, :, :], views[d](kk), ch2(a3)[:, d, :, :], ALU.mult)
                tt(ch2(Rm)[:, d, :, :], views[d](zs[:, 0:8, :]), ch2(a0)[:, d, :, :], ALU.mult)
                tt(ch2(Qm)[:, d, :, :], views[d](kk), ch2(a1)[:, d, :, :], ALU.mult)
            v.drain()
            tt(Qm, Qm, a2, ALU.mult)
            v.tensor_scalar(a3, a1, 1.0, None, ALU.subtract)
            v.drain()
            for d in range(2):
                tt(ch2(a3)[:, d, :, :], ch2(a3)[:, d, :, :], bc(V2["k_a"], 2, 64), ALU.mult)
            v.drain()
            v.tensor_scalar(a3, a3, 1.0, None, ALU.add)
            v.drain()
            for d in range(2):
                tt(ch2(a3)[:, d, :, :], ch2(a3)[:, d, :, :], views[d](zs[:, 8:16, :]), ALU.mult)
            v.drain()
            tt(Km, a3, a2, ALU.mult)
            v.drain().then_inc(pqkr_ready.sem, 1)
            masked(l, "Apk", Apk, lambda d: strict[:, d, :])
            masked(l, "Ark", Ark, lambda d: incl[:, d, :])
            masked(l, "Arq", Arq, lambda d: incl[:, d, :])
            masked(l, "LT", LT, lambda d: strict[:, d, :])
            v.wait_ge(*tokens_ready.at(l))
            banks = [take("L", l) for _ in range(2)]
            for d in range(2):
                done(tt(ch(Loff)[:, 8 * d:8 * d + 8, :], banks[d].rearrange("p (c n) -> p c n", c=8), bc(level[:, 0, 1 - d, :], 1, 8), ALU.mult))
            v.drain()
            for d in range(2):
                c = slice(8 * d, 8 * d + 8)
                tt(ch(Dm)[:, c, :], idb, ch(Loff)[:, c, :], ALU.subtract)
                tt(ch(DTm)[:, c, :], ch(LT)[:, c, :], bc(level[:, 0, d, :], 1, 8), ALU.mult)
            v.drain()
            for d in range(2):
                c = slice(8 * d, 8 * d + 8)
                tt(ch(DTm)[:, c, :], idb, ch(DTm)[:, c, :], ALU.subtract)
                tt(ch(Loff)[:, c, :], ch(LT)[:, c, :], bc(level[:, 1, d, :], 1, 8), ALU.mult)
            v.drain().then_inc(inverse_ready.sem, 1)
            for j in range(5):
                banks = [take("ET", l) for _ in range(2)]
                if j < 4:
                    banks += [take("E", l) for _ in range(2)]
                for i, b in enumerate(banks):
                    m = (DTm, Dm)[i // 2][:, (i % 2) * 512:(i % 2 + 1) * 512]
                    done(tt(m, m, b, ALU.subtract))
                if j < 4:
                    for d in range(2):
                        c = slice(8 * d, 8 * d + 8)
                        tt(ch(Loff)[:, c, :], ch(LT)[:, c, :], bc(level[:, 2 + j, d, :], 1, 8), ALU.mult)
                v.drain().then_inc(inverse_ready.sem, 1)
            for d in range(2):
                s = St[:, d * 512:(d + 1) * 512]
                done(tt(s, take("St", l), s, ALU.add))
            v.drain()
            tt(ch(St), ch(St), bc(Wc, 2, 64), ALU.mult)
            v.wait_ge(*y_stored.at(l))
            yv = yb.rearrange("p d c s n -> p d c (s n)")
            v.tensor_copy(yv[:, 0, :, bass.ds(step * 64, 64)], ch2(YOUT)[:, 0, :, :])
            v.tensor_copy(yv[:, 1, :, bass.ds((3 - step) * 64, 64)], ch2(YOUT)[:, 1, :, :])
            v.drain()
            pad("scan", l)
            v.drain()
        v.sem_inc(scan_done_dve, 1)

        dve_ring.section = "post"
        y0 = yb[:, 0, :, :, :].rearrange("p c s n -> p (c s) n")
        y1 = yb[:, 1, :, :, :].rearrange("p c s n -> p (c s) n")
        tt(y0, y0, y1, ALU.add)
        v.drain()
        v.tensor_reduce(ys, y0, AX.X, ALU.add)
        v.drain()
        v.tensor_scalar(ys, ys, 1.0 / 64, None, ALU.mult)
        v.drain()
        tt(y0, y0, bc(ys, 2, 64), ALU.subtract)
        v.drain()
        tt(y1, y0, y0, ALU.mult)
        v.drain()
        v.tensor_reduce(ys, y1, AX.X, ALU.add)
        v.drain().then_inc(y_var_ready.sem, 1)
        v.wait_ge(*y_root_ready.at(0))
        v.reciprocal(yr, yd)
        v.drain()
        tt(y0, y0, bc(yr, 2, 64), ALU.mult)
        v.drain().then_inc(y_ready.sem, 1)
        tt(rtmp, zs[:, 0:8, T:2 * T], zs[:, 8:16, T:2 * T], ALU.mult)
        v.drain()
        tt(rtmp, rtmp, bc(V2["r_k"], 2, T), ALU.mult)
        v.drain().then_inc(bonus_in_ready.sem, 1)
        for c in range(0, 8, 2):
            b = take("yT")
            for j in range(2):
                last = v.tensor_scalar(obx[:, c + j, :], b[:, j * T:(j + 1) * T], V2["ln_g"][:, c + j:c + j + 1],
                                       V2["ln_b"][:, c + j:c + j + 1], ALU.mult, ALU.add)
            done(last)
        v.drain()
        for c in range(0, 8, 2):
            b = take("bonus")
            done(tt(BON[:, c:c + 2, :], b.rearrange("p (c t) -> p c t", c=2), zs[:, 16 + c:18 + c, T:2 * T], ALU.mult))
        v.drain()
        tt(obx, obx, BON, ALU.add)
        v.drain()
        for c in range(0, 8, 2):
            b = take("g")
            done(tt(obx[:, c:c + 2, :], obx[:, c:c + 2, :], b.rearrange("p (c t) -> p c t", c=2), ALU.mult))
        v.drain().then_inc(obx_ready.sem, 1)
        for m in range(2):
            v.wait_ge(*gate2_ready.at(0, m))
            for c in range(0, 8, 2):
                b = take("mix2").rearrange("p (c t) -> p c t", c=2)
                g = gsig2[:, c:c + 2, :]
                done(tt(mg2[:, c:c + 2, :] if m == 0 else g, b, g, ALU.mult))
            v.drain()
            if m:
                tt(mg2, mg2, gsig2, ALU.add)
                v.drain()
            v.sem_inc((gate2_used, merged2_ready)[m].sem, 1)
        for half in range(2):
            for t in range(TT):
                xs, r = x[:, t, half * 512:(half + 1) * 512], rows2[:, 0, half * 512:(half + 1) * 512]
                j = junk[:, (2 * half + t) * 512:(2 * half + t + 1) * 512]
                done(tt(j, take("out2"), r, ALU.mult))
                v.drain()
                tt(xs, xs, j, ALU.add)
        v.drain()
        model_norm(2, x, xn)
        normed_evac(2, hT)

        for t in range(TT):
            for g in range(4):
                v.wait_ge(*scores_ready.at(0, 4 * t + g))
                for c in range(4 * g, 4 * g + 4):
                    v.max(sv[:, t, c, 0:8], sp_[:, t, c, :])
                v.drain()
                for c in range(4 * g, 4 * g + 4):
                    v.max_index(siu_u[:, t, c, 0:8], sv[:, t, c, 0:8], sp_[:, t, c, :])
                for c in range(4 * g, 4 * g + 4):
                    v.match_replace(sp_[:, t, c, :], sv[:, t, c, 0:8], sp_[:, t, c, :], -3e38)
                v.drain()
                for c in range(4 * g, 4 * g + 4):
                    v.max(sv[:, t, c, 8:16], sp_[:, t, c, :])
                v.drain()
                for c in range(4 * g, 4 * g + 4):
                    v.max_index(siu_u[:, t, c, 8:16], sv[:, t, c, 8:16], sp_[:, t, c, :])
            v.drain()
            v.tensor_copy(sif[:, t, :, :], siu_u[:, t, :, :])
            svv = sv[:, t, :, :].rearrange("p (h s) n -> p h s n", s=2)
            tt(cand.rearrange("p h (i j) -> p h i j", i=16), bc(svv[:, :, 0, :], 3, 16), bc(svv[:, :, 1, :], 2, 16), ALU.add)
            v.drain()
            for h in range(8):
                v.max(tops[:, t, h, 0:8], cand[:, h, :])
            v.drain()
            for h in range(8):
                v.max_index(posu_u[:, t, h, 0:8], tops[:, t, h, 0:8], cand[:, h, :])
            for h in range(8):
                v.match_replace(cand[:, h, :], tops[:, t, h, 0:8], cand[:, h, :], -3e38)
            v.drain()
            for h in range(8):
                v.max(tops[:, t, h, 8:16], cand[:, h, :])
            v.drain()
            for h in range(8):
                v.max_index(posu_u[:, t, h, 8:16], tops[:, t, h, 8:16], cand[:, h, :])
            v.drain()
            pu = posu_u[:, t, :, :].rearrange("p h n -> p (h n)")
            v.tensor_scalar(hiu_u[:, 0:P], pu, 4, None, ALU.logical_shift_right)
            v.tensor_scalar(lou_u[:, 0:P], pu, 15, None, ALU.bitwise_and)
            v.drain()
            v.tensor_copy(hif, hiu_u[:, 0:P])
            v.tensor_copy(lof, lou_u[:, 0:P])
            v.drain()
            siv = sif[:, t, :, :].rearrange("p (h s) n -> p h s n", s=2)
            for s, (src, dst) in enumerate(((hif, i1f), (lof, i2f))):
                e3 = eqb.rearrange("p (k n) -> p k n", n=16)
                tt(e3, bc(src, 2, 16), bc(C2["iota16"], 1, P), ALU.is_equal)
                v.drain()
                e4 = eqb.rearrange("p (h k n) -> p h k n", h=8, k=16)
                tt(e4, e4, bc(siv[:, :, s, :], 2, 16), ALU.mult)
                v.drain()
                v.tensor_reduce(dst, e3, AX.X, ALU.add)
                v.drain()
            v.scalar_tensor_tensor(i1f, i1f, float(P), i2f, ALU.mult, ALU.add)
            v.drain()
            v.tensor_copy(eidx_u[:, t * P:(t + 1) * P], i1f).then_inc(experts_ready.sem, 1)
            tt(gatep[:, t, :, :], tops[:, t, :, :], bc(tops[:, t, :, 0], 2, 16), ALU.subtract)
            v.drain().then_inc(gate_shift_ready.sem, 1)
        for t in range(TT):
            v.wait_ge(*gate_exp_ready.at(0, t))
            v.tensor_reduce(gsm[:, 0:8], gatep[:, t, :, :], AX.X, ALU.add)
            v.drain()
            v.reciprocal(grc[:, 0:8], gsm[:, 0:8])
            v.drain()
            tt(gatep[:, t, :, :], gatep[:, t, :, :], bc(grc[:, 0:8], 2, 16), ALU.mult)
            v.drain()
        v.wait_ge(*h2_ready.at(0))
        NB = P // GB
        for t in range(TT):
            with v.Fori(0, NB) as j:
                for i in range(GB):
                    v.wait_ge(row_landed[i], (j + t * NB) * 16 + 16)
                    v.sem_inc(dve_step, 1)
                    v.tensor_tensor_reduce(gat[:, i, :], gat[:, i, :], h2[:, t, :], 1.0, 0.0, ALU.mult, ALU.add,
                                           dot8[:, i:i + 1]).then_inc(row_used[i], 1)
                v.drain()
                v.tensor_copy(actp[:, bass.ds(j * GB + t * P, GB)], dot8[:, 0:GB])
                v.drain()
        for t in range(TT):
            c = slice(t * P, (t + 1) * P)
            tt(g1[:, c], actp[:, c], actp[:, c], ALU.mult)
            v.drain()
            v.tensor_scalar(g1[:, c], g1[:, c], 0.044715, 1.0, ALU.mult, ALU.add)
            v.drain()
            tt(g1[:, c], g1[:, c], actp[:, c], ALU.mult)
            v.drain().then_inc(gelu_in_ready.sem, 1)
            v.wait_ge(*gelu_tanh_ready.at(0, t))
            v.tensor_scalar(g1[:, c], g1[:, c], 1.0, 0.5, ALU.add, ALU.mult)
            v.drain()
            tt(g1[:, c], g1[:, c], actp[:, c], ALU.mult)
            v.drain()
            tt(g1[:, c], g1[:, c], gatep[:, t, :, :].rearrange("p h n -> p (h n)"), ALU.mult)
            v.drain()
        v.memset(acc, 0.0)
        v.drain()
        for t in range(TT):
            with v.Fori(0, NB) as j:
                v.tensor_copy(wt8[:, 0:GB], g1[:, bass.ds(j * GB + t * P, GB)])
                v.drain()
                for i in range(GB):
                    v.wait_ge(row_landed[i], (j + (TT + t) * NB) * 16 + 16)
                    v.scalar_tensor_tensor(acc[:, t, :], gat[:, i, :], wt8[:, i:i + 1], acc[:, t, :], ALU.mult, ALU.add).then_inc(row_used[i], 1)
                    v.drain()
        for t in range(TT):
            tt(acc[:, t, :], acc[:, t, :], rows2[:, 1, :], ALU.mult)
        v.drain()
        tt(x, x, acc, ALU.add).then_inc(out_ready.sem, 1)
        dve_ring.check("post")

    @block.gpsimd
    def _(pool):
        NB = P // GB
        for i in range(GB):
            pool.sem_inc(row_used[i], 1)
        for k, table in enumerate((PU, PV)):
            for t in range(TT):
                if k == 0:
                    pool.wait_ge(*experts_ready.at(0, t))
                with pool.Fori(0, NB // 2) as pair:
                    for e in range(2):
                        j = pair * 2 + e
                        cols8 = idx8_u[:, e * GB:(e + 1) * GB]
                        pool.tensor_copy(cols8, eidx_u[:, bass.ds(j * GB + t * P, GB)]).then_inc(pool_copied, 1)
                        pool.wait_ge(pool_copied, j + (k * TT + t) * NB + 1)
                        pool.sem_inc(idx_used, 1)
                        for i in range(GB):
                            pool.wait_ge(row_used[i], j + (k * TT + t) * NB + 1)
                            pool.sem_inc(idx_used, 1)
                            pool.indirect_dma_start(out=gat[:, i, :], out_offset=None, in_=table,
                                                    in_offset=bass.IndirectOffsetOnAxis(ap=cols8[:, i:i + 1], axis=0)).then_inc(row_landed[i], 16)

    second_block.close()
    ctx.close()


def kernel(**inputs):
    import concourse.bacc as bacc
    from concourse.bass_utils import run_bass_kernel_spmd

    a = {n: np.asarray(v) for n, v in inputs.items()}
    arrays = {
        "weights1": np.stack([pack_weights1(a, l) for l in range(LAYERS)]),
        "vectors1": np.stack([pack_vectors1(a, l) for l in range(LAYERS)]),
        "tables1": constants(),
        "weights2": pack_weights2(a),
        "vectors2": pack_vectors2(a),
        "tables2": constants2(),
        "gate_rows2": gate_rows2(a),
        "peer_u": a["peer_u_2"][0],
        "peer_v": a["peer_v_2"][0],
        "x": a["x"][0],
        "ctx": a["ctx_2"][0],
    }
    arrays = {n: np.ascontiguousarray(v) for n, v in arrays.items()}
    nc = bacc.Bacc("TRN2", target_bir_lowering=False, num_devices=1)
    args = [nc.dram_tensor(n, v.shape, F32, kind="ExternalInput").ap() for n, v in arrays.items()]
    out = nc.dram_tensor("out", (T, D), F32, kind="ExternalOutput").ap()
    build_program(nc, *args, out)
    r = run_bass_kernel_spmd(nc, [arrays], core_ids=[0])
    return r.results[0]["out"].reshape(1, T, D)
```

```python
from contextlib import ExitStack

import numpy as np

import concourse.bass as bass
from concourse import mybir
from concourse.alu_op_type import AluOpType as ALU

F32 = mybir.dt.float32
U32 = mybir.dt.uint32
ACT = mybir.ActivationFunctionType
AX = mybir.AxisListType

P = 128
T = 256
TT = T // P
D = 1024
DC = D // P
EPS = 1e-6
NEG = -1e30
LAYERS = 2

MH, MQK, MROPE, MNOPE, MV = 8, 96, 32, 64, 64
NH, NG, ND, NROPE, NCMP = 8, 2, 64, 16, 15
CONV_W = 31
C_CQ, C_CKV, C_U, C_QN, C_KVN, C_GN, C_GM = 0, 384, 672, 1696, 2208, 2976, 3000

SLOT = 4608
SLOTS = 3
MEM_COLS = 53200

def sections(*parts):
    out, at = {}, 0
    for name, passes, per in parts:
        out[name] = (at, per)
        at += passes * per
    out["post"] = (at, 0)
    return out


SECTIONS_ACT = sections(("layers", LAYERS, 92), ("attention", 1, 120), ("scan_first", 1, 16), ("scan_ctx", 3, 20),
                        ("scan_turn", 1, 20), ("scan_x", 2, 20), ("scan_end", 1, 20), ("scan_last", 1, 4))
SECTIONS_DVE = sections(("layers", LAYERS, 64), ("attention", 1, 28), ("scan_first", 1, 32), ("scan_ctx", 3, 32),
                        ("scan_turn", 1, 36), ("scan_x", 2, 36), ("scan_end", 1, 32), ("scan_last", 1, 4))

ITEMS1 = ([("u_gate", 4096), ("u_a", 4096), ("cq", 3072), ("ckv_uq", 4608), ("ukv_kvn2", 4288),
           ("qn", 4096), ("kvn1", 4096), ("cmp", 4096)]
          + [(f"{m}{n}", 4096) for m in "ACB" for n in ("g0", "g1", "o")]
          + [("out0", 4096), ("out1", 4096)]
          + [(f"ff1_{i}", 4096) for i in range(8)] + [(f"ff2_{i}", 4096) for i in range(8)]
          + [("pad", 0)])
ITEMS2 = ([(f"mod{i}", 4096) for i in range(12)]
          + [("q0", 4096), ("q1", 4096), ("k0", 4096), ("k1", 4096), ("v0", 4096), ("v1", 4096)]
          + [(f"rw{i}", 4096) for i in range(6)] + [("rw6", 2048)]
          + [("g0A", 4096), ("g1A", 4096), ("oA0", 4096), ("oA1", 4096),
             ("g0B", 4096), ("g1B", 4096), ("oB0", 4096), ("oB1", 4096), ("out0", 4096), ("out1", 4096)]
          + [(f"wq{i}", 4096) for i in range(4)])


def offsets(items):
    out, at = {}, 0
    for name, n in items:
        out[name] = at
        at += n
    return out, at


def layout(fields):
    return offsets(fields)


VEC1 = [("g_mix", 8), ("g_cq", 3), ("g_ckv", 2), ("b_glu", 8), ("b_dw", 4), ("g_ln", 4), ("b_ln", 4),
        ("b_co", 8), ("g_ffn", 8), ("w_dw", 4 * CONV_W), ("pe", 32), ("k2", 64), ("v2", 64),
        ("g_q_mla", 96), ("g_k_mla", 96), ("g_q_nsa", 64), ("g_k_nsa", 64)]
CON = [("ident", 128), ("cmask", 256), ("cmpmask", 2 * NCMP), ("mcos", 32), ("msin", 32),
       ("ncos", 16), ("nsin", 16), ("ccos", 8), ("csin", 8), ("eps", 1), ("l2eps", 1), ("lneps", 1), ("ones", 64)]
CON2 = [("acos", 64), ("asin", 64), ("id2", 64), ("onesbd", 128), ("strict", 128), ("incl", 128),
        ("level", 6 * 128), ("iota16", 16), ("heads", 4)]
VEC2 = [("norm1", 8), ("norm2", 8), ("b_mod", 32), ("c", 16), ("q_norm", 64), ("k_norm", 64), ("lam", 256),
        ("out_g", 128), ("shift", 78), ("w0", 16), ("a0", 16), ("k_k", 8), ("k_a", 8), ("r_k", 8),
        ("ln_g", 8), ("ln_b", 8)]


def constants():
    o, n = layout(CON)
    c = np.zeros((P, n), np.float32)
    p = np.arange(P)

    def put(name, a):
        a = np.asarray(a, np.float32).reshape(a.shape[0], -1)
        c[:a.shape[0], o[name]:o[name] + a.shape[1]] = a

    put("ident", np.eye(P))
    put("cmask", np.concatenate([np.zeros((P, P)), np.where(p[None, :] <= p[:, None], 0.0, NEG)], 1))
    t = p[:, None] + P * np.arange(TT)[None, :]
    cp = np.arange(NCMP) * 16 + 31
    put("cmpmask", np.where(cp[None, None, :] <= t[:, :, None], 0.0, NEG))

    def rot(pos, rot_dim, theta):
        half = rot_dim // 2
        inv = np.power(np.float32(theta), -np.arange(half, dtype=np.float32) * np.float32(2.0 / rot_dim))
        ang = pos[..., None].astype(np.float32) * inv.astype(np.float32)
        return np.cos(ang), np.sin(ang)

    for name, (cs, sn) in (("m", rot(t, MROPE, 500000.0)), ("n", rot(t, NROPE, 500000.0)),
                           ("c", rot(np.tile(cp, NG), NROPE, 500000.0))):
        put(name + "cos", cs)
        put(name + "sin", sn)
    c[:, o["eps"]] = EPS
    c[:, o["l2eps"]] = 1e-12
    c[:, o["lneps"]] = 64e-5
    c[:, o["ones"]:o["ones"] + 64] = 1.0
    return c


def constants2():
    o, n = layout(CON2)
    c = np.zeros((P, n), np.float32)
    p = np.arange(P)

    def put(name, a):
        a = np.asarray(a, np.float32).reshape(P, -1)
        c[:, o[name]:o[name] + a.shape[1]] = a

    t = p[:, None] + P * np.arange(TT)[None, :]
    inv = (10000.0 ** (-np.arange(16, dtype=np.float32) / 16)).astype(np.float32)
    ang = np.stack([(t // 64).astype(np.float32)[..., None] * inv, (t % 64).astype(np.float32)[..., None] * inv], 2)
    put("acos", np.cos(ang))
    put("asin", np.sin(ang))
    put("id2", np.tile(np.eye(64), (2, 1)))
    put("onesbd", p[:, None] // 64 == p[None, :] // 64)
    s = np.arange(64)
    before = np.stack([s[:, None] < s[None, :], s[:, None] > s[None, :]], 1)
    put("strict", np.tile(before, (2, 1, 1)))
    put("incl", np.tile(before | np.eye(64, dtype=bool)[:, None, :], (2, 1, 1)))
    levels = []
    for m in (1, 2, 4, 8, 16, 32):
        same = (s[:, None] // (2 * m) == s[None, :] // (2 * m)) & (s[:, None] // m != s[None, :] // m)
        levels.append(before & same[:, None, :])
    put("level", np.tile(np.stack(levels, 1), (2, 1, 1, 1)))
    put("iota16", np.tile(np.arange(16), (P, 1)))
    even = (p < 64).astype(np.float32)
    put("heads", np.stack([even, 1 - even, -even, even - 1], 1))
    return c


def km(w):
    k, n = w.shape
    return w.reshape(k // P, P, n).transpose(1, 0, 2).reshape(P, -1)


def cols(v):
    return v.reshape(-1, P).T


def rows(v):
    return np.broadcast_to(v.reshape(1, -1), (P, v.size))


KV_ORDER = np.concatenate([np.arange(o, o + 64) for o in (0, 128, 64, 192)] + [np.arange(256, 512)])


def pack_weights1(a, l):
    w = a["w_in"][l]
    u = C_U
    parts = [km(w[:, u + 512:u + 1024]), km(w[:, u:u + 512]), km(w[:, C_CQ:C_CKV]),
             km(w[:, C_CKV:C_U]), km(a["w_uq"][l]), km(a["w_ukv"][l]), km(w[:, C_KVN + 512:C_GM]),
             km(w[:, C_QN:C_KVN]), km(w[:, C_KVN:C_KVN + 512][:, KV_ORDER])]
    c1 = [a[n][l].reshape(32, 64, P).transpose(1, 0, 2).reshape(64, -1) for n in ("w_cmp_k1", "w_cmp_v1")]
    parts.append(np.concatenate(c1, 0))
    for m, o in ((0, "w_o_mla"), (2, "w_o_nsa"), (1, "w_conv_out")):
        g = C_GM + m * D
        parts += [km(w[:, g:g + 512]), km(w[:, g + 512:g + 1024]), km(a[o][l])]
    parts += [km(a["w_out"][l][:, :512]), km(a["w_out"][l][:, 512:])]
    parts += [km(a["w_ff1"][l][:, i * 512:(i + 1) * 512]) for i in range(8)]
    parts += [km(a["w_ff2"][l][i * 512:(i + 1) * 512]) for i in range(8)]
    return np.concatenate(parts, 1)


def pack_vectors1(a, l):
    f = {"g_mix": cols(a["g_mix"][l]), "g_cq": cols(a["g_cq"][l]), "g_ckv": cols(a["g_ckv"][l]),
         "b_glu": cols(a["b_glu"][l]), "b_dw": cols(a["b_dw"][l]), "g_ln": cols(a["g_conv_ln"][l]),
         "b_ln": cols(a["b_conv_ln"][l]), "b_co": cols(a["b_conv_out"][l]), "g_ffn": cols(a["g_ffn"][l]),
         "w_dw": a["w_dw"][l].reshape(CONV_W, 4, P).transpose(2, 1, 0).reshape(P, -1),
         "pe": np.concatenate([a["pe_cmp_k"][l].T, a["pe_cmp_v"][l].T], 0),
         "k2": a["w_cmp_k2"][l], "v2": a["w_cmp_v2"][l],
         "g_q_mla": rows(a["g_q_mla"][l]), "g_k_mla": rows(a["g_k_mla"][l]),
         "g_q_nsa": rows(a["g_q_nsa"][l]), "g_k_nsa": rows(a["g_k_nsa"][l])}
    return np.concatenate([f[n] for n, _ in VEC1], 1)


def pack_weights2(a):
    g = {n[:-2]: v[0] for n, v in a.items() if n.endswith("_2") and v.ndim > 1 and n not in ("c_2", "ctx_2")}
    w, m = g["w_in"], g["w_mod"]
    parts = [km(m[:, i * 512:(i + 1) * 512]) for i in range(12)]
    parts += [km(w[:, i * 512:(i + 1) * 512]) for i in range(6)]
    parts += [km(w[:, 3072 + i * 512:min(3072 + (i + 1) * 512, 6400)]) for i in range(7)]
    for i, n in enumerate(("w_branch_a", "w_branch_b")):
        gate = w[:, 6400 + i * D:6400 + (i + 1) * D]
        parts += [km(gate[:, :512]), km(gate[:, 512:]), km(g[n][:, :512]), km(g[n][:, 512:])]
    parts += [km(g["w_out"][:, :512]), km(g["w_out"][:, 512:])]
    parts += [km(g["peer_wq"][:, i * 512:(i + 1) * 512]) for i in range(4)]
    up = np.concatenate([g["rw_w_up"], g["rw_a_up"]], 1).transpose(1, 0, 2).reshape(P, -1)
    keys = g["peer_keys"].reshape(16, P, P).transpose(2, 0, 1).reshape(P, -1)
    parts += [up, g["rw_g_up"], keys]
    return np.concatenate(parts, 1)


def pack_vectors2(a):
    b = a["b_mod_2"][0]
    r = lambda v: cols(v.reshape(-1))
    f = {"norm1": cols(a["norm1_g_2"][0]), "norm2": cols(a["norm2_g_2"][0]),
         "b_mod": np.concatenate([cols(b[m * D:(m + 1) * D]) for m in (0, 1, 3, 4)], 1),
         "c": np.stack([cols(a["c_2"][0]), cols(a["c_ctx_2"])], 2).reshape(P, 16),
         "q_norm": rows(a["q_norm_g_2"][0]), "k_norm": rows(a["k_norm_g_2"][0]), "lam": rows(a["diff_lambda_2"][0]),
         "out_g": rows(a["diff_out_g_2"][0]), "shift": r(a["rw_shift_2"][0]),
         "w0": r(a["rw_w0_2"][0]), "a0": r(a["rw_a0_2"][0]), "k_k": r(a["rw_k_k_2"][0]), "k_a": r(a["rw_k_a_2"][0]),
         "r_k": r(a["rw_r_k_2"][0]), "ln_g": r(a["rw_ln_g_2"][0]), "ln_b": r(a["rw_ln_b_2"][0])}
    return np.concatenate([f[n] for n, _ in VEC2], 1)


def gate_rows2(a):
    b = a["b_mod_2"][0]
    return np.concatenate([rows(b[2 * D:3 * D]), rows(b[5 * D:6 * D])], 1)


class Signal:

    def __init__(self, sem, per):
        self.sem, self.per = sem, per

    def at(self, l, i=0):
        return self.sem, l * self.per + i + 1


class PsumRing:

    def __init__(self, banks, full, free, sections):
        self.banks, self.full, self.free, self.sections = banks, full, free, sections
        self.filled = {name: [] for name in sections}
        self.emptied = {name: [] for name in sections}
        self.pe_section = self.section = "layers"

    def count(self, section, l, n):
        before, per = self.sections[section]
        return l * per + (before + n + 1)

    def open(self, pe, l, tag):
        tags = self.filled[self.pe_section]
        tags.append(tag)
        n = len(tags) - 1
        pe.wait_ge(self.free, self.count(self.pe_section, l, n))
        return self.banks[:, n % 4, :]

    def take(self, eng, l, tag):
        tags = self.emptied[self.section]
        tags.append(tag)
        n = len(tags) - 1
        eng.wait_ge(self.full, self.count(self.section, l, n))
        return self.banks[:, n % 4, :]

    def peek(self, eng, section, tag, k):
        n = [i for i, t in enumerate(self.filled[section]) if t == tag][k]
        eng.wait_ge(self.full, self.count(section, 0, n))
        return self.banks[:, n % 4, :]

    def check(self, section):
        f, e = self.filled[section], self.emptied[section]
        assert f == e, [z for z in zip(f + [None] * 9, e + [None] * 9) if z[0] != z[1]][:3]


class WeightRing:

    def __init__(self, slots, landed, used):
        self.slots, self.landed, self.used = slots, landed, used

    def view(self, n, count):
        s = (n % SLOTS) * SLOT
        return self.slots[:, s:s + count]

    def loads_before(self, n):
        return sum(1 for m in range(n % SLOTS, n + 1, SLOTS) if ITEMS1[m][1])


def km_view(ap, n):
    return ap.rearrange("p (k n) -> p k n", n=n)


def build_program(nc, W1, V1, K1, W2, VV2, K2, R2, PU, PV, xin, cin, out):
    ctx = ExitStack()
    mem = ctx.enter_context(nc.sbuf_tensor("mem", [P, MEM_COLS], F32))
    psum = ctx.enter_context(nc.psum_tensor("psum", [P, 8, 512], F32))
    used_cols = [0]

    def sb(n, at=None):
        if at is None:
            at = used_cols[0]
            used_cols[0] += n
        return mem[:, at:at + n]

    def sem(name):
        return ctx.enter_context(nc.semaphore(name))

    def signal(name, per=1):
        return Signal(sem(name), per)

    def bc(ap, axis, n):
        ap = ap.unsqueeze(axis)
        shape = list(ap.shape)
        shape[axis] = n
        return ap.to_broadcast(shape)

    x = sb(TT * D).rearrange("p (t n) -> p t n", t=TT)
    hT = sb(DC * T).rearrange("p (c t) -> p c t", c=DC)
    slots = sb(SLOTS * SLOT)
    vo1, nv1 = layout(VEC1)
    co, ncon = layout(CON)
    vec, con = sb(nv1), sb(ncon)
    V = {n: vec[:, vo1[n]:vo1[n] + w] for n, w in VEC1}
    C = {n: con[:, co[n]:co[n] + w] for n, w in CON}
    ident = C["ident"]
    vo2, nv2 = layout(VEC2)
    co2, ncon2 = layout(CON2)
    vec2, con2 = sb(nv2), sb(ncon2)
    V2 = {n: vec2[:, vo2[n]:vo2[n] + w] for n, w in VEC2}
    C2 = {n: con2[:, co2[n]:co2[n] + w] for n, w in CON2}
    base = used_cols[0]

    junk = sb(2560)
    xn = junk[:, 0:2048].rearrange("p (t n) -> p t n", t=TT)
    sg = sb(1024).rearrange("p (c t) -> p c t", c=4)
    upad = sb(4 * (T + CONV_W - 1)).rearrange("p (c t) -> p c t", c=4)
    cacc = sb(1024).rearrange("p (c t) -> p c t", c=4)
    cvT = sb(1024).rearrange("p (c t) -> p c t", c=4)
    r1 = used_cols[0]
    cq = sb(768).rearrange("p (t n) -> p t n", t=TT)
    ckvr = sb(576).rearrange("p (t n) -> p t n", t=TT)
    cqT = sb(768).rearrange("p (c t) -> p c t", c=3)
    ckvT = sb(512).rearrange("p (c t) -> p c t", c=2)
    r2 = used_cols[0]
    qm = sb(1536).rearrange("p (t h n) -> p t h n", t=TT, h=MH)
    kf = sb(1536).rearrange("p (t h n) -> p t h n", t=TT, h=MH)
    r3 = used_cols[0]
    qT = sb(2048).rearrange("p (h t) -> p h t", h=MH)
    kT = sb(2048).rearrange("p (h t) -> p h t", h=MH)
    vm = sb(1024).rearrange("p (t h n) -> p t h n", t=TT, h=MH)
    S = sb(8 * 384).rearrange("p (h n) -> p h n", h=8)
    PT = sb(8 * 384).rearrange("p (h n) -> p h n", h=8)
    oTm = sb(1024).rearrange("p (c t) -> p c t", c=4)
    oTn = sb(1024).rearrange("p (c t) -> p c t", c=4)
    qn = sb(1024).rearrange("p (t h n) -> p t h n", t=TT, h=NH)
    kvn = sb(TT * 792).rearrange("p (t n) -> p t n", t=TT)
    nk = sb(512).rearrange("p (s t g n) -> p s t g n", s=2, t=TT, g=NG)
    small = sb(512)
    gates = sb(48)
    hid = sb(180)
    kc = sb(64)
    scmp = sb(240).rearrange("p (t h n) -> p t h n", t=TT, h=NH)
    pcmp = sb(512).rearrange("p (t h n) -> p t h n", t=TT, h=NH)
    vbd = sb(512).rearrange("p (c n) -> p c n", c=4)
    blk = sb(960, r1).rearrange("p (l g c) -> p l g c", l=32, g=NG)
    kcT = sb(512, r1 + 960).rearrange("p (g t) -> p g t", g=NG)
    pcT = sb(512, r1 + 1472).rearrange("p (g t) -> p g t", g=NG)
    nkT = sb(1024, r2).rearrange("p (s g t) -> p s g t", s=2, g=NG)
    kcmpT = sb(30, r2 + 1024)
    qnT = qT
    gsig = sb(4096, r2).rearrange("p (b c t) -> p b c t", b=2, c=DC)
    mg = sb(2048, r2 + 4096).rearrange("p (c t) -> p c t", c=DC)
    fT = sb(8192, r2).rearrange("p (f t) -> p f t", f=32)
    assert r2 + 8192 <= MEM_COLS
    ss, sd, rs = small[:, 0:16], small[:, 16:32], small[:, 32:48]
    mx, neg, se, scl = (small[:, 64 + 16 * i:80 + 16 * i].rearrange("p (h t) -> p h t", h=8) for i in range(4))
    stats = small[:, 128:140].rearrange("p (t n) -> p t n", t=TT)
    aggr = small[:, 140:144].rearrange("p (t n) -> p t n", t=TT)
    css, csd, crs = small[:, 144:148], small[:, 148:152], small[:, 152:156]
    cmx, cse, cgs = small[:, 160:176], small[:, 176:192], small[:, 192:208]
    lsd, lrs = small[:, 208:210], small[:, 210:212]
    nss, nsd, nrs = small[:, 216:218], small[:, 218:220], small[:, 220:222]

    act_ring = PsumRing(psum[:, 0:4, :], sem("act_bank_full"), sem("act_bank_free"), SECTIONS_ACT)
    dve_ring = PsumRing(psum[:, 4:8, :], sem("dve_bank_full"), sem("dve_bank_free"), SECTIONS_DVE)
    weights = WeightRing(slots, [sem(f"weights_landed{s}") for s in range(SLOTS)], sem("weights_used"))
    pe_step, act_step, dve_step = sem("pe_step"), sem("act_step"), sem("dve_step")
    const_landed, vec_landed, x_landed = sem("const_landed"), sem("vec_landed"), sem("x_landed")
    layer_done = signal("layer_done")
    sumsq_ready = signal("sumsq_ready", 2)
    root_ready = signal("root_ready", 2)
    xn_ready = signal("xn_ready", 2)
    hT_by_act, hT_by_dve = signal("hT_by_act", 2), signal("hT_by_dve", 2)
    glu_gate_ready = signal("glu_gate_ready")
    latent_root_ready = signal("latent_root_ready")
    latent_ready = signal("latent_ready")
    latentT_ready = signal("latentT_ready")
    qm_copied = signal("qm_copied")
    vm_ready = signal("vm_ready")
    kvn_copied = signal("kvn_copied")
    qn_copied = signal("qn_copied")
    gates_ready = signal("gates_ready")
    conv_ready = signal("conv_ready")
    ln_var_ready, ln_root_ready = signal("ln_var_ready"), signal("ln_root_ready")
    conv_normed = signal("conv_normed")
    conv_silu_parts = signal("conv_silu_parts")
    conv_act_ready = signal("conv_act_ready")
    head_sumsq_ready, head_root_ready = signal("head_sumsq_ready", 5), signal("head_root_ready", 5)
    heads_ready = signal("heads_ready", 5)
    qkT_ready = signal("qkT_ready", 2)
    score_max_ready = signal("score_max_ready", 6)
    exp_ready = signal("exp_ready", 6)
    probs_ready = signal("probs_ready", 6)
    probsT_ready = signal("probsT_ready", 6)
    mla_out_ready = signal("mla_out_ready")
    blocks_copied = signal("blocks_copied")
    blocks_ready = signal("blocks_ready")
    hidden_parts_ready = signal("hidden_parts_ready")
    hidden_ready = signal("hidden_ready")
    kcmpT_ready = signal("kcmpT_ready")
    vcmp_ready = signal("vcmp_ready")
    cmp_shifted_ready, cmp_exp_ready = signal("cmp_shifted_ready"), signal("cmp_exp_ready")
    cmp_probs_ready, cmp_probsT_ready = signal("cmp_probs_ready"), signal("cmp_probsT_ready")
    nsa_out_ready = signal("nsa_out_ready")
    merge_gate_ready = signal("merge_gate_ready", 3)
    merge_gate_used = signal("merge_gate_used", 3)
    merged_ready = signal("merged_ready")
    relu_ready = signal("relu_ready", 16)
    ff_ready = signal("ff_ready", 16)
    stored = sem("stored")
    const2_landed = sem("const2_landed")

    first_block = ExitStack()
    block = first_block.enter_context(nc.Block())
    ITEM = {name: i for i, (name, _) in enumerate(ITEMS1)}
    N1 = len(ITEMS1)
    w1_off, _ = offsets(ITEMS1)

    @block.sync
    def _(sp):
        sp.dma_start(con, K1).then_inc(const_landed, 16)
        sp.dma_start(x, xin.rearrange("(t p) n -> p t n", p=P)).then_inc(x_landed, 16)
        sp.dma_start(con2, K2).then_inc(const2_landed, 16)
        sp.dma_start(vec2, VV2).then_inc(const2_landed, 16)
        with sp.Fori(0, LAYERS) as l:
            for n, (name, count) in enumerate(ITEMS1):
                if not count:
                    continue
                sp.wait_ge(weights.used, l * N1 + n + 2)
                sp.dma_start(weights.view(n, count), W1[l, :, w1_off[name]:w1_off[name] + count]).then_inc(
                    weights.landed[n % SLOTS], 16)

    @block.tensor
    def _(pe):
        pe.sem_inc(weights.used, SLOTS)

        def stand():
            pe.sem_inc(pe_step, 1)

        item_now = {}

        def item(l, name):
            n = ITEM[name]
            loads = sum(1 for m in range(n % SLOTS, N1, SLOTS) if ITEMS1[m][1])
            pe.wait_ge(weights.landed[n % SLOTS], (l * loads + weights.loads_before(n)) * 16)
            stand()
            item_now["fresh"] = True
            return weights.view(n, ITEMS1[n][1])

        def mm(out, lhsT, rhs, start, stop, skip=False):
            ins = pe.matmul(out, lhsT, rhs, start=start, stop=stop, skip_group_check=skip)
            if item_now.get("fresh"):
                item_now["fresh"] = False
                assert not stop
                ins.then_inc(weights.used, 1)
            return ins

        def open_(ring, l, tag):
            b = ring.open(pe, l, tag)
            stand()
            return b

        def transposes(ring, l, tag, blocks, rows_=P):
            b = open_(ring, l, tag)
            at = 0
            for src in blocks:
                n = src.shape[0]
                last = pe.transpose(b[0:rows_, at:at + n], src, ident[0:n, 0:n])
                at += n
            last.then_inc(ring.full, 1)

        def normed_transposes(l, i):
            pe.wait_ge(*xn_ready.at(l, i))
            for pair in range(4):
                ring = (act_ring, dve_ring)[pair % 2]
                transposes(ring, l, f"hT{pair}", [xn[:, t, (2 * pair + c) * P:(2 * pair + c + 1) * P]
                                                  for c in range(2) for t in range(TT)])

        def token_major(ring, l, tag, srcT, w, kchunks, n0, n1):
            for t in range(TT):
                b = open_(ring, l, tag)
                for k in range(kchunks):
                    last = mm(b[:, 0:n1 - n0], srcT[:, k, t * P:(t + 1) * P], w[:, k, n0:n1], k == 0, k == kchunks - 1)
                last.then_inc(ring.full, 1)

        def channel_major(ring, l, tag, srcT, w, kchunks, chunks):
            for c in range(0, chunks, 2):
                b = open_(ring, l, tag)
                for j in range(2):
                    for k in range(kchunks):
                        last = mm(b[:, j * T:(j + 1) * T], w[:, k, (c + j) * P:(c + j + 1) * P], srcT[:, k, :],
                                  k == 0, k == kchunks - 1)
                last.then_inc(ring.full, 1)

        def attend(l, r, q, k, v, d):
            for h in range(8):
                b = open_(dve_ring, l, f"S{r}")
                mm(b[:, 0:P], q(h)[0:d, 0:P], k(h)[0:d, 0:P], True, True)
                mm(b[:, P:3 * P], q(h)[0:d, P:T], k(h)[0:d, :], True, True).then_inc(dve_ring.full, 1)
            for half in range(2):
                pe.wait_ge(*probs_ready.at(l, 2 * r + half))
                for part in range(3):
                    transposes(act_ring, l, f"PT{r}", [
                        S[:, half * 4 + (part * 4 + j) // 3, ((part * 4 + j) % 3) * P:((part * 4 + j) % 3 + 1) * P]
                        for j in range(4)])
            ring = act_ring if r == 0 else dve_ring
            for half in range(2):
                pe.wait_ge(*probsT_ready.at(l, 2 * r + half))
                b = open_(ring, l, f"PV{r}")
                for pair in range(2):
                    for e in range(2):
                        h = half * 4 + pair * 2 + e
                        o = b[64 * e:64 * e + 64, pair * T:(pair + 1) * T]
                        mm(o, v(h, 0), PT[:, h, 0:T], True, False, skip=True)
                        last = mm(o[:, P:T], v(h, 1), PT[:, h, T:T + P], False, True, skip=True)
                last.then_inc(ring.full, 1)

        pe.wait_ge(const_landed, 16)
        with pe.Fori(0, LAYERS) as l:
            normed_transposes(l, 0)
            pe.wait_ge(*hT_by_act.at(l, 0))
            pe.wait_ge(*hT_by_dve.at(l, 0))
            channel_major(act_ring, l, "u_gate", hT, km_view(item(l, "u_gate"), 512), 8, 4)
            channel_major(dve_ring, l, "u_a", hT, km_view(item(l, "u_a"), 512), 8, 4)
            token_major(act_ring, l, "cq", hT, km_view(item(l, "cq"), 384), 8, 0, 384)
            w = item(l, "ckv_uq")
            token_major(act_ring, l, "ckv", hT, km_view(w[:, 0:2304], 288), 8, 0, 288)
            pe.wait_ge(*latent_ready.at(l))
            blocks = [cq[:, t, c * P:(c + 1) * P] for c in range(3) for t in range(TT)]
            blocks += [ckvr[:, t, c * P:(c + 1) * P] for c in range(2) for t in range(TT)]
            for i in range(0, 10, 4):
                transposes(act_ring, l, "latentT", blocks[i:i + 4])
            pe.wait_ge(*latentT_ready.at(l))
            wq = km_view(w[:, 2304:4608], 768)
            for n0 in (0, 384):
                token_major(act_ring, l, "qm", cqT, wq, 3, n0, n0 + 384)
            w = item(l, "ukv_kvn2")
            for n0 in (0, 512):
                token_major(dve_ring, l, "kvm", ckvT, km_view(w[:, 0:2048], 1024), 2, n0, n0 + 512)
            token_major(act_ring, l, "kvn2", hT, km_view(w[:, 2048:4288], 280), 8, 0, 280)
            token_major(act_ring, l, "qn", hT, km_view(item(l, "qn"), 512), 8, 0, 512)
            token_major(act_ring, l, "kvn1", hT, km_view(item(l, "kvn1"), 512), 8, 0, 512)

            pe.wait_ge(*heads_ready.at(l, 0))
            for h in range(0, 8, 2):
                transposes(act_ring, l, "qmT", [qm[:, t, h + j, :] for j in range(2) for t in range(TT)], MQK)
            pe.wait_ge(*heads_ready.at(l, 1))
            for h in range(0, 8, 2):
                transposes(act_ring, l, "kmT", [kf[:, t, h + j, :] for j in range(2) for t in range(TT)], MQK)
            pe.wait_ge(*qkT_ready.at(l, 0))
            pe.wait_ge(*vm_ready.at(l))
            attend(l, 0, lambda h: qT[:, h, :], lambda h: kT[:, h, :], lambda h, t: vm[:, t, h, :], MQK)

            pe.wait_ge(*kvn_copied.at(l))
            transposes(act_ring, l, "kcT", [kvn[:, t, g * P:(g + 1) * P] for g in range(NG) for t in range(TT)])
            w = km_view(item(l, "cmp"), P)
            pe.wait_ge(*blocks_ready.at(l))
            for s in range(2):
                b = open_(act_ring, l, "hid")
                for j in range(32):
                    last = mm(b[:, 0:30], w[64 * s:64 * s + 64, j, :],
                              blk[64 * s:64 * s + 64, j, :, :].rearrange("p g c -> p (g c)"), j == 0, j == 31)
                last.then_inc(act_ring.full, 1)
            pe.wait_ge(*hidden_ready.at(l))
            b = open_(dve_ring, l, "kvcmp")
            mm(b[0:30, 0:64], hid[:, 120:150], V["k2"], True, True)
            for g in range(NG):
                for j in range(4):
                    last = mm(b[32 * j:32 * j + NCMP, 64 + 64 * g:128 + 64 * g],
                              hid[:, 150 + NCMP * g:150 + NCMP * (g + 1)], V["v2"], True, True)
            last.then_inc(dve_ring.full, 1)
            pe.wait_ge(*heads_ready.at(l, 2))
            for s in range(2):
                transposes(act_ring, l, "nkT", [nk[:, s, t, g, :] for g in range(NG) for t in range(TT)], 64)
            pe.wait_ge(*heads_ready.at(l, 3))
            for h in range(0, 8, 2):
                transposes(act_ring, l, "qnT", [qn[:, t, h + j, :] for j in range(2) for t in range(TT)], 64)
            pe.wait_ge(*heads_ready.at(l, 4))
            transposes(act_ring, l, "kcmpT", [kc[0:30, :]], 64)
            pe.wait_ge(*kcmpT_ready.at(l))
            b = open_(dve_ring, l, "Scmp")
            for t in range(TT):
                for h in range(8):
                    g = h // 4
                    last = mm(b[:, t * T + h * 32:t * T + h * 32 + NCMP], qnT[0:64, h, t * P:(t + 1) * P],
                              kcmpT[0:64, g * NCMP:(g + 1) * NCMP], True, True)
            last.then_inc(dve_ring.full, 1)
            pe.wait_ge(*cmp_probs_ready.at(l))
            transposes(act_ring, l, "PTcmp", [pcmp[:, t, 4 * g:4 * g + 4, :].rearrange("p h n -> p (h n)")
                                              for g in range(NG) for t in range(TT)])
            pe.wait_ge(*cmp_probsT_ready.at(l))
            pe.wait_ge(*vcmp_ready.at(l))
            for g in range(NG):
                b = open_(dve_ring, l, "PVcmp")
                for j in range(2):
                    last = mm(b[:, j * T:(j + 1) * T], vbd[:, 2 * g + j, :], pcT[:, g, :], True, True)
                last.then_inc(dve_ring.full, 1)
            pe.wait_ge(*qkT_ready.at(l, 1))
            for r in (1, 2):
                c0 = 384 + 256 * (r - 1)
                attend(l, r, lambda h: qnT[:, h, :], lambda h: nkT[:, r - 1, h // 4, :],
                       lambda h, t: kvn[:, t, c0 + 64 * (h // 4):c0 + 64 * (h // 4) + 64], 64)

            for m, (name, ready, src) in enumerate((("A", mla_out_ready, oTm), ("C", nsa_out_ready, oTn),
                                                    ("B", conv_act_ready, cvT))):
                for half in range(2):
                    channel_major(act_ring, l, "gate", hT, km_view(item(l, f"{name}g{half}"), 512), 8, 4)
                if name == "B":
                    pe.wait_ge(*conv_ready.at(l))
                    for t in range(TT):
                        transposes(dve_ring, l, "conv", [cacc[:, c, t * P:(t + 1) * P] for c in range(4)])
                    pe.wait_ge(*conv_normed.at(l))
                    yn = cacc.rearrange("p c t -> p (c t)").rearrange("p (t n) -> p t n", t=TT)
                    for c in range(0, 4, 2):
                        transposes(act_ring, l, "convT", [yn[:, t, (c + j) * P:(c + j + 1) * P] for j in range(2) for t in range(TT)])
                pe.wait_ge(*ready.at(l))
                channel_major(dve_ring, l, "mix", src, km_view(item(l, f"{name}o"), D), 4, 8)
            pe.wait_ge(*merged_ready.at(l))
            for half in range(2):
                token_major(dve_ring, l, "out", mg, km_view(item(l, f"out{half}"), 512), 8, 0, 512)

            normed_transposes(l, 1)
            pe.wait_ge(*hT_by_act.at(l, 1))
            pe.wait_ge(*hT_by_dve.at(l, 1))
            for i in range(8):
                channel_major(act_ring, l, "ff1", hT, km_view(item(l, f"ff1_{i}"), 512), 8, 4)
            banks = []
            for i in range(8):
                w = km_view(item(l, f"ff2_{i}"), D)
                pe.wait_ge(*ff_ready.at(l, 2 * i + 1))
                for k in range(4):
                    for t in range(TT):
                        for half in range(2):
                            if i == 0 and k == 0:
                                banks.append(open_(dve_ring, l, "ff2"))
                            last = mm(banks[2 * t + half], fT[:, 4 * i + k, t * P:(t + 1) * P],
                                      w[:, k, half * 512:(half + 1) * 512], i + k == 0, i == 7 and k == 3)
                            if i == 7 and k == 3:
                                last.then_inc(dve_ring.full, 1)
            pe.drain().then_inc(weights.used, 1)
            while len(act_ring.filled["layers"]) % 4:
                open_(act_ring, l, "pad")
                pe.drain().then_inc(act_ring.full, 1)
        assert len(act_ring.filled["layers"]) == 92 and len(dve_ring.filled["layers"]) == 64

    @block.scalar
    def _(act):
        act.sem_inc(act_ring.free, 4)
        A = act.activation

        def normed_evac(l, i, gain):
            for pair in range(0, 4, 2):
                b = act_ring.take(act, l, f"hT{pair}")
                for c in range(2):
                    last = A(hT[:, 2 * pair + c, :], b[:, c * T:(c + 1) * T], ACT.Copy, scale=gain[:, 2 * pair + c:2 * pair + c + 1])
                last.then_inc(act_ring.free, 1)
                act.drain()
            act.sem_inc(hT_by_act.sem, 1)

        def roots(l, i):
            act.wait_ge(*sumsq_ready.at(l, i))
            A(nsd, nss, ACT.Sqrt, bias=C["eps"], scale=1.0 / D).then_inc(root_ready.sem, 1)

        def head_roots(l, i, rows_, n, d):
            act.wait_ge(*head_sumsq_ready.at(l, i))
            A(sd[0:rows_, 0:n], ss[0:rows_, 0:n], ACT.Sqrt, bias=C["eps"][0:rows_, :], scale=1.0 / d).then_inc(head_root_ready.sem, 1)

        def copy_bank(l, tag, dst, src=None, func=ACT.Copy):
            b = act_ring.take(act, l, tag)
            return A(dst, src(b) if src else b, func).then_inc(act_ring.free, 1)

        def attend(l, r, scale):
            for half in range(2):
                act.wait_ge(*score_max_ready.at(l, 2 * r + half))
                for h in range(4 * half, 4 * half + 4):
                    A(S[:, h, 0:P], S[:, h, 0:P], ACT.Exp, bias=neg[:, h, 0:1], accum_out=se[:, h, 0:1])
                    last = A(S[:, h, P:3 * P], S[:, h, P:3 * P], ACT.Exp, bias=neg[:, h, 1:2], accum_out=se[:, h, 1:2])
                last.then_inc(exp_ready.sem, 1)
            for half in range(2):
                for part in range(3):
                    f = PT[:, 4 * half:4 * half + 4, :].rearrange("p h n -> p (h n)")
                    copy_bank(l, f"PT{r}", f[:, part * 512:(part + 1) * 512])
                act.drain().then_inc(probsT_ready.sem, 1)
            if r == 0:
                for half in range(2):
                    copy_bank(l, "PV0", oTm[:, 2 * half:2 * half + 2, :], lambda b: b.rearrange("p (c t) -> p c t", c=2))
                act.drain().then_inc(mla_out_ready.sem, 1)

        with act.Fori(0, LAYERS) as l:
            act.wait_ge(const_landed, 16)
            roots(l, 0)
            act.wait_ge(vec_landed, l * 16 + 16)
            normed_evac(l, 0, V["g_mix"])
            for c in range(0, 4, 2):
                b = act_ring.take(act, l, "u_gate")
                for j in range(2):
                    last = A(sg[:, c + j, :], b[:, j * T:(j + 1) * T], ACT.Sigmoid, bias=V["b_glu"][:, 4 + c + j:5 + c + j])
                last.then_inc(act_ring.free, 1)
            act.drain().then_inc(glu_gate_ready.sem, 1)
            for t in range(TT):
                b = act_ring.take(act, l, "cq")
                A(cq[:, t, :], b[:, 0:384], ACT.Copy)
                A(junk[:, 0:384], b[:, 0:384], ACT.Square, accum_out=css[:, t:t + 1]).then_inc(act_ring.free, 1)
                act.drain()
            for t in range(TT):
                b = act_ring.take(act, l, "ckv")
                A(ckvr[:, t, :], b[:, 0:288], ACT.Copy)
                A(junk[:, 0:256], b[:, 0:256], ACT.Square, accum_out=css[:, 2 + t:3 + t]).then_inc(act_ring.free, 1)
                act.drain()
            A(csd[:, 0:2], css[:, 0:2], ACT.Sqrt, bias=C["eps"], scale=1.0 / 384)
            A(csd[:, 2:4], css[:, 2:4], ACT.Sqrt, bias=C["eps"], scale=1.0 / 256).then_inc(latent_root_ready.sem, 1)
            for i in range(3):
                b = act_ring.take(act, l, "latentT")
                for j in range(2 if i < 2 else 1):
                    c = 2 * i + j
                    dst = cqT[:, c, :] if c < 3 else ckvT[:, c - 3, :]
                    gain = V["g_cq"][:, c:c + 1] if c < 3 else V["g_ckv"][:, c - 3:c - 2]
                    last = A(dst, b[:, j * T:(j + 1) * T], ACT.Copy, scale=gain)
                last.then_inc(act_ring.free, 1)
            act.drain().then_inc(latentT_ready.sem, 1)
            qf = qm.rearrange("p t h n -> p t (h n)")
            for half in range(2):
                for t in range(TT):
                    copy_bank(l, "qm", qf[:, t, half * 384:(half + 1) * 384], lambda b: b[:, 0:384])
            act.drain().then_inc(qm_copied.sem, 1)
            for t in range(TT):
                copy_bank(l, "kvn2", kvn[:, t, 512:792], lambda b: b[:, 0:280])
            for t in range(TT):
                copy_bank(l, "qn", qn[:, t, :, :].rearrange("p h n -> p (h n)"))
            act.drain().then_inc(qn_copied.sem, 1)
            for t in range(TT):
                copy_bank(l, "kvn1", kvn[:, t, 0:512])
            act.drain().then_inc(kvn_copied.sem, 1)
            A(gates.rearrange("p (t n) -> p t n", t=TT), kvn[:, :, 768:792], ACT.Sigmoid).then_inc(gates_ready.sem, 1)
            head_roots(l, 0, P, 16, MQK)
            head_roots(l, 1, P, 16, MQK)
            for dst, tag in ((qT, "qmT"), (kT, "kmT")):
                for h in range(0, 8, 2):
                    copy_bank(l, tag, dst[0:MQK, h:h + 2, :], lambda b: b[0:MQK, :].rearrange("p (h t) -> p h t", h=2))
            act.drain().then_inc(qkT_ready.sem, 1)
            attend(l, 0, 1.0)
            copy_bank(l, "kcT", kcT, lambda b: b.rearrange("p (g t) -> p g t", g=NG))
            act.drain().then_inc(blocks_copied.sem, 1)
            for s in range(2):
                b = act_ring.take(act, l, "hid")
                A(hid[:, 30 * s:30 * s + 30], b[:, 0:30], ACT.Copy)
                A(hid[:, 60 + 30 * s:90 + 30 * s], b[:, 0:30], ACT.Sigmoid).then_inc(act_ring.free, 1)
            act.drain().then_inc(hidden_parts_ready.sem, 1)
            head_roots(l, 2, P, 8, 64)
            head_roots(l, 3, P, 16, 64)
            for s in range(2):
                copy_bank(l, "nkT", nkT[0:64, s, :, :], lambda b: b[0:64, :].rearrange("p (g t) -> p g t", g=NG))
            for h in range(0, 8, 2):
                copy_bank(l, "qnT", qnT[0:64, h:h + 2, :], lambda b: b[0:64, :].rearrange("p (h t) -> p h t", h=2))
            act.drain().then_inc(qkT_ready.sem, 1)
            head_roots(l, 4, 30, 1, 64)
            copy_bank(l, "kcmpT", kcmpT[0:64, :], lambda b: b[0:64, 0:30])
            act.drain().then_inc(kcmpT_ready.sem, 1)
            act.wait_ge(*cmp_shifted_ready.at(l))
            A(pcmp[:, :, :, 0:NCMP].rearrange("p t h n -> p (t h) n"), scmp.rearrange("p t h n -> p (t h) n"),
              ACT.Exp, scale=ND ** -0.5).then_inc(cmp_exp_ready.sem, 1)
            copy_bank(l, "PTcmp", pcT, lambda b: b.rearrange("p (g t) -> p g t", g=NG))
            act.drain().then_inc(cmp_probsT_ready.sem, 1)
            attend(l, 1, 1.0)
            attend(l, 2, 1.0)
            for m in range(3):
                if m == 2:
                    act.wait_ge(*merge_gate_used.at(l, 0))
                for c in range(0, 8, 2):
                    copy_bank(l, "gate", gsig[:, m % 2, c:c + 2, :], lambda b: b.rearrange("p (c t) -> p c t", c=2), ACT.Sigmoid)
                act.drain().then_inc(merge_gate_ready.sem, 1)
                if m == 2:
                    act.wait_ge(*ln_var_ready.at(l))
                    A(lsd, aggr[:, :, 1], ACT.Sqrt, bias=C["eps"]).then_inc(ln_root_ready.sem, 1)
                    for c in range(0, 4, 2):
                        b = act_ring.take(act, l, "convT")
                        for j in range(2):
                            k = c + j
                            A(cvT[:, k, :], b[:, j * T:(j + 1) * T], ACT.Identity, bias=V["b_ln"][:, k:k + 1], scale=V["g_ln"][:, k:k + 1])
                            last = A(sg[:, k, :], b[:, j * T:(j + 1) * T], ACT.Sigmoid, bias=V["b_ln"][:, k:k + 1], scale=V["g_ln"][:, k:k + 1])
                        last.then_inc(act_ring.free, 1)
                    act.drain().then_inc(conv_silu_parts.sem, 1)
            roots(l, 1)
            normed_evac(l, 1, V["g_ffn"])
            for i in range(16):
                b = act_ring.take(act, l, "ff1")
                A(fT[:, 2 * i:2 * i + 2, :], b.rearrange("p (c t) -> p c t", c=2), ACT.Relu).then_inc(act_ring.free, 1)
                act.drain().then_inc(relu_ready.sem, 1)
            while len(act_ring.emptied["layers"]) % 4:
                act_ring.take(act, l, "pad")
                act.sem_inc(act_step, 1)
                act.drain().then_inc(act_ring.free, 1)
        act_ring.check("layers")

    @block.vector
    def _(v):
        v.sem_inc(dve_ring.free, 4)
        v.memset(upad, 0.0)
        v.memset(vbd, 0.0)
        v.memset(pcmp, 0.0)
        v.drain()

        def model_norm(l, i):
            for t in range(TT):
                v.tensor_tensor_reduce(xn[:, t, :], x[:, t, :], x[:, t, :], 1.0, 0.0, ALU.mult, ALU.add, nss[:, t:t + 1])
            v.drain().then_inc(sumsq_ready.sem, 1)
            v.wait_ge(*root_ready.at(l, i))
            v.reciprocal(nrs, nsd)
            v.drain()
            for t in range(TT):
                v.tensor_scalar(xn[:, t, :], x[:, t, :], nrs[:, t:t + 1], None, ALU.mult)
            v.drain().then_inc(xn_ready.sem, 1)

        def normed_evac(l, i, gain):
            for pair in range(1, 4, 2):
                b = dve_ring.take(v, l, f"hT{pair}")
                for c in range(2):
                    k = 2 * pair + c
                    last = v.tensor_scalar(hT[:, k, :], b[:, c * T:(c + 1) * T], gain[:, k:k + 1], None, ALU.mult)
                last.then_inc(dve_ring.free, 1)
            v.drain().then_inc(hT_by_dve.sem, 1)

        def head_norm(l, i, y, gain):
            p, n, d = y.shape
            sq = junk[0:p, 0:n * d].rearrange("p (n d) -> p n d", n=n)
            v.tensor_tensor(sq, y, y, ALU.mult)
            v.drain()
            v.tensor_reduce(ss[0:p, 0:n], sq, AX.X, ALU.add).then_inc(head_sumsq_ready.sem, 1)
            v.wait_ge(*head_root_ready.at(l, i))
            v.reciprocal(rs[0:p, 0:n], sd[0:p, 0:n])
            v.drain()
            v.tensor_tensor(y, y, bc(rs[0:p, 0:n], 2, d), ALU.mult)
            v.drain()
            v.tensor_tensor(y, y, bc(gain[0:p, :], 1, n), ALU.mult)
            v.drain()

        def rope(y, cos, sin):
            p, t, n, _ = y.shape
            half = cos.shape[2]
            x1, x2 = y[:, :, :, 0:half], y[:, :, :, half:2 * half]
            k = t * n * half
            a, b, c, d = (junk[0:p, 1536 + i * k:1536 + (i + 1) * k].rearrange("p (t n h) -> p t n h", t=t, n=n) for i in range(4))
            cb, sn = bc(cos, 2, n), bc(sin, 2, n)
            v.tensor_tensor(a, x1, cb, ALU.mult)
            v.tensor_tensor(b, x2, sn, ALU.mult)
            v.tensor_tensor(c, x2, cb, ALU.mult)
            v.tensor_tensor(d, x1, sn, ALU.mult)
            v.drain()
            v.tensor_tensor(x1, a, b, ALU.subtract)
            return v.tensor_tensor(x2, c, d, ALU.add)

        def table(name, t):
            return C[name].rearrange("p (t n) -> p t n", t=t)

        def convolve(chunks):
            for tap in range(CONV_W):
                for c in chunks:
                    w = V["w_dw"][:, c * CONV_W + tap:c * CONV_W + tap + 1]
                    src = upad[:, c, tap:tap + T]
                    if tap == 0:
                        v.tensor_scalar(cacc[:, c, :], src, w, V["b_dw"][:, c:c + 1], ALU.mult, ALU.add)
                    else:
                        v.scalar_tensor_tensor(cacc[:, c, :], src, w, cacc[:, c, :], ALU.mult, ALU.add)
                v.drain()

        def attend(l, r, scale):
            for half in range(2):
                for h in range(4 * half, 4 * half + 4):
                    b = dve_ring.take(v, l, f"S{r}")
                    v.sem_inc(dve_step, 1)
                    v.tensor_tensor_reduce(S[:, h, 0:P], b[:, 0:P], C["cmask"][:, P:T], scale, -3e38, ALU.add, ALU.max, mx[:, h, 0:1])
                    v.tensor_tensor_reduce(S[:, h, P:3 * P], b[:, P:3 * P], C["cmask"], scale, -3e38, ALU.add, ALU.max,
                                           mx[:, h, 1:2]).then_inc(dve_ring.free, 1)
                v.drain()
                v.tensor_scalar(neg[:, 4 * half:4 * half + 4, :], mx[:, 4 * half:4 * half + 4, :], -1.0, None,
                                ALU.mult).then_inc(score_max_ready.sem, 1)
            for half in range(2):
                hs = slice(4 * half, 4 * half + 4)
                v.wait_ge(*exp_ready.at(l, 2 * r + half))
                v.reciprocal(scl[:, hs, :], se[:, hs, :])
                v.drain()
                if r:
                    g = gates.rearrange("p (t h n) -> p h t n", t=TT, h=NH)[:, hs, :, r]
                    v.tensor_tensor(scl[:, hs, :], scl[:, hs, :], g, ALU.mult)
                    v.drain()
                v.tensor_tensor(S[:, hs, 0:P], S[:, hs, 0:P], bc(scl[:, hs, 0], 2, P), ALU.mult)
                v.tensor_tensor(S[:, hs, P:3 * P], S[:, hs, P:3 * P], bc(scl[:, hs, 1], 2, T), ALU.mult).then_inc(probs_ready.sem, 1)
            if r:
                for half in range(2):
                    b = dve_ring.take(v, l, f"PV{r}").rearrange("p (c t) -> p c t", c=2)
                    o = oTn[:, 2 * half:2 * half + 2, :]
                    v.tensor_tensor(o, b, o, ALU.add).then_inc(dve_ring.free, 1)
                v.drain()

        v.wait_ge(x_landed, 16)
        v.wait_ge(const_landed, 16)
        with v.Fori(0, LAYERS) as l:
            model_norm(l, 0)
            v.wait_ge(vec_landed, l * 16 + 16)
            normed_evac(l, 0, V["g_mix"])
            v.wait_ge(*glu_gate_ready.at(l))
            for c in range(0, 4, 2):
                b = dve_ring.take(v, l, "u_a")
                for j in range(2):
                    k = c + j
                    last = v.scalar_tensor_tensor(upad[:, k, CONV_W - 1:], b[:, j * T:(j + 1) * T], V["b_glu"][:, k:k + 1],
                                                  sg[:, k, :], ALU.add, ALU.mult)
                last.then_inc(dve_ring.free, 1)
            v.drain()
            v.wait_ge(*latent_root_ready.at(l))
            v.reciprocal(crs, csd)
            v.drain()
            for t in range(TT):
                v.tensor_scalar(cq[:, t, :], cq[:, t, :], crs[:, t:t + 1], None, ALU.mult)
                v.tensor_scalar(ckvr[:, t, 0:256], ckvr[:, t, 0:256], crs[:, 2 + t:3 + t], None, ALU.mult)
            v.tensor_copy(kf[:, :, :, 0:MROPE], bc(ckvr[:, :, 256:288], 2, MH))
            v.drain().then_inc(latent_ready.sem, 1)
            for half in range(2):
                for t in range(TT):
                    b = dve_ring.take(v, l, "kvm").rearrange("p (h s n) -> p h s n", h=4, s=2)
                    v.tensor_copy(kf[:, t, 4 * half:4 * half + 4, MROPE:MQK], b[:, :, 0, :])
                    v.tensor_copy(vm[:, t, 4 * half:4 * half + 4, :], b[:, :, 1, :]).then_inc(dve_ring.free, 1)
            v.drain().then_inc(vm_ready.sem, 1)
            v.wait_ge(*qm_copied.at(l))
            head_norm(l, 0, qm.rearrange("p t h n -> p (t h) n"), V["g_q_mla"])
            rope(qm, table("mcos", TT), table("msin", TT)).then_inc(heads_ready.sem, 1)
            v.drain()
            head_norm(l, 1, kf.rearrange("p t h n -> p (t h) n"), V["g_k_mla"])
            rope(kf, table("mcos", TT), table("msin", TT)).then_inc(heads_ready.sem, 1)
            v.drain()
            attend(l, 0, MQK ** -0.5)
            v.wait_ge(*blocks_copied.at(l))
            kb = kcT.rearrange("p g (n b) -> p b g n", b=16)
            for a in range(2):
                pe_b = bc(bc(V["pe"][:, 16 * a:16 * a + 16], 2, NG), 3, NCMP)
                v.tensor_tensor(blk[:, 16 * a:16 * a + 16, :, :], kb[:, :, :, a:a + NCMP], pe_b, ALU.add)
            v.drain().then_inc(blocks_ready.sem, 1)
            v.wait_ge(*hidden_parts_ready.at(l))
            v.tensor_tensor(hid[:, 120:180], hid[:, 0:60], hid[:, 60:120], ALU.mult).then_inc(hidden_ready.sem, 1)
            v.wait_ge(*kvn_copied.at(l))
            for s in range(2):
                v.tensor_copy(nk[:, s, :, :, :], kvn[:, :, 256 + 256 * s:384 + 256 * s].rearrange("p t (g n) -> p t g n", g=NG))
            b = dve_ring.take(v, l, "kvcmp")
            v.tensor_copy(kc[0:30, :], b[0:30, 0:64])
            for g in range(NG):
                for j in range(4):
                    last = v.tensor_copy(vbd[32 * j:32 * j + NCMP, 2 * g + j // 2, (j % 2) * 64:(j % 2) * 64 + 64],
                                         b[32 * j:32 * j + NCMP, 64 + 64 * g:128 + 64 * g])
            last.then_inc(dve_ring.free, 1)
            v.drain().then_inc(vcmp_ready.sem, 1)
            head_norm(l, 2, nk.rearrange("p s t g n -> p (s t g) n"), V["g_k_nsa"])
            for s in range(2):
                last = rope(nk[:, s, :, :, :], table("ncos", TT), table("nsin", TT))
                v.drain()
            v.sem_inc(heads_ready.sem, 1)
            v.wait_ge(*qn_copied.at(l))
            head_norm(l, 3, qn.rearrange("p t h n -> p (t h) n"), V["g_q_nsa"])
            rope(qn, table("ncos", TT), table("nsin", TT)).then_inc(heads_ready.sem, 1)
            v.drain()
            head_norm(l, 4, kc[0:30, :].unsqueeze(1), V["g_k_nsa"])
            rope(kc[0:30, :].unsqueeze(1).unsqueeze(1), C["ccos"][0:30, :].unsqueeze(1),
                 C["csin"][0:30, :].unsqueeze(1)).then_inc(heads_ready.sem, 1)
            b = dve_ring.take(v, l, "Scmp").rearrange("p (t h n) -> p t h n", t=TT, h=NH)[:, :, :, 0:NCMP]
            v.tensor_tensor(scmp, b, bc(C["cmpmask"].rearrange("p (t n) -> p t n", t=TT), 2, NH), ALU.add).then_inc(dve_ring.free, 1)
            v.drain()
            s3, p3 = scmp.rearrange("p t h n -> p (t h) n"), pcmp.rearrange("p t h n -> p (t h) n")[:, :, 0:NCMP]
            v.tensor_reduce(cmx, s3, AX.X, ALU.max)
            v.drain()
            v.tensor_scalar(cmx, cmx, NEG * 1e-5, None, ALU.max)
            v.drain()
            v.tensor_tensor(s3, s3, bc(cmx, 2, NCMP), ALU.subtract).then_inc(cmp_shifted_ready.sem, 1)
            v.wait_ge(*cmp_exp_ready.at(l))
            v.tensor_reduce(cse, p3, AX.X, ALU.add)
            v.drain()
            v.tensor_scalar(cse, cse, 1e-30, None, ALU.max)
            v.drain()
            v.reciprocal(cgs, cse)
            v.wait_ge(*gates_ready.at(l))
            v.tensor_copy(cmx, gates.rearrange("p (n k) -> p n k", k=3)[:, :, 0])
            v.drain()
            v.tensor_tensor(cgs, cgs, cmx, ALU.mult)
            v.drain()
            v.tensor_tensor(p3, p3, bc(cgs, 2, NCMP), ALU.mult).then_inc(cmp_probs_ready.sem, 1)
            for g in range(NG):
                b = dve_ring.take(v, l, "PVcmp")
                v.tensor_copy(oTn[:, 2 * g:2 * g + 2, :], b.rearrange("p (c t) -> p c t", c=2)).then_inc(dve_ring.free, 1)
            v.drain()
            attend(l, 1, ND ** -0.5)
            attend(l, 2, ND ** -0.5)
            v.sem_inc(nsa_out_ready.sem, 1)
            for m in range(3):
                if m < 2:
                    convolve((2 * m, 2 * m + 1))
                else:
                    v.drain().then_inc(conv_ready.sem, 1)
                    yn = cacc.rearrange("p c t -> p (c t)").rearrange("p (t n) -> p t n", t=TT)
                    b2 = [dve_ring.take(v, l, "conv") for _ in range(TT)]
                    for t in range(TT):
                        v.bn_stats(stats[:, t, :], b2[t])
                    v.drain()
                    for t in range(TT):
                        v.bn_aggr(aggr[:, t, :], stats[:, t, :])
                    v.drain().then_inc(ln_var_ready.sem, 1)
                    v.wait_ge(*ln_root_ready.at(l))
                    v.reciprocal(lrs, lsd)
                    v.drain()
                    for t in range(TT):
                        v.tensor_scalar(yn[:, t, :], b2[t], aggr[:, t, 0:1], lrs[:, t:t + 1], ALU.subtract, ALU.mult).then_inc(dve_ring.free, 1)
                    v.drain().then_inc(conv_normed.sem, 1)
                    v.wait_ge(*conv_silu_parts.at(l))
                    v.tensor_tensor(cvT, cvT, sg, ALU.mult).then_inc(conv_act_ready.sem, 1)
                v.wait_ge(*merge_gate_ready.at(l, m))
                for c in range(0, 8, 2):
                    b = dve_ring.take(v, l, "mix").rearrange("p (c t) -> p c t", c=2)
                    g, o = gsig[:, m % 2, c:c + 2, :], mg[:, c:c + 2, :]
                    if m == 0:
                        v.tensor_tensor(o, b, g, ALU.mult).then_inc(dve_ring.free, 1)
                    elif m == 2:
                        for j in range(2):
                            last = v.scalar_tensor_tensor(g[:, j, :], b[:, j, :], V["b_co"][:, c + j:c + j + 1], g[:, j, :], ALU.add, ALU.mult)
                        last.then_inc(dve_ring.free, 1)
                    else:
                        v.tensor_tensor(g, b, g, ALU.mult).then_inc(dve_ring.free, 1)
                v.drain()
                if m:
                    for c in range(0, 8, 2):
                        v.tensor_tensor(mg[:, c:c + 2, :], mg[:, c:c + 2, :], gsig[:, m % 2, c:c + 2, :], ALU.add)
                    v.drain()
                v.sem_inc(merge_gate_used.sem, 1)
            v.sem_inc(merged_ready.sem, 1)
            for half in range(2):
                for t in range(TT):
                    xs = x[:, t, half * 512:(half + 1) * 512]
                    v.tensor_tensor(xs, dve_ring.take(v, l, "out"), xs, ALU.add).then_inc(dve_ring.free, 1)
            v.drain()
            model_norm(l, 1)
            normed_evac(l, 1, V["g_ffn"])
            for i in range(16):
                v.wait_ge(*relu_ready.at(l, i))
                f = fT[:, 2 * i:2 * i + 2, :]
                v.tensor_tensor(f, f, f, ALU.mult).then_inc(ff_ready.sem, 1)
            for t in range(TT):
                for half in range(2):
                    xs = x[:, t, half * 512:(half + 1) * 512]
                    v.tensor_tensor(xs, dve_ring.take(v, l, "ff2"), xs, ALU.add).then_inc(dve_ring.free, 1)
            v.drain().then_inc(layer_done.sem, 1)
        dve_ring.check("layers")

    @block.gpsimd
    def _(pool):
        for l in range(LAYERS):
            if l:
                pool.wait_ge(*layer_done.at(l - 1))
            pool.dma_start(vec, V1[l]).then_inc(vec_landed, 16)

    first_block.close()

    top = [base]

    def sb2(n, at=None):
        if at is None:
            at = top[0]
            top[0] += n
        return mem[:, at:at + n]

    sb2(2560)
    hcT = sb2(2048).rearrange("p (c t) -> p c t", c=DC)
    rows2 = sb2(2048).rearrange("p (m n) -> p m n", m=2)
    oaxT = sb2(2048).rearrange("p (c t) -> p c t", c=DC)
    modT = sb2(64).rearrange("p (m c s) -> p m c s", m=4, c=DC)
    AB = sb2(48).rearrange("p (k c) -> p k c", k=6)
    sm2 = sb2(224)
    free2 = top[0]
    ctxs = sb2(2048).rearrange("p (t n) -> p t n", t=TT)
    q2 = sb2(2048).rearrange("p (t n) -> p t n", t=TT)
    k2 = sb2(4096).rearrange("p (t n) -> p t n", t=4)
    v2 = sb2(4096).rearrange("p (t n) -> p t n", t=4)
    mod_rows = v2.rearrange("p t n -> p (t n)")
    qT2 = sb2(2048).rearrange("p (h t) -> p h t", h=8)
    kT2 = sb2(4096).rearrange("p (h t) -> p h t", h=8)
    o2 = sb2(2048).rearrange("p (t n) -> p t n", t=TT)
    PT2 = sb2(2048).rearrange("p (h n) -> p h n", h=4)
    S_junk = sb2(1024, top[0] - 1024)
    S2 = sb2(4096, free2).rearrange("p (h m n) -> p h m n", h=4, m=2)
    assert top[0] <= MEM_COLS, top[0]
    csb = sb2(1024, free2 + 4096).rearrange("p (k n) -> p k n", k=8)
    cs = sm2[:, 0:16].rearrange("p (k s) -> p k s", s=2)
    csig = sm2[:, 16:32].rearrange("p (k s) -> p k s", s=2)
    ss2, sd2, rs2 = sm2[:, 32:48], sm2[:, 48:64], sm2[:, 64:80]
    mx2, se2, sc2 = (sm2[:, 80 + 8 * i:88 + 8 * i].rearrange("p (h m) -> p h m", m=2) for i in range(3))
    lam2, nlam = sm2[:, 104:106], sm2[:, 106:107]
    css2, csd2, crs2 = sm2[:, 108:110], sm2[:, 110:112], sm2[:, 112:114]
    ys, yd, yr = sm2[:, 120:152], sm2[:, 152:184], sm2[:, 184:216]

    HALF = 512
    rtop = [free2]

    def rb(n):
        at = rtop[0]
        rtop[0] += n
        return mem[:, at:at + n]

    zr = rb(8 * T).rearrange("p (c t) -> p c t", c=8)
    zs = rb(18 * HALF).rearrange("p (c t) -> p c t", c=18)
    zk, zv, zwa, zg = zs[:, 0:8, :], zs[:, 8:16, :], zs[:, 16, :], zs[:, 17, T:2 * T]
    kk = sb2(8 * HALF, base).rearrange("p (c t) -> p c t", c=8)
    restart = sb2(512, base + 8 * HALF)
    yb = rb(8 * T).rearrange("p (c t) -> p c t", c=8)
    lora = rb(2048)
    Wc, Wnext = rb(16), rb(16)
    lor = rb(256).rearrange("p (d s t) -> p d s t", d=2, s=2)
    zraw = sb2(1024, base).rearrange("p (b t) -> p b t", b=2)
    slots_at = 2 * TT * D
    Z = [sb2(1024, slots_at + 1024 * i) for i in range(14)] + [sb2(1024, 1024 * i) for i in range(2)] + [rb(1024) for _ in range(7)]
    assert slots_at + 14 * 1024 <= base - nv2 - ncon2 - ncon and rtop[0] <= MEM_COLS, rtop[0]
    r0, r1, r2, r3, P0, P1, R0, R1, L0, L1, E0, E1, Dm, DTm, VT0, VT1, Kt, Qt, Apk, Ark, Arq, LT, St = Z
    SIG2 = sb2(2048, slots_at)
    Z_sq = sb2(4096, slots_at).rearrange("p (c t) -> p c t", c=8)
    Pm, Rm, VT_TOK = (P0, P1), (R0, R1), (VT0, VT1)
    Qm, Km, Vt = E0, E1, r3
    Loff, ARm = (L0, L1), (E0, E1)
    U0, nU = (L0, L1), (LT, Dm)

    even_odd = C2["heads"]

    def shift_out(c):
        if c < 8:
            return zr[:, c, :], T
        return (zg, T) if c == 25 else (zs[:, c - 8, :], HALF)

    def ch(ap):
        return ap.rearrange("p (c n) -> p c n", c=16)

    def ch2(ap):
        return ap.rearrange("p (d c n) -> p d c n", d=2, c=8)

    gsig2 = sb2(2048, rtop[0] - 4096).rearrange("p (c t) -> p c t", c=DC)
    mg2 = sb2(2048, free2 + 2048).rearrange("p (c t) -> p c t", c=DC)
    obx = sb2(2048, base).rearrange("p (c t) -> p c t", c=DC)
    rtmp = sb2(2048, base + 2048).rearrange("p (c t) -> p c t", c=DC)
    BON = sb2(2048, rtop[0] - 2048).rearrange("p (c t) -> p c t", c=DC)
    ptop = [free2]

    def pb(n):
        at = ptop[0]
        ptop[0] += n
        return mem[:, at:at + n]

    h2 = sb2(2048, base + 2560 + 4096).rearrange("p (t n) -> p t n", t=TT)
    acc = sb2(2048, base + 2560).rearrange("p (t n) -> p t n", t=TT)
    qTp = pb(4096).rearrange("p (c t) -> p c t", c=16)
    sp_ = pb(4096).rearrange("p (t c n) -> p t c n", t=TT, c=16)
    keysT = pb(2048).rearrange("p (c n) -> p c n", c=16)
    sv = pb(512).rearrange("p (t c n) -> p t c n", t=TT, c=16)
    siu = pb(512)
    sif = pb(512).rearrange("p (t c n) -> p t c n", t=TT, c=16)
    cand = sb2(2048, slots_at + 9216).rearrange("p (h n) -> p h n", h=8)
    eqb = sb2(2048, slots_at + 11264)
    tops = pb(256).rearrange("p (t h n) -> p t h n", t=TT, h=8)
    posu, hiu, lou, eidx = (pb(256) for _ in range(4))
    hif, lof, i1f, i2f = (pb(128) for _ in range(4))
    gatep = pb(256).rearrange("p (t h n) -> p t h n", t=TT, h=8)
    actp, g1, g2 = (pb(256) for _ in range(3))
    idx8 = pb(16)
    dot8 = pb(16)
    wt8 = pb(16)
    gmx, gsm, grc = (pb(16) for _ in range(3))
    GB = 8
    gat = sb2(GB * D, slots_at).rearrange("p (b n) -> p b n", b=GB)
    assert ptop[0] <= MEM_COLS, ptop[0]
    siu_u = siu.bitcast(U32).rearrange("p (t c n) -> p t c n", t=TT, c=16)
    posu_u = posu.bitcast(U32).rearrange("p (t h n) -> p t h n", t=TT, h=8)
    hiu_u, lou_u, eidx_u, idx8_u = hiu.bitcast(U32), lou.bitcast(U32), eidx.bitcast(U32), idx8.bitcast(U32)

    w2_off, w2_total = offsets(ITEMS2)
    ITEM2 = {name: i for i, (name, _) in enumerate(ITEMS2)}
    N2 = len(ITEMS2)
    LAST_BEFORE_SCAN = ITEM2["rw6"]
    landed0 = [LAYERS * sum(1 for m in range(s, len(ITEMS1), SLOTS) if ITEMS1[m][1]) for s in range(SLOTS)]
    used0 = LAYERS * len(ITEMS1)
    DECAY = -float(np.exp(np.float32(-0.5)))

    rows_landed, ctx_landed, lora_landed, keys_landed = sem("rows_landed"), sem("ctx_landed"), sem("lora_landed"), sem("keys_landed")
    cond_sig_ready, cond_ready = signal("cond_sig_ready"), signal("cond_ready")
    mod_rows_ready, mod_ready = signal("mod_rows_ready"), signal("mod_ready")
    sumsq2_ready, root2_ready, xn2_ready = signal("sumsq2_ready"), signal("root2_ready"), signal("xn2_ready")
    hT2_by_act, hT2_by_dve = signal("hT2_by_act"), signal("hT2_by_dve")
    qk2_copied = signal("qk2_copied")
    head2_sumsq_ready, head2_root_ready = signal("head2_sumsq_ready"), signal("head2_root_ready")
    qk2_ready, qkT2_ready = signal("qk2_ready"), signal("qkT2_ready")
    v2_copied = signal("v2_copied")
    lam_parts_ready, lam_exp_ready = signal("lam_parts_ready"), signal("lam_exp_ready")
    diff_max_ready, diff_exp_ready, diff_probs_ready, diff_probsT_ready = (
        signal("diff_max_ready"), signal("diff_exp_ready"), signal("diff_probs_ready"), signal("diff_probsT_ready"))
    diff_out_copied, diff_out_ready, oaxT_ready = signal("diff_out_copied"), signal("diff_out_ready"), signal("oaxT_ready")
    shift_parts_ready, shift_parts_used = signal("shift_parts_ready"), signal("shift_parts_used")
    shifted_ready, lora_act_ready = signal("shifted_ready"), signal("lora_act_ready")
    kk_sq_ready, kk_root_ready, scan_ready = signal("kk_sq_ready"), signal("kk_root_ready"), signal("scan_ready")
    step_in_ready, values_in_ready = signal("step_in_ready"), signal("values_in_ready")
    inputs_used = signal("inputs_used")
    lora_sums_ready, rates_ready = signal("lora_sums_ready"), signal("rates_ready")
    cumsum_ready, decays_ready = signal("cumsum_ready"), signal("decays_ready")
    pq_ready, k_ready, r_ready = signal("pq_ready"), signal("k_ready"), signal("r_ready")
    intra_ready, tokens_ready = signal("intra_ready"), signal("tokens_ready")
    level_left_ready, inverse_ready, inverseT_ready = (
        signal("level_left_ready", 10), signal("inverse_ready", 10), signal("inverseT_ready", 12))
    u0_ready, u_ready = signal("u0_ready", 2), signal("u_ready", 2)
    state_ready = signal("state_ready")
    x_back = sem("x_back")
    scan_done_act, scan_done_dve = sem("scan_done_act"), sem("scan_done_dve")
    y_var_ready, y_root_ready, y_ready = signal("y_var_ready"), signal("y_root_ready"), signal("y_ready")
    bonus_in_ready, gd_sig_ready, obx_ready = signal("bonus_in_ready"), signal("gd_sig_ready"), signal("obx_ready")
    gate2_ready, gate2_used, merged2_ready = signal("gate2_ready"), signal("gate2_used"), signal("merged2_ready")
    qTp_ready, h2_ready, scores_ready = signal("qTp_ready"), signal("h2_ready"), signal("scores_ready")
    gate_shift_ready, gate_exp_ready = signal("gate_shift_ready"), signal("gate_exp_ready")
    experts_ready = signal("experts_ready")
    idx_used = sem("idx_used")
    pool_copied = sem("pool_copied")
    row_landed = [sem(f"row_landed{i}") for i in range(GB)]
    row_used = [sem(f"row_used{i}") for i in range(GB)]
    gelu_in_ready, gelu_tanh_ready = signal("gelu_in_ready"), signal("gelu_tanh_ready")
    out_ready = signal("out_ready")

    act_ring.pe_section = act_ring.section = dve_ring.pe_section = dve_ring.section = "attention"
    second_block = ExitStack()
    block = second_block.enter_context(nc.Block())

    @block.sync
    def _(sp):
        sp.dma_start(rows2, R2.rearrange("p (m n) -> p m n", m=2)).then_inc(rows_landed, 16)
        sp.dma_start(ctxs, cin.rearrange("(t p) n -> p t n", p=P)).then_inc(ctx_landed, 16)
        for n, (name, count) in enumerate(ITEMS2):
            if n == LAST_BEFORE_SCAN + 1:
                sp.wait_ge(shift_parts_ready.sem, 1)
                sp.dma_start(lora, W2[:, w2_total:w2_total + 2048]).then_inc(lora_landed, 16)
                sp.wait_ge(*xn2_ready.at(0, 0))
                sp.dma_start(out.rearrange("(t p) n -> p t n", p=P), x).then_inc(stored, 16)
                sp.wait_ge(scan_done_act, 1)
                sp.wait_ge(scan_done_dve, 1)
            if n == LAST_BEFORE_SCAN + 3:
                sp.wait_ge(stored, 16)
                sp.dma_start(lora[:, 0:1024], W2[:, w2_total + 2048:w2_total + 3072]).then_inc(lora_landed, 16)
                sp.dma_start(x, out.rearrange("(t p) n -> p t n", p=P)).then_inc(x_back, 16)
            if name == "wq2":
                sp.wait_ge(*obx_ready.at(0))
                sp.wait_ge(*merged2_ready.at(0))
                sp.dma_start(keysT, W2[:, w2_total + 3072:w2_total + 5120].rearrange("p (c n) -> p c n", c=16)).then_inc(keys_landed, 16)
            sp.wait_ge(weights.used, used0 + n + 2)
            sp.dma_start(weights.view(n, count), W2[:, w2_off[name]:w2_off[name] + count]).then_inc(
                weights.landed[n % SLOTS], 16)
        sp.wait_ge(*out_ready.at(0))
        sp.dma_start(out.rearrange("(t p) n -> p t n", p=P), x).then_inc(stored, 16)
        sp.wait_ge(stored, 32)

    @block.tensor
    def _(pe):
        item_now = {}

        def item(name):
            n = ITEM2[name]
            s = n % SLOTS
            pe.wait_ge(weights.landed[s], (landed0[s] + n // SLOTS + 1) * 16)
            item_now["fresh"] = True
            return weights.view(n, ITEMS2[n][1])

        def mm(out, lhsT, rhs, start, stop, skip=False):
            ins = pe.matmul(out, lhsT, rhs, start=start, stop=stop, skip_group_check=skip)
            if item_now.get("fresh"):
                item_now["fresh"] = False
                assert not stop
                ins.then_inc(weights.used, 1)
            return ins

        def transposes(ring, tag, blocks):
            b = ring.open(pe, 0, tag)
            for j, src in enumerate(blocks):
                last = pe.transpose(b[:, j * P:(j + 1) * P], src, ident)
            last.then_inc(ring.full, 1)

        def token_major(ring, tag, srcT, w, kchunks, t):
            b = ring.open(pe, 0, tag)
            for k in range(kchunks):
                last = mm(b, srcT[:, k, t * P:(t + 1) * P], w[:, k, :], k == 0, k == kchunks - 1)
            last.then_inc(ring.full, 1)

        def channel_major(ring, tag, srcT, w, kchunks, chunks):
            for c in range(0, chunks, 2):
                b = ring.open(pe, 0, tag)
                for j in range(2):
                    for k in range(kchunks):
                        last = mm(b[:, j * T:(j + 1) * T], w[:, k, (c + j) * P:(c + j + 1) * P], srcT[:, k, :],
                                  k == 0, k == kchunks - 1)
                last.then_inc(ring.full, 1)

        def normed_transposes(src):
            for pair in range(4):
                ring = (act_ring, dve_ring)[pair % 2]
                transposes(ring, f"hT{pair}", [src[:, t, (2 * pair + c) * P:(2 * pair + c + 1) * P]
                                               for c in range(2) for t in range(TT)])

        def pad(section, na, nd):
            for ring, n in ((act_ring, na), (dve_ring, nd)):
                while len(ring.filled[section]) < n:
                    ring.open(pe, 0, "pad")
                    pe.drain().then_inc(ring.full, 1)
                assert len(ring.filled[section]) == n, (section, len(ring.filled[section]), n)

        pe.wait_ge(*cond_ready.at(0))
        for i in range(12):
            w = km_view(item(f"mod{i}"), 512)
            b = dve_ring.open(pe, 0, "mod")
            for k in range(8):
                if i // 2 in (2, 5):
                    last = mm(b, csb[:, k, :], w[:, k, :], k == 0, k == 7)
                else:
                    last = mm(b[0:2, :], cs[:, k, :], w[:, k, :], k == 0, k == 7)
            last.then_inc(dve_ring.full, 1)
        pe.wait_ge(*mod_rows_ready.at(0))
        b = dve_ring.open(pe, 0, "modT")
        for j in range(32):
            last = pe.transpose(b[:, 2 * j:2 * j + 2], mod_rows[0:2, j * P:(j + 1) * P], ident[0:2, 0:2])
        last.then_inc(dve_ring.full, 1)
        pe.wait_ge(*xn2_ready.at(0, 0))
        normed_transposes(xn)
        pe.wait_ge(*xn2_ready.at(0, 1))
        normed_transposes(ctxs)
        pe.wait_ge(*hT2_by_act.at(0, 1))
        pe.wait_ge(*hT2_by_dve.at(0, 1))
        for i in range(2):
            w = km_view(item(f"q{i}"), 512)
            for t in range(TT):
                token_major(act_ring, "q2", hT, w, 8, t)
        for n in "kv":
            for i in range(2):
                w = km_view(item(f"{n}{i}"), 512)
                for t in range(4):
                    token_major(act_ring, n + "2", (hcT, hT)[t // 2], w, 8, t % 2)
        for t in range(TT):
            pe.wait_ge(*qk2_ready.at(0, t))
        for h in range(0, 8, 2):
            transposes(act_ring, "qT2", [q2[:, t, (h + j) * P:(h + j + 1) * P] for j in range(2) for t in range(TT)])
        for t in range(2, 6):
            pe.wait_ge(*qk2_ready.at(0, t))
        for h in range(8):
            transposes(act_ring, "kT2", [k2[:, t, h * P:(h + 1) * P] for t in range(4)])
        pe.wait_ge(*qkT2_ready.at(0))
        pe.wait_ge(*v2_copied.at(0))
        def diff_scores(grp):
            t, half = grp // 2, grp % 2
            for hh in range(4):
                h = 4 * half + hh
                for m in range(2):
                    b = act_ring.open(pe, 0, "S2")
                    mm(b, qT2[64 * m:64 * m + 64, h, t * P:(t + 1) * P], kT2[64 * m:64 * m + 64, h, :], True, True).then_inc(act_ring.full, 1)

        diff_scores(0)
        for grp in range(4):
            pe.wait_ge(*diff_probs_ready.at(0, grp))
            for hh in range(4):
                transposes(act_ring, "PT2", [S2[:, hh, 0, j * P:(j + 1) * P] for j in range(4)])
            if grp < 3:
                diff_scores(grp + 1)
            pe.wait_ge(*diff_probsT_ready.at(0, grp))
            b = act_ring.open(pe, 0, "PV2")
            for hh in range(4):
                h = 4 * (grp % 2) + hh
                for j in range(4):
                    last = mm(b[:, hh * P:(hh + 1) * P], PT2[:, hh, j * P:(j + 1) * P], v2[:, j, h * P:(h + 1) * P], j == 0, j == 3)
            last.then_inc(act_ring.full, 1)
        pe.wait_ge(*diff_out_ready.at(0))
        for h in range(0, 8, 2):
            transposes(act_ring, "oaxT", [o2[:, t, (h + j) * P:(h + j + 1) * P] for j in range(2) for t in range(TT)])
        for i in range(7):
            w = km_view(item(f"rw{i}"), 512 if i < 6 else 256)
            for c in range(4 if i < 6 else 2):
                b = act_ring.open(pe, 0, "rw")
                for s, src in enumerate((hcT, hT)):
                    if s == 0 and (i < 2 or (i, c) == (6, 1)):
                        continue
                    for k in range(8):
                        last = mm(b[:, s * T:(s + 1) * T], w[:, k, c * P:(c + 1) * P], src[:, k, :], k == 0, k == 7)
                last.then_inc(act_ring.full, 1)
        pe.wait_ge(*kk_sq_ready.at(0))
        sq = Z_sq
        for c in range(8):
            b = dve_ring.open(pe, 0, "kk")
            mm(b, C2["onesbd"], sq[:, c, :], True, True).then_inc(dve_ring.full, 1)
        pad("attention", act_ring.sections["attention"][1], dve_ring.sections["attention"][1])

        pe.wait_ge(lora_landed, 16)
        pe.wait_ge(*scan_ready.at(0))
        def stand():
            pe.sem_inc(pe_step, 1)

        def section(name):
            act_ring.pe_section = dve_ring.pe_section = name

        def operand(buf, head, chain):
            if buf is None:
                return ident[:, 64 * head:64 * head + 64]
            return ch(buf[head] if isinstance(buf, tuple) else buf)[:, chain, :]

        def product(ring, it, tag, *terms, ready=None):
            for d in range(2):
                b = ring.open(pe, it, tag)
                if ready is not None:
                    for r in ready(d):
                        pe.wait_ge(*r)
                stand()
                for c in range(8):
                    for head in range(2):
                        for i, (lhsT, rhs) in enumerate(terms):
                            last = mm(b[64 * head:64 * head + 64, c * 64:(c + 1) * 64], operand(lhsT, head, 8 * d + c),
                                      operand(rhs, head, 8 * d + c), i == 0, i == len(terms) - 1, skip=True)
                last.then_inc(ring.full, 1)

        def rates(it, h):
            pe.wait_ge(*step_in_ready.at(h))
            stand()
            for d in range(2):
                for c in range(8):
                    if c % 4 == 0:
                        b = dve_ring.open(pe, it, "lora")
                        stand()
                    last = mm(b[:, (c % 4) * P:(c % 4 + 1) * P], lora[:, d * D + c * P:d * D + (c + 1) * P],
                              lor[:, d, :, :].rearrange("p s t -> p (s t)"), True, True)
                    if c % 4 == 3:
                        last.then_inc(dve_ring.full, 1)

        def head(it, h, of_x, next_rates=True):
            product(dve_ring, it, "LT", (Qm, Pm), ready=lambda d: (pq_ready.at(h),))
            product(dve_ring, it, "L", (Pm, Qm))
            product(dve_ring, it, "Apk", (Km, Pm), ready=lambda d: (k_ready.at(h),))
            product(act_ring, it, "Kt", (Km, None))
            product(act_ring, it, "Qt", (Qm, None))
            product(act_ring, it, "Vt", (Vt, None), ready=lambda d: (values_in_ready.at(h),))
            if of_x:
                product(dve_ring, it, "Ark", (Km, Rm), ready=lambda d: (r_ready.at(h),))
                product(dve_ring, it, "Arq", (Qm, Rm))
            if next_rates:
                rates(it, h + 1)
            for j in range(5):
                product(act_ring, it, "AL", (Loff, Dm), ready=lambda d: (inverse_ready.at(h, 2 * j + d),))
                ready = lambda d: (level_left_ready.at(h, 2 * j + d), inverseT_ready.at(h, 2 * j + d))
                if j < 4:
                    product(dve_ring, it, "E", (DTm, ARm), ready=ready)
                    product(dve_ring, it, "ET", (ARm, DTm))
                else:
                    product(dve_ring, it, "ET", (ARm, DTm), ready=ready)

        def tail(it, l, of_x):
            product(act_ring, it, "U0", (Pm, St), (Apk, VT_TOK), ready=lambda d: (state_ready.at(l), intra_ready.at(l), tokens_ready.at(l)))
            product(act_ring, it, "U", (DTm, U0), ready=lambda d: (inverseT_ready.at(l, 10 + d), u0_ready.at(l, d)))
            ready = lambda d: (u_ready.at(l, d),)
            if of_x:
                product(dve_ring, it, "Y", (Rm, St), (Ark, VT_TOK), (Arq, nU), ready=ready)
                ready = None
            product(dve_ring, it, "St", (Kt, VT_TOK), (Qt, nU), ready=ready)

        def pads(it):
            for ring in (act_ring, dve_ring):
                tags, n = ring.filled[ring.pe_section], ring.sections[ring.pe_section][1]
                while len(tags) < n:
                    ring.open(pe, it, "pad")
                    stand()
                    pe.drain().then_inc(ring.full, 1)
                assert len(tags) == n, (ring.pe_section, len(tags), n)

        section("scan_first")
        rates(0, 0)
        head(0, 0, False)
        pads(0)
        section("scan_ctx")
        with pe.Fori(0, 3) as it:
            tail(it, it, False)
            head(it, it + 1, False)
            pads(it)
        section("scan_turn")
        tail(0, 3, False)
        head(0, 4, True)
        pads(0)
        section("scan_x")
        with pe.Fori(0, 2) as it:
            tail(it, it + 4, True)
            head(it, it + 5, True)
            pads(it)
        section("scan_end")
        tail(0, 6, True)
        head(0, 7, True, next_rates=False)
        pads(0)
        section("scan_last")
        tail(0, 7, True)
        pads(0)

        act_ring.pe_section = dve_ring.pe_section = "post"
        for half in range(2):
            channel_major(act_ring, "gate2", hT, km_view(item(f"g{half}A"), 512), 8, 4)
        pe.wait_ge(*y_ready.at(0))
        for c in range(0, 8, 2):
            b = dve_ring.open(pe, 0, "yT")
            for head in range(2):
                for j in range(2):
                    for ck in range(4):
                        last = mm(b[64 * head:64 * head + 64, j * T + ck * 64:j * T + ck * 64 + 64], yb[:, c + j, ck * 64:(ck + 1) * 64],
                                  ident[:, 64 * head:64 * head + 64], True, True, skip=True)
            last.then_inc(dve_ring.full, 1)
        pe.wait_ge(*bonus_in_ready.at(0))
        for c in range(0, 8, 2):
            b = dve_ring.open(pe, 0, "bonus")
            mm(b, C2["onesbd"], rtmp[:, c:c + 2, :].rearrange("p c t -> p (c t)"), True, True).then_inc(dve_ring.full, 1)
        pe.wait_ge(*gd_sig_ready.at(0))
        pe.wait_ge(lora_landed, 32)
        for c in range(0, 8, 2):
            b = dve_ring.open(pe, 0, "g")
            for j in range(2):
                last = mm(b[:, j * T:(j + 1) * T], lora[:, (c + j) * P:(c + j + 1) * P], zg, True, True)
            last.then_inc(dve_ring.full, 1)
        pe.wait_ge(*oaxT_ready.at(0))
        for m, (n, src) in enumerate((("A", oaxT), ("B", obx))):
            if m:
                for half in range(2):
                    channel_major(act_ring, "gate2", hT, km_view(item(f"g{half}{n}"), 512), 8, 4)
                pe.wait_ge(*obx_ready.at(0))
            for half in range(2):
                channel_major(dve_ring, "mix2", src, km_view(item(f"o{n}{half}"), 512), 8, 4)
        pe.wait_ge(*merged2_ready.at(0))
        for half in range(2):
            w = km_view(item(f"out{half}"), 512)
            for t in range(TT):
                token_major(dve_ring, "out2", mg2, w, 8, t)
        pe.wait_ge(*xn2_ready.at(0, 2))
        normed_transposes(xn)
        pe.wait_ge(*hT2_by_act.at(0, 2))
        pe.wait_ge(*hT2_by_dve.at(0, 2))
        for t in range(TT):
            for half in range(2):
                transposes(act_ring, "h2", [hT[:, 4 * half + j, t * P:(t + 1) * P] for j in range(4)])
        for g in range(5):
            if g < 4:
                channel_major(act_ring, "qp", hT, km_view(item(f"wq{g}"), 512), 8, 4)
            if g == 0:
                continue
            pe.wait_ge(keys_landed, 16)
            pe.wait_ge(*qTp_ready.at(0, g - 1))
            for t in range(TT):
                b = act_ring.open(pe, 0, "sp")
                for c in range(4 * g - 4, 4 * g):
                    last = mm(b[:, (c % 4) * P:(c % 4 + 1) * P], qTp[:, c, t * P:(t + 1) * P], keysT[:, c, :], True, True)
                last.then_inc(act_ring.full, 1)

    @block.scalar
    def _(act):
        A = act.activation

        def take(tag, l=0):
            return act_ring.take(act, l, tag)

        def done(ins):
            return ins.then_inc(act_ring.free, 1)

        def roots(i):
            act.wait_ge(*sumsq2_ready.at(0, i))
            A(csd2, css2, ACT.Sqrt, bias=C["eps"], scale=1.0 / D).then_inc(root2_ready.sem, 1)

        def normed_evac(i, dst):
            for pair in range(0, 4, 2):
                b = take(f"hT{pair}")
                for c in range(2):
                    k = 2 * pair + c
                    last = A(dst[:, k, :], b[:, c * T:(c + 1) * T], ACT.Identity, bias=AB[:, 2 * i + 1, k:k + 1], scale=AB[:, 2 * i, k:k + 1])
                done(last)
            act.drain().then_inc(hT2_by_act.sem, 1)

        def heads(n):
            for i in range(n):
                act.wait_ge(*head2_sumsq_ready.at(0, head_count[0]))
                head_count[0] += 1
                A(sd2, ss2, ACT.Sqrt, bias=C["eps"], scale=1.0 / 64 if head_count[0] <= 6 else 1.0 / P).then_inc(head2_root_ready.sem, 1)

        def pad(section, l=0):
            tags = act_ring.filled[section]
            while len(act_ring.emptied[section]) < len(tags):
                act_ring.take(act, l, "pad")
                act.sem_inc(act_step, 1)
                act.drain().then_inc(act_ring.free, 1)
            act_ring.check(section)

        head_count = [0]
        act.wait_ge(const2_landed, 32)
        A(csig, V2["c"].rearrange("p (k s) -> p k s", s=2), ACT.Sigmoid).then_inc(cond_sig_ready.sem, 1)
        roots(0)
        roots(1)
        act.wait_ge(*mod_ready.at(0))
        normed_evac(0, hT)
        normed_evac(1, hcT)
        for i in range(2):
            for t in range(TT):
                done(A(q2[:, t, i * 512:(i + 1) * 512], take("q2"), ACT.Copy))
        for i in range(2):
            for t in range(4):
                done(A(k2[:, t, i * 512:(i + 1) * 512], take("k2"), ACT.Copy))
        act.drain().then_inc(qk2_copied.sem, 1)
        for i in range(8):
            done(A(v2[:, i % 4, (i // 4) * 512:(i // 4 + 1) * 512], take("v2"), ACT.Copy))
            if i < 6:
                heads(1)
        act.drain().then_inc(v2_copied.sem, 1)
        act.wait_ge(*lam_parts_ready.at(0))
        A(lam2, lam2, ACT.Exp).then_inc(lam_exp_ready.sem, 1)
        for h in range(0, 8, 2):
            done(A(qT2[:, h:h + 2, :], take("qT2").rearrange("p (h t) -> p h t", h=2), ACT.Copy))
        for h in range(8):
            done(A(kT2[:, h, :], take("kT2"), ACT.Copy))
        act.drain().then_inc(qkT2_ready.sem, 1)
        def diff_exps(grp):
            for i in range(8):
                act.wait_ge(*diff_max_ready.at(0, 8 * grp + i))
                done(A(S2[:, i // 2, i % 2, :], take("S2"), ACT.Exp, bias=mx2[:, i // 2, i % 2:i % 2 + 1], scale=0.125,
                       accum_out=se2[:, i // 2, i % 2:i % 2 + 1]))
            act.drain().then_inc(diff_exp_ready.sem, 1)

        diff_exps(0)
        for grp in range(4):
            t, half = grp // 2, grp % 2
            for hh in range(4):
                done(A(PT2[:, hh, :], take("PT2"), ACT.Copy))
            act.drain().then_inc(diff_probsT_ready.sem, 1)
            if grp < 3:
                diff_exps(grp + 1)
            done(A(o2[:, t, half * 512:(half + 1) * 512], take("PV2"), ACT.Copy))
        act.drain().then_inc(diff_out_copied.sem, 1)
        heads(1)
        for h in range(0, 8, 2):
            done(A(oaxT[:, h:h + 2, :], take("oaxT").rearrange("p (h t) -> p h t", h=2), ACT.Copy))
        act.drain().then_inc(oaxT_ready.sem, 1)
        for c in range(26):
            b = take("rw")
            if c >= 2:
                act.wait_ge(*shift_parts_used.at(0, c - 2))
            dst, w = shift_out(c)
            A(dst, b[:, HALF - w:HALF], ACT.Copy, scale=V2["shift"][:, 26 + c:27 + c])
            done(A(zraw[:, c % 2, HALF - w:HALF], b[:, HALF - w:HALF], ACT.Copy))
            act.drain().then_inc(shift_parts_ready.sem, 1)
        for c in range(8):
            A(Z_sq[:, c, :], dve_ring.peek(act, "attention", "kk", c), ACT.Sqrt, bias=C["l2eps"]).then_inc(kk_root_ready.sem, 1)
        act.wait_ge(*shifted_ready.at(0))
        A(zwa[0:64, :], zwa[0:64, :], ACT.Tanh).then_inc(lora_act_ready.sem, 1)
        pad("attention")

        def evac(it, tag, dst, minus=0, ready=None):
            for d in range(2):
                b = take(tag, it)
                if isinstance(dst, tuple):
                    A(dst[0][:, d * 512:(d + 1) * 512], b, ACT.Copy, scale=even_odd[:, minus:minus + 1])
                    done(A(dst[1][:, d * 512:(d + 1) * 512], b, ACT.Copy, scale=even_odd[:, minus + 1:minus + 2]))
                else:
                    done(A(dst[:, d * 512:(d + 1) * 512], b, ACT.Copy))
                if ready is not None:
                    act.drain().then_inc(ready.sem, 1)

        def sigmoids(h):
            act.wait_ge(*lora_sums_ready.at(h))
            act.sem_inc(act_step, 1)
            A(SIG2, SIG2, ACT.Sigmoid).then_inc(rates_ready.sem, 1)

        def decays(h):
            act.wait_ge(*cumsum_ready.at(h))
            act.sem_inc(act_step, 1)
            A(r0, r2, ACT.Exp, scale=DECAY)
            A(r3, r3, ACT.Exp, scale=DECAY)
            act.drain()
            A(r2, r2, ACT.Exp, scale=-DECAY).then_inc(decays_ready.sem, 1)

        def scan_pass(it, name, l, h, next_rates=True):
            act_ring.section = name
            if l is not None:
                evac(it, "U0", U0, ready=u0_ready)
                evac(it, "U", nU, minus=2, ready=u_ready)
            if h is not None:
                evac(it, "Kt", Kt)
                evac(it, "Qt", Qt)
                evac(it, "Vt", VT_TOK)
                act.drain().then_inc(tokens_ready.sem, 1)
                for j in range(5):
                    evac(it, "AL", ARm, ready=level_left_ready)
                    if next_rates and j == 0:
                        sigmoids(h + 1)
                if next_rates:
                    decays(h + 1)
            pad(name, it)

        act.wait_ge(*scan_ready.at(0))
        sigmoids(0)
        decays(0)
        scan_pass(0, "scan_first", None, 0)
        with act.Fori(0, 3) as it:
            scan_pass(it, "scan_ctx", it, it + 1)
        scan_pass(0, "scan_turn", 3, 4)
        with act.Fori(0, 2) as it:
            scan_pass(it, "scan_x", it + 4, it + 5)
        scan_pass(0, "scan_end", 6, 7, next_rates=False)
        scan_pass(0, "scan_last", 7, None)
        act.sem_inc(scan_done_act, 1)

        act_ring.section = "post"
        act.wait_ge(*y_var_ready.at(0))
        A(yd, ys, ACT.Sqrt, bias=C["lneps"], scale=1.0 / 64).then_inc(y_root_ready.sem, 1)
        A(zg, zg, ACT.Sigmoid).then_inc(gd_sig_ready.sem, 1)
        for m in range(2):
            if m:
                act.wait_ge(*gate2_used.at(0))
            for c in range(0, 8, 2):
                done(A(gsig2[:, c:c + 2, :], take("gate2").rearrange("p (c t) -> p c t", c=2), ACT.Sigmoid))
            act.drain().then_inc(gate2_ready.sem, 1)
        roots(2)
        normed_evac(2, hT)
        for t in range(TT):
            for half in range(2):
                done(A(h2[:, t, half * 512:(half + 1) * 512], take("h2"), ACT.Copy))
        act.drain().then_inc(h2_ready.sem, 1)
        for g in range(5):
            if g < 4:
                for c in range(4 * g, 4 * g + 4, 2):
                    done(A(qTp[:, c:c + 2, :], take("qp").rearrange("p (c t) -> p c t", c=2), ACT.Copy))
                act.drain().then_inc(qTp_ready.sem, 1)
            if g:
                for t in range(TT):
                    done(A(sp_[:, t, 4 * g - 4:4 * g, :], take("sp").rearrange("p (c n) -> p c n", c=4), ACT.Copy))
                    act.drain().then_inc(scores_ready.sem, 1)
        for t in range(TT):
            act.wait_ge(*gate_shift_ready.at(0, t))
            A(gatep[:, t, :, :], gatep[:, t, :, :], ACT.Exp).then_inc(gate_exp_ready.sem, 1)
        for t in range(TT):
            act.wait_ge(*gelu_in_ready.at(0, t))
            A(g1[:, t * P:(t + 1) * P], g1[:, t * P:(t + 1) * P], ACT.Tanh, scale=float(np.sqrt(2.0 / np.pi))).then_inc(gelu_tanh_ready.sem, 1)
        act_ring.check("post")

    @block.vector
    def _(v):
        def take(tag, l=0):
            return dve_ring.take(v, l, tag)

        def done(ins):
            return ins.then_inc(dve_ring.free, 1)

        def tt(o, a, b, op):
            return v.tensor_tensor(o, a, b, op)

        def model_norm(i, src, dst):
            for t in range(TT):
                v.tensor_tensor_reduce(xn[:, t, :] if dst is xn else S_junk, src[:, t, :], src[:, t, :], 1.0, 0.0, ALU.mult, ALU.add, css2[:, t:t + 1])
                if dst is not xn:
                    v.drain()
            v.drain().then_inc(sumsq2_ready.sem, 1)
            v.wait_ge(*root2_ready.at(0, i))
            v.reciprocal(crs2, csd2)
            v.drain()
            for t in range(TT):
                v.tensor_scalar(dst[:, t, :], src[:, t, :], crs2[:, t:t + 1], None, ALU.mult)
            v.drain().then_inc(xn2_ready.sem, 1)

        def normed_evac(i, dst):
            for pair in range(1, 4, 2):
                b = take(f"hT{pair}")
                for c in range(2):
                    k = 2 * pair + c
                    last = v.tensor_scalar(dst[:, k, :], b[:, c * T:(c + 1) * T], AB[:, 2 * i, k:k + 1], AB[:, 2 * i + 1, k:k + 1], ALU.mult, ALU.add)
                done(last)
            v.drain().then_inc(hT2_by_dve.sem, 1)

        def head_norm(i, y, gain, n, d, factor=None):
            sq = junk[:, 0:n * d].rearrange("p (n d) -> p n d", n=n)
            tt(sq, y, y, ALU.mult)
            v.drain()
            v.tensor_reduce(ss2[:, 0:n], sq, AX.X, ALU.add).then_inc(head2_sumsq_ready.sem, 1)
            v.wait_ge(*head2_root_ready.at(0, i))
            v.reciprocal(rs2[:, 0:n], sd2[:, 0:n])
            v.drain()
            if factor is not None:
                v.tensor_scalar(rs2[:, 0:n], rs2[:, 0:n], factor, None, ALU.mult)
                v.drain()
            tt(y, y, bc(rs2[:, 0:n], 2, d), ALU.mult)
            v.drain()
            tt(y, y, bc(gain, 1, n), ALU.mult)
            v.drain()

        def pad(section, l=0):
            tags = dve_ring.filled[section]
            while len(dve_ring.emptied[section]) < len(tags):
                dve_ring.take(v, l, "pad")
                v.sem_inc(dve_step, 1)
                v.drain().then_inc(dve_ring.free, 1)
            dve_ring.check(section)

        v.wait_ge(const2_landed, 32)
        v.wait_ge(*cond_sig_ready.at(0))
        tt(cs, V2["c"].rearrange("p (k s) -> p k s", s=2), csig, ALU.mult)
        v.drain()
        v.tensor_copy(csb, bc(cs[:, :, 0], 2, P))
        v.drain().then_inc(cond_ready.sem, 1)
        model_norm(0, x, xn)
        v.wait_ge(ctx_landed, 16)
        model_norm(1, ctxs, ctxs)
        v.wait_ge(rows_landed, 16)
        for i in range(12):
            m, half = i // 2, i % 2
            b = take("mod")
            if m in (2, 5):
                r = rows2[:, m // 5, half * 512:(half + 1) * 512]
                done(tt(r, b, r, ALU.add))
            else:
                at = {0: 0, 1: 1, 3: 2, 4: 3}[m] * D + half * 512
                done(v.tensor_copy(mod_rows[0:2, at:at + 512], b[0:2, :]))
        v.drain().then_inc(mod_rows_ready.sem, 1)
        b = take("modT")[:, 0:64].rearrange("p (m s) -> p m s", s=2)
        done(tt(modT.rearrange("p m c s -> p (m c) s"), b, bc(V2["b_mod"], 2, 2), ALU.add))
        v.drain()
        for i, (scale_m, shift_m, s, g) in enumerate(((1, 0, 0, "norm1"), (1, 0, 1, "norm1"), (3, 2, 0, "norm2"))):
            v.scalar_tensor_tensor(AB[:, 2 * i, :], modT[:, scale_m, :, s], 1.0, V2[g], ALU.add, ALU.mult)
            v.tensor_copy(AB[:, 2 * i + 1, :], modT[:, shift_m, :, s])
        v.drain().then_inc(mod_ready.sem, 1)
        normed_evac(0, hT)
        normed_evac(1, hcT)
        lam = V2["lam"].rearrange("p (k n) -> p k n", k=4)
        for i in range(2):
            v.tensor_tensor_reduce(junk[:, 0:64], lam[:, 2 * i, :], lam[:, 2 * i + 1, :], 1.0, 0.0, ALU.mult, ALU.add, lam2[:, i:i + 1])
            v.drain()
        v.sem_inc(lam_parts_ready.sem, 1)
        v.wait_ge(*qk2_copied.at(0))
        acos, asin = (C2[n].rearrange("p (t a n) -> p t a n", t=TT, a=2) for n in ("acos", "asin"))
        for i in range(6):
            src = q2[:, i, :] if i < 2 else k2[:, i - 2, :]
            head_norm(i, src.rearrange("p (n d) -> p n d", n=16), V2["q_norm"] if i < 2 else V2["k_norm"], 16, 64)
            if i < 2 or i >= 4:
                t = i % 2
                y = src.rearrange("p (n a s f) -> p n a s f", n=16, a=2, s=2)
                x1, x2 = y[:, :, :, 0, :], y[:, :, :, 1, :]
                ta, tb, tc, td = (junk[:, 512 * j:512 * (j + 1)].rearrange("p (n a f) -> p n a f", n=16, a=2) for j in range(4))
                cb, sn = bc(acos[:, t, :, :], 1, 16), bc(asin[:, t, :, :], 1, 16)
                tt(ta, x1, cb, ALU.mult)
                tt(tb, x2, sn, ALU.mult)
                tt(tc, x2, cb, ALU.mult)
                tt(td, x1, sn, ALU.mult)
                v.drain()
                tt(x1, ta, tb, ALU.subtract)
                tt(x2, tc, td, ALU.add)
                v.drain()
            v.sem_inc(qk2_ready.sem, 1)
        v.wait_ge(*lam_exp_ready.at(0))
        tt(nlam, lam2[:, 1:2], lam2[:, 0:1], ALU.subtract)
        v.drain()
        v.tensor_scalar(nlam, nlam, -(0.8 - 0.6 * float(np.exp(-0.3 * 0))), None, ALU.add)
        v.drain()
        for grp in range(4):
            for i in range(8):
                b = act_ring.peek(v, "attention", "S2", 8 * grp + i)
                m = mx2[:, i // 2, i % 2:i % 2 + 1]
                v.tensor_reduce(m, b, AX.X, ALU.max)
                v.drain()
                v.tensor_scalar(m, m, -0.125, None, ALU.mult).then_inc(diff_max_ready.sem, 1)
            v.wait_ge(*diff_exp_ready.at(0, grp))
            v.reciprocal(sc2, se2)
            v.drain()
            v.tensor_scalar(sc2[:, :, 1], sc2[:, :, 1], nlam, None, ALU.mult)
            v.drain()
            for hh in range(4):
                v.tensor_scalar(S2[:, hh, 1, :], S2[:, hh, 1, :], sc2[:, hh, 1:2], None, ALU.mult)
            v.drain()
            for hh in range(4):
                last = v.scalar_tensor_tensor(S2[:, hh, 0, :], S2[:, hh, 0, :], sc2[:, hh, 0:1], S2[:, hh, 1, :], ALU.mult, ALU.add)
            last.then_inc(diff_probs_ready.sem, 1)
        v.wait_ge(*diff_out_copied.at(0))
        head_norm(6, o2.rearrange("p t (h n) -> p (t h) n", h=8), V2["out_g"], 16, P, factor=0.6 * float(np.exp(-0.3 * 0)) + 0.2)
        v.sem_inc(diff_out_ready.sem, 1)
        for c in range(26):
            v.wait_ge(*shift_parts_ready.at(0, c))
            dst, w = shift_out(c)
            z = dst.rearrange("p (s t) -> p s t", t=T)
            r = zraw[:, c % 2, HALF - w:HALF].rearrange("p (s t) -> p s t", t=T)
            v.scalar_tensor_tensor(z[:, :, 1:T], r[:, :, 0:T - 1], V2["shift"][:, c:c + 1], z[:, :, 1:T], ALU.mult, ALU.add)
            v.drain()
            v.scalar_tensor_tensor(z[:, :, 0:T - 1], r[:, :, 1:T], V2["shift"][:, 52 + c:53 + c], z[:, :, 0:T - 1],
                                   ALU.mult, ALU.add).then_inc(shift_parts_used.sem, 1)
        v.drain().then_inc(shifted_ready.sem, 1)
        tt(kk, zk, bc(V2["k_k"], 2, HALF), ALU.mult)
        v.drain()
        tt(Z_sq, kk, kk, ALU.mult)
        v.drain().then_inc(kk_sq_ready.sem, 1)
        for c in range(8):
            take("kk")
            v.wait_ge(*kk_root_ready.at(0, c))
            done(v.reciprocal(Z_sq[:, c, :], Z_sq[:, c, :]))
            v.drain()
            tt(kk[:, c, :], kk[:, c, :], Z_sq[:, c, :], ALU.mult)
        v.wait_ge(stored, 16)
        v.memset(St, 0.0)
        v.memset(lor, 0.0)
        v.memset(yb, 0.0)
        v.memset(restart, 1.0)
        v.drain()
        v.memset(restart.rearrange("p (c t) -> p c t", c=8)[:, :, 0:1], 0.0)
        v.wait_ge(*lora_act_ready.at(0))
        pad("attention")
        v.drain().then_inc(state_ready.sem, 1)
        v.drain().then_inc(inputs_used.sem, 1)
        v.drain().then_inc(scan_ready.sem, 1)

        strict, incl = (C2[n].rearrange("p (d t) -> p d t", d=2) for n in ("strict", "incl"))
        level = C2["level"].rearrange("p (m d t) -> p m d t", m=6, d=2)
        idb = bc(C2["id2"], 1, 8)

        def dir_(ap, d):
            return ch2(ap)[:, d, :, :]

        def masked(it, tag, dst, mask):
            for d in range(2):
                done(tt(dir_(dst, d), take(tag, it).rearrange("p (c n) -> p c n", c=8), bc(mask[:, d, :], 1, 8), ALU.mult))

        def split(dst, d, a, b):
            for head in range(2):
                v.scalar_tensor_tensor(dir_(dst[head], d), a, even_odd[:, head:head + 1], b, ALU.mult, ALU.mult)

        def add_outputs(it, y_at):
            for d in range(2):
                b = take("Y", it)
                v.sem_inc(dve_step, 1)
                y = yb[:, :, bass.ds(y_at[d], 64)]
                done(tt(y, b.rearrange("p (c n) -> p c n", c=8), y, ALU.add))
                v.drain()

        def new_state(it):
            for d in range(2):
                s = St[:, d * 512:(d + 1) * 512]
                done(tt(s, take("St", it), s, ALU.add))
            v.drain()
            tt(ch(St), ch(St), bc(Wc, 2, 64), ALU.mult)
            v.drain().then_inc(state_ready.sem, 1)

        def rate_sums(it, h):
            for d in range(2):
                for c in (0, 4):
                    b = take("lora", it).rearrange("p (c s n) -> p c s n", c=4, s=2)
                    for part, bias in enumerate(("w0", "a0")):
                        last = tt(dir_((r0, r1)[part], d)[:, c:c + 4, :], b[:, :, part, :],
                                  bc(V2[bias].rearrange("p (d c) -> p d c", d=2)[:, d, c:c + 4], 2, 64), ALU.add)
                    done(last)
            v.drain().then_inc(lora_sums_ready.sem, 1)
            v.drain().then_inc(inputs_used.sem, 1)

        def cumulate(h, d):
            if d == 0:
                v.wait_ge(*rates_ready.at(h))
                v.sem_inc(dve_step, 1)
            s = slice(512 * d, 512 * d + 512)
            out, decay = (r2[:, s][:, ::-1], r0[:, s][:, ::-1]) if d else (r2[:, s], r0[:, s])
            v.tensor_tensor_scan(out, restart, decay, 0.0, ALU.mult, ALU.add)

        def exclude(h):
            v.drain()
            tt(r3, r2, r0, ALU.subtract)
            v.drain().then_inc(cumsum_ready.sem, 1)

        def scan_pass(it, name, l, h, of_x, at=None, y_at=None, next_rates=True):
            dve_ring.section = name
            if h is None:
                add_outputs(it, y_at)
                new_state(it)
                pad(name, it)
                return
            if l is None:
                rate_sums(it, h)
                cumulate(h, 0)
                cumulate(h, 1)
                exclude(h)
            at_time = lambda src, d, off=0: src[:, :, bass.ds(at[d] - off, 64)]
            v.wait_ge(*decays_ready.at(h))
            v.sem_inc(dve_step, 1)
            v.tensor_copy(Wnext[:, 0:8], dir_(r0, 0)[:, :, 63])
            v.tensor_copy(Wnext[:, 8:16], dir_(r0, 1)[:, :, 0])
            for d in range(2):
                v.scalar_tensor_tensor(dir_(Km, d), dir_(r1, d), 1.0, bc(V2["k_a"], 2, 64), ALU.subtract, ALU.mult)
            v.drain()
            for d in range(2):
                v.scalar_tensor_tensor(dir_(Km, d), dir_(Km, d), 1.0, at_time(zk, d), ALU.add, ALU.mult)
                tt(dir_(r1, d), at_time(kk, d), dir_(r1, d), ALU.mult)
            v.drain()
            tt(Qm, r1, r2, ALU.mult)
            if l is not None:
                v.wait_ge(*u0_ready.at(l, 1))
                v.sem_inc(dve_step, 1)
            for d in range(2):
                split(Pm, d, at_time(kk, d), dir_(r3, d))
            v.drain().then_inc(pq_ready.sem, 1)
            tt(Km, Km, r2, ALU.mult)
            v.drain().then_inc(k_ready.sem, 1)
            if y_at is not None:
                add_outputs(it, y_at)
            if l is not None:
                new_state(it)
            v.tensor_copy(Wc, Wnext)
            masked(it, "LT", LT, strict)
            v.drain()
            for d in range(2):
                tt(dir_(DTm, d), dir_(LT, d), bc(level[:, 0, d, :], 1, 8), ALU.mult)
            for d in range(2):
                done(tt(dir_(Dm, d), take("L", it).rearrange("p (c n) -> p c n", c=8), bc(level[:, 0, 1 - d, :], 1, 8), ALU.mult))
            v.drain()
            for d in range(2):
                tt(dir_(Dm, d), idb, dir_(Dm, d), ALU.subtract)
                tt(dir_(DTm, d), idb, dir_(DTm, d), ALU.subtract)
                split(Loff, d, dir_(LT, d), bc(level[:, 1, d, :], 1, 8))
            for d in range(2):
                v.drain().then_inc(inverse_ready.sem, 1)
                v.drain().then_inc(inverseT_ready.sem, 1)
            if of_x:
                for d in range(2):
                    split(Rm, d, at_time(zr, d, T), dir_(r0, d))
            v.drain().then_inc(r_ready.sem, 1)
            masked(it, "Apk", Apk, strict)
            if of_x:
                masked(it, "Ark", Ark, incl)
                masked(it, "Arq", Arq, incl)
            v.drain().then_inc(intra_ready.sem, 1)
            if next_rates:
                rate_sums(it, h + 1)
            for j in range(5):
                if j < 4:
                    for d in range(2):
                        done(tt(Dm[:, d * 512:(d + 1) * 512], Dm[:, d * 512:(d + 1) * 512], take("E", it), ALU.subtract))
                        split(Loff, d, dir_(LT, d), bc(level[:, 2 + j, d, :], 1, 8))
                        v.drain().then_inc(inverse_ready.sem, 1)
                for d in range(2):
                    done(tt(DTm[:, d * 512:(d + 1) * 512], DTm[:, d * 512:(d + 1) * 512], take("ET", it), ALU.subtract))
                    v.drain().then_inc(inverseT_ready.sem, 1)
                if next_rates and j in (1, 2):
                    cumulate(h + 1, j - 1)
                if next_rates and j == 3:
                    exclude(h + 1)
            pad(name, it)

        scan_pass(0, "scan_first", None, 0, False, at=(0, 192))
        with v.Fori(0, 3) as it:
            scan_pass(it, "scan_ctx", it, it + 1, False, at=(it * 64 + 64, 128 - it * 64))
        scan_pass(0, "scan_turn", 3, 4, True, at=(T, T + 192))
        with v.Fori(0, 2) as it:
            scan_pass(it, "scan_x", it + 4, it + 5, True, at=(it * 64 + T + 64, T + 128 - it * 64), y_at=(it * 64, 192 - it * 64))
        scan_pass(0, "scan_end", 6, 7, True, at=(T + 192, T), y_at=(128, 64), next_rates=False)
        scan_pass(0, "scan_last", 7, None, True, y_at=(192, 0))
        v.sem_inc(scan_done_dve, 1)

        dve_ring.section = "post"
        y0 = yb.rearrange("p c (s n) -> p (c s) n", n=64)
        y1 = BON.rearrange("p c (s n) -> p (c s) n", n=64)
        v.tensor_reduce(ys, y0, AX.X, ALU.add)
        v.drain()
        v.tensor_scalar(ys, ys, 1.0 / 64, None, ALU.mult)
        v.drain()
        tt(y0, y0, bc(ys, 2, 64), ALU.subtract)
        v.drain()
        tt(y1, y0, y0, ALU.mult)
        v.drain()
        v.tensor_reduce(ys, y1, AX.X, ALU.add)
        v.drain().then_inc(y_var_ready.sem, 1)
        v.wait_ge(*y_root_ready.at(0))
        v.reciprocal(yr, yd)
        v.drain()
        tt(y0, y0, bc(yr, 2, 64), ALU.mult)
        v.drain().then_inc(y_ready.sem, 1)
        tt(rtmp, zr, zk[:, :, T:2 * T], ALU.mult)
        v.drain()
        tt(rtmp, rtmp, bc(V2["r_k"], 2, T), ALU.mult)
        v.drain().then_inc(bonus_in_ready.sem, 1)
        for c in range(0, 8, 2):
            b = take("yT")
            for j in range(2):
                last = v.tensor_scalar(obx[:, c + j, :], b[:, j * T:(j + 1) * T], V2["ln_g"][:, c + j:c + j + 1],
                                       V2["ln_b"][:, c + j:c + j + 1], ALU.mult, ALU.add)
            done(last)
        v.drain()
        for c in range(0, 8, 2):
            b = take("bonus")
            done(tt(BON[:, c:c + 2, :], b.rearrange("p (c t) -> p c t", c=2), zv[:, c:c + 2, T:2 * T], ALU.mult))
        v.drain()
        tt(obx, obx, BON, ALU.add)
        v.drain()
        for c in range(0, 8, 2):
            b = take("g")
            done(tt(obx[:, c:c + 2, :], obx[:, c:c + 2, :], b.rearrange("p (c t) -> p c t", c=2), ALU.mult))
        v.drain().then_inc(obx_ready.sem, 1)
        for m in range(2):
            v.wait_ge(*gate2_ready.at(0, m))
            for c in range(0, 8, 2):
                b = take("mix2").rearrange("p (c t) -> p c t", c=2)
                g = gsig2[:, c:c + 2, :]
                done(tt(mg2[:, c:c + 2, :] if m == 0 else g, b, g, ALU.mult))
            v.drain()
            if m:
                tt(mg2, mg2, gsig2, ALU.add)
                v.drain()
            v.sem_inc((gate2_used, merged2_ready)[m].sem, 1)
        v.wait_ge(x_back, 16)
        for half in range(2):
            for t in range(TT):
                xs, r = x[:, t, half * 512:(half + 1) * 512], rows2[:, 0, half * 512:(half + 1) * 512]
                j = junk[:, (2 * half + t) * 512:(2 * half + t + 1) * 512]
                done(tt(j, take("out2"), r, ALU.mult))
                v.drain()
                tt(xs, xs, j, ALU.add)
        v.drain()
        model_norm(2, x, xn)
        normed_evac(2, hT)

        for t in range(TT):
            for g in range(4):
                v.wait_ge(*scores_ready.at(0, TT * g + t))
                for c in range(4 * g, 4 * g + 4):
                    v.max(sv[:, t, c, 0:8], sp_[:, t, c, :])
                v.drain()
                for c in range(4 * g, 4 * g + 4):
                    v.max_index(siu_u[:, t, c, 0:8], sv[:, t, c, 0:8], sp_[:, t, c, :])
                for c in range(4 * g, 4 * g + 4):
                    v.match_replace(sp_[:, t, c, :], sv[:, t, c, 0:8], sp_[:, t, c, :], -3e38)
                v.drain()
                for c in range(4 * g, 4 * g + 4):
                    v.max(sv[:, t, c, 8:16], sp_[:, t, c, :])
                v.drain()
                for c in range(4 * g, 4 * g + 4):
                    v.max_index(siu_u[:, t, c, 8:16], sv[:, t, c, 8:16], sp_[:, t, c, :])
            v.drain()
            v.tensor_copy(sif[:, t, :, :], siu_u[:, t, :, :])
            svv = sv[:, t, :, :].rearrange("p (h s) n -> p h s n", s=2)
            tt(cand.rearrange("p h (i j) -> p h i j", i=16), bc(svv[:, :, 0, :], 3, 16), bc(svv[:, :, 1, :], 2, 16), ALU.add)
            v.drain()
            for h in range(8):
                v.max(tops[:, t, h, 0:8], cand[:, h, :])
            v.drain()
            for h in range(8):
                v.max_index(posu_u[:, t, h, 0:8], tops[:, t, h, 0:8], cand[:, h, :])
            for h in range(8):
                v.match_replace(cand[:, h, :], tops[:, t, h, 0:8], cand[:, h, :], -3e38)
            v.drain()
            for h in range(8):
                v.max(tops[:, t, h, 8:16], cand[:, h, :])
            v.drain()
            for h in range(8):
                v.max_index(posu_u[:, t, h, 8:16], tops[:, t, h, 8:16], cand[:, h, :])
            v.drain()
            pu = posu_u[:, t, :, :].rearrange("p h n -> p (h n)")
            v.tensor_scalar(hiu_u[:, 0:P], pu, 4, None, ALU.logical_shift_right)
            v.tensor_scalar(lou_u[:, 0:P], pu, 15, None, ALU.bitwise_and)
            v.drain()
            v.tensor_copy(hif, hiu_u[:, 0:P])
            v.tensor_copy(lof, lou_u[:, 0:P])
            v.drain()
            siv = sif[:, t, :, :].rearrange("p (h s) n -> p h s n", s=2)
            for s, (src, dst) in enumerate(((hif, i1f), (lof, i2f))):
                e3 = eqb.rearrange("p (k n) -> p k n", n=16)
                tt(e3, bc(src, 2, 16), bc(C2["iota16"], 1, P), ALU.is_equal)
                v.drain()
                e4 = eqb.rearrange("p (h k n) -> p h k n", h=8, k=16)
                tt(e4, e4, bc(siv[:, :, s, :], 2, 16), ALU.mult)
                v.drain()
                v.tensor_reduce(dst, e3, AX.X, ALU.add)
                v.drain()
            v.scalar_tensor_tensor(i1f, i1f, float(P), i2f, ALU.mult, ALU.add)
            v.drain()
            v.tensor_copy(eidx_u[:, t * P:(t + 1) * P], i1f).then_inc(experts_ready.sem, 1)
            tt(gatep[:, t, :, :], tops[:, t, :, :], bc(tops[:, t, :, 0], 2, 16), ALU.subtract)
            v.drain().then_inc(gate_shift_ready.sem, 1)
        for t in range(TT):
            v.wait_ge(*gate_exp_ready.at(0, t))
            v.tensor_reduce(gsm[:, 0:8], gatep[:, t, :, :], AX.X, ALU.add)
            v.drain()
            v.reciprocal(grc[:, 0:8], gsm[:, 0:8])
            v.drain()
            tt(gatep[:, t, :, :], gatep[:, t, :, :], bc(grc[:, 0:8], 2, 16), ALU.mult)
            v.drain()
        v.wait_ge(*h2_ready.at(0))
        NB = P // GB
        for t in range(TT):
            with v.Fori(0, NB) as j:
                for i in range(GB):
                    v.wait_ge(row_landed[i], (j + t * NB) * 16 + 16)
                    v.sem_inc(dve_step, 1)
                    v.tensor_tensor_reduce(gat[:, i, :], gat[:, i, :], h2[:, t, :], 1.0, 0.0, ALU.mult, ALU.add,
                                           dot8[:, i:i + 1]).then_inc(row_used[i], 1)
                v.drain()
                v.tensor_copy(actp[:, bass.ds(j * GB + t * P, GB)], dot8[:, 0:GB])
                v.drain()
        for t in range(TT):
            c = slice(t * P, (t + 1) * P)
            tt(g1[:, c], actp[:, c], actp[:, c], ALU.mult)
            v.drain()
            v.tensor_scalar(g1[:, c], g1[:, c], 0.044715, 1.0, ALU.mult, ALU.add)
            v.drain()
            tt(g1[:, c], g1[:, c], actp[:, c], ALU.mult)
            v.drain().then_inc(gelu_in_ready.sem, 1)
            v.wait_ge(*gelu_tanh_ready.at(0, t))
            v.tensor_scalar(g1[:, c], g1[:, c], 1.0, 0.5, ALU.add, ALU.mult)
            v.drain()
            tt(g1[:, c], g1[:, c], actp[:, c], ALU.mult)
            v.drain()
            tt(g1[:, c], g1[:, c], gatep[:, t, :, :].rearrange("p h n -> p (h n)"), ALU.mult)
            v.drain()
        v.memset(acc, 0.0)
        v.drain()
        for t in range(TT):
            with v.Fori(0, NB) as j:
                v.tensor_copy(wt8[:, 0:GB], g1[:, bass.ds(j * GB + t * P, GB)])
                v.drain()
                for i in range(GB):
                    v.wait_ge(row_landed[i], (j + (TT + t) * NB) * 16 + 16)
                    v.scalar_tensor_tensor(acc[:, t, :], gat[:, i, :], wt8[:, i:i + 1], acc[:, t, :], ALU.mult, ALU.add).then_inc(row_used[i], 1)
                    v.drain()
        for t in range(TT):
            tt(acc[:, t, :], acc[:, t, :], rows2[:, 1, :], ALU.mult)
        v.drain()
        tt(x, x, acc, ALU.add).then_inc(out_ready.sem, 1)
        dve_ring.check("post")

    @block.gpsimd
    def _(pool):
        NB = P // GB
        pool.wait_ge(*scan_ready.at(0))
        with pool.Fori(0, 2) as stream, pool.Fori(0, 4) as step:
            l = stream * 4 + step
            starts = (stream * T + step * 64, stream * T + 192 - step * 64)
            pool.wait_ge(*inputs_used.at(l))
            pool.sem_inc(idx_used, 1)
            for d in range(2):
                for part in range(2):
                    s = slice(64 * part, 64 * part + 64)
                    pool.tensor_copy(lor[s, d, part, :], zwa[s, bass.ds(starts[d], 64)])
            pool.drain().then_inc(step_in_ready.sem, 1)
            pool.wait_ge(k_ready.sem, l + 1)
            pool.sem_inc(idx_used, 1)
            for d in range(2):
                pool.tensor_copy(ch2(Vt)[:, d, :, :], zv[:, :, bass.ds(starts[d], 64)])
            pool.drain().then_inc(values_in_ready.sem, 1)

        for i in range(GB):
            pool.sem_inc(row_used[i], 1)
        for k, table in enumerate((PU, PV)):
            for t in range(TT):
                if k == 0:
                    pool.wait_ge(*experts_ready.at(0, t))
                with pool.Fori(0, NB // 2) as pair:
                    for e in range(2):
                        j = pair * 2 + e
                        cols8 = idx8_u[:, e * GB:(e + 1) * GB]
                        pool.tensor_copy(cols8, eidx_u[:, bass.ds(j * GB + t * P, GB)]).then_inc(pool_copied, 1)
                        pool.wait_ge(pool_copied, j + (k * TT + t) * NB + 1)
                        pool.sem_inc(idx_used, 1)
                        for i in range(GB):
                            pool.wait_ge(row_used[i], j + (k * TT + t) * NB + 1)
                            pool.sem_inc(idx_used, 1)
                            pool.indirect_dma_start(out=gat[:, i, :], out_offset=None, in_=table,
                                                    in_offset=bass.IndirectOffsetOnAxis(ap=cols8[:, i:i + 1], axis=0)).then_inc(row_landed[i], 16)

    second_block.close()
    ctx.close()


def kernel(**inputs):
    import concourse.bacc as bacc
    from concourse.bass_utils import run_bass_kernel_spmd

    a = {n: np.asarray(v) for n, v in inputs.items()}
    arrays = {
        "weights1": np.stack([pack_weights1(a, l) for l in range(LAYERS)]),
        "vectors1": np.stack([pack_vectors1(a, l) for l in range(LAYERS)]),
        "tables1": constants(),
        "weights2": pack_weights2(a),
        "vectors2": pack_vectors2(a),
        "tables2": constants2(),
        "gate_rows2": gate_rows2(a),
        "peer_u": a["peer_u_2"][0],
        "peer_v": a["peer_v_2"][0],
        "x": a["x"][0],
        "ctx": a["ctx_2"][0],
    }
    arrays = {n: np.ascontiguousarray(v) for n, v in arrays.items()}
    nc = bacc.Bacc("TRN2", target_bir_lowering=False, num_devices=1)
    args = [nc.dram_tensor(n, v.shape, F32, kind="ExternalInput").ap() for n, v in arrays.items()]
    out = nc.dram_tensor("out", (T, D), F32, kind="ExternalOutput").ap()
    build_program(nc, *args, out)
    r = run_bass_kernel_spmd(nc, [arrays], core_ids=[0])
    return r.results[0]["out"].reshape(1, T, D)
```
